# Optimizing a Trainium2 kernel written in Bass

```python
import jax, jax.numpy as jnp
from jax import lax
import numpy as np

D_MODEL = 1024
BATCH = 1
SEQ = 128
DEPTH = 4
DEC_BATCH = 1
DEC_SEQ = 512
PAST_LEN = 128

GRID_W = 64
N_MIXERS = 3
N_FNET_LAYERS = (DEPTH + 2) // N_MIXERS
N_POOL_LAYERS = (DEPTH + 1) // N_MIXERS
N_MLA_LAYERS = DEPTH // N_MIXERS
N_FOURIER_GROUPS = 4
FOURIER_GROUP = D_MODEL // N_FOURIER_GROUPS
POOL_WINDOWS = (2, 4, 8, 16)
N_POOL_GROUPS = len(POOL_WINDOWS)
POOL_GROUP = D_MODEL // N_POOL_GROUPS
N_HEADS = 8
QK_NOPE = 128
QK_ROPE = 64
V_HEAD = 128
Q_RANK = 768
KV_RANK = 512
ROPE_AXIS = QK_ROPE // 2
ROPE_BASE = 10000.0
Q_BLOCK = 128
SM_SCALE = (QK_NOPE + QK_ROPE) ** -0.5
D_FF = 2816
CONV_W = 3
N_MOD = 6
EPS = 1e-6

kernel_name = 'hybrid_fnet_pool_mla_diffusion_step'

def rms_norm(x):
    xf = x.astype(jnp.float32)
    y = xf * lax.rsqrt(jnp.mean(xf * xf, axis=-1, keepdims=True) + EPS)
    return y.astype(x.dtype)

def rms_norm_gain(x, g):
    return rms_norm(x) * g

def ada_mod(cond, w, b):
    mod = jax.nn.silu(cond) @ w + b
    return tuple(m[:, None, :] for m in jnp.split(mod, N_MOD, axis=-1))

def modulate(x, shift, scale):
    return rms_norm(x) * (1 + scale) + shift

def fourier_mix(h, w_out):
    B, T, D = h.shape
    hg = h.astype(jnp.float32).reshape(B, T, N_FOURIER_GROUPS, FOURIER_GROUP)
    f = jnp.fft.fftn(hg, axes=(1, 3), norm='ortho').real
    return f.astype(h.dtype).reshape(B, T, D) @ w_out

def pool_mix(h, w_pool, scale):
    B, T, D = h.shape
    hg = h.astype(jnp.float32).reshape(B, T, N_POOL_GROUPS, POOL_GROUP)
    cs = jnp.concatenate([jnp.zeros((B, 1, N_POOL_GROUPS, POOL_GROUP), jnp.float32),
                          jnp.cumsum(hg, axis=1)], axis=1)
    t = jnp.arange(T)
    outs = []
    for g, w in enumerate(POOL_WINDOWS):
        lo = jnp.clip(t - w // 2, 0, T)
        hi = jnp.clip(t - w // 2 + w, 0, T)
        s = cs[:, hi, g] - cs[:, lo, g]
        cnt = (hi - lo).astype(jnp.float32)[None, :, None]
        outs.append(s / cnt - hg[:, :, g])
    pooled = jnp.stack(outs, axis=2).astype(h.dtype)
    y = jnp.einsum('btgc,gcd->btgd', pooled, w_pool).reshape(B, T, D)
    return y * scale

def dwconv3(u, w, b):
    up = jnp.pad(u, ((0, 0), (1, 1), (0, 0)))
    return up[:, :-2] * w[0] + up[:, 1:-1] * w[1] + up[:, 2:] * w[2] + b

def conv_ffn(h, w_in, w_conv, b_conv, w_out):
    u = dwconv3(h @ w_in, w_conv, b_conv)
    gate, val = jnp.split(u, 2, axis=-1)
    return (jax.nn.silu(gate) * val) @ w_out

def axial_rope_tables(n_tok):
    rows = n_tok // GRID_W
    row = jnp.repeat(jnp.arange(rows), GRID_W).astype(jnp.float32)
    col = jnp.tile(jnp.arange(GRID_W), rows).astype(jnp.float32)
    inv = 1.0 / (ROPE_BASE ** (jnp.arange(0, ROPE_AXIS, 2, dtype=jnp.float32) / ROPE_AXIS))
    ang_r = (row[:, None] * inv)[:, None, :]
    ang_c = (col[:, None] * inv)[:, None, :]
    return (jnp.cos(ang_r), jnp.sin(ang_r), jnp.cos(ang_c), jnp.sin(ang_c))

def rotate_half(x, cos, sin):
    x1, x2 = jnp.split(x, 2, axis=-1)
    cos = cos.astype(x.dtype)
    sin = sin.astype(x.dtype)
    return jnp.concatenate([x1 * cos - x2 * sin, x2 * cos + x1 * sin], axis=-1)

def apply_axial_rope(x, tabs):
    cos_r, sin_r, cos_c, sin_c = tabs
    xr, xc = jnp.split(x, 2, axis=-1)
    return jnp.concatenate([rotate_half(xr, cos_r, sin_r), rotate_half(xc, cos_c, sin_c)], axis=-1)

def mla_project(h, w_dq, g_q, w_uq, w_dkv, g_kv):
    B, T, _ = h.shape
    cq = rms_norm_gain(h @ w_dq, g_q)
    q = (cq @ w_uq).reshape(B, T, N_HEADS, QK_NOPE + QK_ROPE)
    ckv = h @ w_dkv
    c_kv = rms_norm_gain(ckv[..., :KV_RANK], g_kv)
    k_pe = ckv[..., KV_RANK:]
    return q[..., :QK_NOPE], q[..., QK_NOPE:], c_kv, k_pe

def mla_expand(c_kv, w_ukv):
    B, T, _ = c_kv.shape
    kv = (c_kv @ w_ukv).reshape(B, T, N_HEADS, QK_NOPE + V_HEAD)
    return kv[..., :QK_NOPE], kv[..., QK_NOPE:]

def mla_attend(q_nope, q_pe, k_nope, k_pe, v):
    B, Tq = q_nope.shape[:2]
    nb = Tq // Q_BLOCK
    qn = q_nope.reshape(B, nb, Q_BLOCK, N_HEADS, QK_NOPE).transpose(1, 0, 2, 3, 4)
    qp = q_pe.reshape(B, nb, Q_BLOCK, N_HEADS, QK_ROPE).transpose(1, 0, 2, 3, 4)

    def block(args):
        qn_b, qp_b = args
        s = (jnp.einsum('bqhd,bkhd->bhqk', qn_b, k_nope)
             + jnp.einsum('bqhr,bkr->bhqk', qp_b, k_pe))
        p = jax.nn.softmax(s.astype(jnp.float32) * SM_SCALE, axis=-1).astype(v.dtype)
        return jnp.einsum('bhqk,bkhd->bqhd', p, v)

    o = lax.map(block, (qn, qp))
    return o.transpose(1, 0, 2, 3, 4).reshape(B, Tq, N_HEADS * V_HEAD)

def mla_context(h, w_dq, g_q, w_uq, w_dkv, g_kv, w_ukv, w_o):
    q_nope, q_pe, c_kv, k_pe = mla_project(h, w_dq, g_q, w_uq, w_dkv, g_kv)
    k_nope, v = mla_expand(c_kv, w_ukv)
    out = mla_attend(q_nope, q_pe, k_nope, k_pe, v) @ w_o
    return out, c_kv, k_pe

def mla_latent(h, ctx_ckv, ctx_kpe, tabs, w_dq, g_q, w_uq, w_dkv, g_kv, w_ukv, w_o):
    q_nope, q_pe, c_kv, k_pe = mla_project(h, w_dq, g_q, w_uq, w_dkv, g_kv)
    q_pe = apply_axial_rope(q_pe, tabs)
    k_pe = apply_axial_rope(k_pe[:, :, None, :], tabs)[:, :, 0, :]
    c_all = jnp.concatenate([ctx_ckv.astype(c_kv.dtype), c_kv], axis=1)
    kpe_all = jnp.concatenate([ctx_kpe.astype(k_pe.dtype), k_pe], axis=1)
    k_nope, v = mla_expand(c_all, w_ukv)
    return mla_attend(q_nope, q_pe, k_nope, kpe_all, v) @ w_o

def setup_inputs(seed: int = 0) -> dict:
    key = jax.random.key(seed)
    ks = jax.random.split(key, 24)

    def nrm(k, shape, scale):
        return jax.random.normal(k, shape, jnp.float32) * scale

    D = D_MODEL
    return {
        'x_prompt': nrm(ks[0], (BATCH, SEQ, D), 1.0),
        'x_sample': nrm(ks[1], (DEC_BATCH, DEC_SEQ, D), 1.0),
        'cache_ckv': nrm(ks[2], (DEC_BATCH, N_MLA_LAYERS, PAST_LEN, KV_RANK), 1.0),
        'cache_kpe': nrm(ks[3], (DEC_BATCH, N_MLA_LAYERS, PAST_LEN, QK_ROPE), 1.0),
        'c': nrm(ks[4], (DEC_BATCH, D), 1.0),
        'c_ctx': nrm(ks[5], (D,), 1.0),
        'w_ada': nrm(ks[6], (DEPTH, D, N_MOD * D), D ** -0.5),
        'b_ada': nrm(ks[7], (DEPTH, N_MOD * D), 0.02),
        'w_fnet': nrm(ks[8], (N_FNET_LAYERS, D, D), D ** -0.5),
        'w_pool': nrm(ks[9], (N_POOL_LAYERS, N_POOL_GROUPS, POOL_GROUP, POOL_GROUP), POOL_GROUP ** -0.5),
        'pool_scale': 1.0 + nrm(ks[10], (N_POOL_LAYERS, D), 0.1),
        'w_dq': nrm(ks[11], (N_MLA_LAYERS, D, Q_RANK), D ** -0.5),
        'g_q': 1.0 + nrm(ks[12], (N_MLA_LAYERS, Q_RANK), 0.1),
        'w_uq': nrm(ks[13], (N_MLA_LAYERS, Q_RANK, N_HEADS * (QK_NOPE + QK_ROPE)), Q_RANK ** -0.5),
        'w_dkv': nrm(ks[14], (N_MLA_LAYERS, D, KV_RANK + QK_ROPE), D ** -0.5),
        'g_kv': 1.0 + nrm(ks[15], (N_MLA_LAYERS, KV_RANK), 0.1),
        'w_ukv': nrm(ks[16], (N_MLA_LAYERS, KV_RANK, N_HEADS * (QK_NOPE + V_HEAD)), KV_RANK ** -0.5),
        'w_o': nrm(ks[17], (N_MLA_LAYERS, N_HEADS * V_HEAD, D), (N_HEADS * V_HEAD) ** -0.5),
        'w_ffn_in': nrm(ks[18], (DEPTH, D, 2 * D_FF), D ** -0.5),
        'w_ffn_conv': nrm(ks[19], (DEPTH, CONV_W, 2 * D_FF), CONV_W ** -0.5),
        'b_ffn_conv': nrm(ks[20], (DEPTH, 2 * D_FF), 0.02),
        'w_ffn_out': nrm(ks[21], (DEPTH, D_FF, D), D_FF ** -0.5),
        'g_final': 1.0 + nrm(ks[22], (D,), 0.1),
    }

def reference(x_prompt, x_sample, cache_ckv, cache_kpe, c, c_ctx, w_ada, b_ada, w_fnet,
              w_pool, pool_scale, w_dq, g_q, w_uq, w_dkv, g_kv, w_ukv, w_o,
              w_ffn_in, w_ffn_conv, b_ffn_conv, w_ffn_out, g_final):
    lat_rope = axial_rope_tables(x_sample.shape[1])
    xp, xs = x_prompt, x_sample
    new_ckv, new_kpe = [], []
    j_f = 0
    j_p = 0
    j_a = 0
    for i in range(DEPTH):
        sh1p, sc1p, g1p, sh2p, sc2p, g2p = ada_mod(c_ctx[None, :], w_ada[i], b_ada[i])
        sh1s, sc1s, g1s, sh2s, sc2s, g2s = ada_mod(c, w_ada[i], b_ada[i])
        hp = modulate(xp, sh1p, sc1p)
        hs = modulate(xs, sh1s, sc1s)
        kind = i % N_MIXERS
        if kind == 0:
            mp = fourier_mix(hp, w_fnet[j_f])
            ms = fourier_mix(hs, w_fnet[j_f])
            j_f += 1
        elif kind == 1:
            mp = pool_mix(hp, w_pool[j_p], pool_scale[j_p])
            ms = pool_mix(hs, w_pool[j_p], pool_scale[j_p])
            j_p += 1
        else:
            prm = (w_dq[j_a], g_q[j_a], w_uq[j_a], w_dkv[j_a], g_kv[j_a], w_ukv[j_a], w_o[j_a])
            mp, ckv_p, kpe_p = mla_context(hp, *prm)
            ms = mla_latent(hs, cache_ckv[:, j_a], cache_kpe[:, j_a], lat_rope, *prm)
            new_ckv.append(ckv_p)
            new_kpe.append(kpe_p)
            j_a += 1
        xp = xp + g1p * mp
        xs = xs + g1s * ms
        xp = xp + g2p * conv_ffn(modulate(xp, sh2p, sc2p), w_ffn_in[i], w_ffn_conv[i],
                                 b_ffn_conv[i], w_ffn_out[i])
        xs = xs + g2s * conv_ffn(modulate(xs, sh2s, sc2s), w_ffn_in[i], w_ffn_conv[i],
                                 b_ffn_conv[i], w_ffn_out[i])
    y_prompt = rms_norm_gain(xp, g_final)
    y_sample = rms_norm_gain(xs, g_final)
    state_ckv = jnp.stack(new_ckv, axis=1)
    state_kpe = jnp.stack(new_kpe, axis=1)
    return (y_prompt, y_sample, state_ckv, state_kpe)


_drawn_inputs = setup_inputs


def setup_inputs(seed=0):
    import zlib

    import numpy as np

    out = dict(_drawn_inputs(seed))
    spreads = {}
    factors = {'cache_ckv': 4.129, 'cache_kpe': 7.408, 'g_q': 8.0, 'b_ffn_conv': 2.903}
    for name, (base, spread) in spreads.items():
        noise = np.random.default_rng([zlib.crc32(name.encode()), seed]).standard_normal(out[name].shape)
        drawn = base * np.exp(spread * noise) if base else spread * noise
        out[name] = __import__('jax').numpy.asarray(drawn.astype(out[name].dtype))
    for name, factor in factors.items():
        out[name] = (out[name] * factor).astype(out[name].dtype)
    return out
```

```python
from contextlib import ExitStack

import concourse.bass as bass
import numpy as np
from concourse import mybir

P = 128
D = 1024
KC = D // P
CTX, LAT, PAST = 128, 512, 128
GAP = 2
LAT0 = CTX + GAP
LAT1 = LAT0 + LAT
W = LAT1 + GAP
HALF = W // 2
DEPTH = 4
N_MOD = 6
MODS = N_MOD * KC
D_FF = 2816
PAIRS = D_FF // P
PARTS = [(0, 8), (8, 8), (16, 6)]
GROUPS, GROUP = 4, 256
HEADS, NOPE, ROPE, VH = 8, 128, 64, 128
Q_RANK, KV_RANK = 768, 512
QC, RC = Q_RANK // P, KV_RANK // P
SM_SCALE = (NOPE + ROPE) ** -0.5
EPS = 1e-6
UNIT = 1024
SLOTS = 4
KEYS = LAT1 + PAST
KW = KEYS + GAP
KHALF = KW // 2
NK = LAT + PAST
SHALF = NK // 2
KTILES = NK // P
PADW = 8 + CTX + 8 + LAT + 8
PC, PL = 8, 8 + CTX + 8
MIXERS = ["fnet", "pool", "mla", "fnet"]
ADA_REST = 4
SH1, SC1, G1, SH2, SC2, G2 = (KC * i for i in range(N_MOD))


TABLES = 8
LATENT_SIZES = [UNIT] * RC + [UNIT // 2] * 2 + [UNIT] * QC
HEAD_SIZES = [RC * 2 * VH, QC * P, RC * P, QC * P, RC * P, QC * P]
Q_TILES = [(LAT0 + P * t, LAT0, SHALF, 2) for t in range(4)] + [(0, 0, CTX, 1)]
SMALL_LOADS = 16 * (2 + KC + 4)
TABLES_POOL, TABLES_MLA, TABLES_ROPE = 16, 32, 48


def layer_loads(layer):
    return 16 * (2 * layer + min(2, DEPTH - layer))


def ada_in_ffn(layer):
    return MODS - ADA_REST if layer + 1 < DEPTH else 0


class Counts:

    def __init__(self):
        self.unit = 0
        self.split = 0
        self.result = 0
        self.ada = 0
        self.pair = 0
        self.rounded = 0
        self.norm = 0
        self.stat = 0
        self.chunk = 0
        self.squared = 0
        self.score = 0
        self.cleared = 0


def build_backbone(nc, a):
    f32, f32r = mybir.dt.float32, mybir.dt.float32r
    ACT = mybir.ActivationFunctionType
    ALU = mybir.AluOpType
    AX = mybir.AxisListType
    ds = bass.ds
    n_units = a["stream"].shape[0]

    with ExitStack() as ctx:
        sem = lambda name: ctx.enter_context(nc.semaphore(name))
        pb = lambda name, shape: ctx.enter_context(nc.psum_tensor(name, shape, f32))
        at = [(nc.sbuf_base + 31) // 32 * 32]

        def place(name, shape, dt=f32, offset=None):
            size = 4 * int(np.prod(shape[1:]))
            where = at[0] if offset is None else offset
            if offset is None:
                at[0] += size
            assert where + size <= nc.sbuf_usable_end, name
            return nc.alloc_sbuf_tensor_at(name, shape, dt, offset=where, align_bytes=4)

        x = place("x", [P, KC, W])
        h_at = at[0]
        h_hi, h_lo = place("h_hi", [P, KC, W], f32r), place("h_lo", [P, KC, W], f32r)
        raw = [place(f"raw{s}", [P, UNIT]) for s in range(SLOTS)]
        w_hi = [place(f"w_hi{s}", [P, UNIT], f32r) for s in range(2)]
        w_lo = [place(f"w_lo{s}", [P, UNIT], f32r) for s in range(2)]
        rows = place("rows", [P, 7, W])
        mod = place("mod", [P, 2, MODS, 2])
        b_ada = place("b_ada", [P, 2, MODS])
        conv_w = place("conv_w", [P, 2 * PAIRS, 4])
        ident, ones, perm = place("ident", [P, P]), place("ones", [P, P]), place("perm", [P, P])
        cond = place("cond", [P, KC, 2])
        gains = place("gains", [P, QC + RC + 2 * KC])
        g_q, g_kv = gains[:, 0:QC], gains[:, QC:QC + RC]
        g_final = gains[:, QC + RC:QC + RC + KC]
        pool_scale = gains[:, QC + RC + KC:]
        eps = place("eps", [P, 1])
        gate_pool = place("gate_pool", [P, KC, 2])
        top, negtop, total, inverse = (place(n, [P, 2]) for n in ("top", "negtop", "total", "inverse"))
        g_at = at[0]
        g_hi, g_lo = place("g_hi", [P, 8, W], f32r), place("g_lo", [P, 8, W], f32r)
        seq_t = [[place(f"seq_t{c}{p}", [P, 4, LAT], f32r, g_at + (2 * c + p) * 8192) for p in range(2)]
                 for c in range(2)]
        ctx_t = [[place(f"ctx_t{c}{p}", [P, CTX], f32r, g_at + 32768 + (2 * c + p) * 512) for p in range(2)]
                 for c in range(2)]
        cq_hi = place("cq_hi", [P, QC, W], f32r, g_at)
        cq_lo = place("cq_lo", [P, QC, W], f32r, g_at + 4 * QC * W)
        cache = place("cache", [P, RC + 1, PAST], f32, g_at)
        tail = g_at + 8 * QC * W
        ckv_raw = place("ckv_raw", [P, RC, W], f32, tail)
        q_hi, q_lo = place("q_hi", [P, W], f32r, tail), place("q_lo", [P, W], f32r, tail + 4 * W)
        pt_hi = place("pt_hi", [P, KTILES, P], f32r, tail + 8 * W)
        pt_lo = place("pt_lo", [P, KTILES, P], f32r, tail + 8 * W + 4 * NK)
        e_at = at[0]
        conv = [place(f"conv{j}", [P, W + 2], f32, e_at + 4 * (W + 2) * j) for j in range(2)]
        gated = place("gated", [P, W], f32, e_at + 8 * (W + 2))
        chan_t = [place(f"chan_t{p}", [P, 2, 2 * GROUP], f32r, e_at + 4096 * p) for p in range(2)]
        freq = [place(f"freq{p}", [P, 5, 2 * GROUP], f32r, e_at + 8192 + 10240 * p) for p in range(2)]
        inv_count = place("inv_count", [P, 4, PADW], f32, e_at)
        padded = [place(f"padded{j}", [P, PADW], f32, e_at + 4 * PADW * (4 + j)) for j in range(2)]
        window = [place(f"window{j}", [P, PADW], f32, e_at + 4 * PADW * (6 + j)) for j in range(2)]
        scratch = place("scratch", [P, PADW], f32, e_at + 4 * PADW * 8)
        y = place("y", [P, KC, W], f32, g_at)
        ckv_hi, ckv_lo = place("ckv_hi", [P, RC, KW], f32r), place("ckv_lo", [P, RC, KW], f32r)
        kpe_hi, kpe_lo = place("kpe_hi", [P, KW], f32r), place("kpe_lo", [P, KW], f32r)
        v_at = at[0]
        v_hi, v_lo = place("v_hi", [P, 6, 2 * VH], f32r), place("v_lo", [P, 6, 2 * VH], f32r)
        k_hi, k_lo = place("k_hi", [P, KW], f32r), place("k_lo", [P, KW], f32r)
        qpe_hi, qpe_lo = place("qpe_hi", [P, W], f32r), place("qpe_lo", [P, W], f32r)
        cq_raw = place("cq_raw", [P, QC, W], f32, v_at)
        kpe_raw, kpe_cos, kpe_sin = (place(f"kpe_{n}", [P, W], f32, v_at + 4 * W * (QC + j))
                                     for j, n in enumerate(("raw", "cos", "sin")))
        SUM, SQ, RSTD, XN, HF = 0, 1, 2, 3, 5
        row = lambda i: rows[:, i, :]
        tab_cos, tab_sin = row(5), row(6)
        sum_q, rstd_q = row(3), row(4)
        probs = [row(3), row(4)]
        q_raw, q_rot = row(0), row(1)

        acc = [pb("acc0", [P, 2, 512]), pb("acc1", [P, 2, 512])]
        sacc = [pb("sacc0", [P, 2, 512]), pb("sacc1", [P, 2, 512])]
        halves = lambda t: t[:, :, 0:HALF]
        two = lambda ap: ap.rearrange("p (a b) -> p a b", a=2)

        loaded = sem("loaded")
        layer_loaded = sem("layer_loaded")
        table_loaded = sem("table_loaded")
        raw_ready = [sem(f"raw_ready{s}") for s in range(SLOTS)]
        unit_done = [sem(f"unit_done{s}") for s in range(SLOTS)]
        weights_hi = sem("weights_hi")
        result_ready = sem("result_ready")
        result_taken = sem("result_taken")
        result_rounded = sem("result_rounded")
        ada_taken = sem("ada_taken")
        cond_ready = sem("cond_ready")
        centered = sem("centered")
        left_done = sem("left_done")
        silu_done = sem("silu_done")
        gated_done = sem("gated_done")
        g_rounded = sem("g_rounded")
        g_ready = sem("g_ready")
        squared = sem("squared")
        summed = sem("summed")
        stat_ready = sem("stat_ready")
        rooted = sem("rooted")
        rstd_done = sem("rstd_done")
        xn_ready = sem("xn_ready")
        h_full = sem("h_full")
        h_rounded = sem("h_rounded")
        h_ready = sem("h_ready")
        mod_ready = sem("mod_ready")
        setup_done = sem("setup_done")
        pool_step = sem("pool_step")
        pooled_full = sem("pooled_full")
        rope_step = sem("rope_step")
        raw_copied = sem("raw_copied")
        score_ready = sem("score_ready")
        score_taken = sem("score_taken")
        top_done = sem("top_done")
        bias_done = sem("bias_done")
        exp_done = sem("exp_done")
        inverse_done = sem("inverse_done")
        latent_normed = sem("latent_normed")
        latent_squared = sem("latent_squared")
        latent_rounded = sem("latent_rounded")
        latent_ready = sem("latent_ready")
        sum_cleared = sem("sum_cleared")
        conv_padded = sem("conv_padded")
        cached = sem("cached")
        cache_rounded = sem("cache_rounded")
        stored = sem("stored")
        y_ready = sem("y_ready")

        block = ctx.enter_context(nc.Block())

        CXS, LTS = slice(0, CTX), slice(LAT0, LAT1)

        def fnet_tables():
            out = [(chan_t[0][:, k, :], chan_t[1][:, k, :], 2 * GROUP) for k in range(2)]
            out += [(ctx_t[c][0][:], ctx_t[c][1][:], CTX) for c in range(2)]
            flat = lambda t, k: t[:, 2 * k:2 * k + 2, :].rearrange("p a b -> p (a b)")
            out += [(flat(seq_t[c][0], k), flat(seq_t[c][1], k), UNIT) for c in range(2) for k in range(2)]
            return out

        def transposed_pieces(dst, src, tiles):
            flat = lambda z0, z1: dst[:, z0:z1, :].rearrange("p a b -> p (a b)")
            if tiles == 1:
                return [(flat(0, 1), src[:, 0, 0:P])]
            return [(flat(0, 4), src[:, 0, :]), (flat(4, 5), src[:, 1, 0:P])]

        def head_out(dst, i, h2, hh, q0):
            return dst[:, ds(4 * i + 2 * h2 + hh, 1), q0:q0 + P].rearrange("p o t -> p (o t)")

        def after_ffn_in(n, layer, count):
            n.unit += 4 * count if ada_in_ffn(layer) else 2 * count
            n.split += 2 * count
            n.result += 2 * count
            n.pair += count
            n.ada += 2 * count if ada_in_ffn(layer) else 0

        def after_project(n, units=KC, splits=KC, squares=True):
            n.unit += units
            n.split += splits
            n.result += KC
            n.squared += KC if squares else 0

        def after_norm(n):
            n.norm += 1
            n.stat += 1
            n.chunk += KC

        @block.sync
        def _(sp):
            for s in range(SLOTS):
                sp.dma_start(raw[s][:], a["stream"][s]).then_inc(raw_ready[s], 16)
            with sp.Fori(1, n_units // SLOTS) as i:
                for s in range(SLOTS):
                    sp.wait_ge(unit_done[s], i)
                    sp.dma_start(raw[s][:], a["stream"][ds(i * SLOTS + s, 1)].rearrange("o p n -> (o p) n")
                                 ).then_inc(raw_ready[s], 16)

        @block.gpsimd
        def _(pool):
            n = Counts()

            def cut(slot, split, hi, lo, raw_size):
                pool.wait_ge(weights_hi, split + 1)
                nc.gpsimd.tensor_tensor(lo, raw[slot][:, 0:raw_size], hi.bitcast(f32), ALU.subtract
                                        ).then_inc(unit_done[slot], 1)

            def ring(slot, split, size=UNIT):
                cut(slot, split, w_hi[slot % 2][:, 0:size], w_lo[slot % 2][:, 0:size], size)

            def project(size=UNIT):
                with pool.Fori(0, 2) as i:
                    for j in range(4):
                        ring(j, n.split + 4 * i + j, size)

            def ffn(layer):
                for part, (_, count) in enumerate(PARTS):
                    per_turn = 2 if ada_in_ffn(layer) else 4
                    with pool.Fori(0, 2 * count // per_turn) as i:
                        for j in range(per_turn):
                            ring(j, n.split + per_turn * i + j)
                    after_ffn_in(n, layer, count)
                    project(count * P)
                    after_project(n, squares=part == 2)

            for layer, kind in enumerate(MIXERS):
                if kind == "fnet":
                    ring(0, n.split)
                    for j, (hi, lo, size) in enumerate(fnet_tables()):
                        cut((1 + j) % SLOTS, n.split + 1 + j, hi, lo, size)
                    n.split += TABLES
                    for j in range(1, KC):
                        ring(j % SLOTS, n.split + j)
                    n.split += KC
                elif kind == "pool":
                    for j in range(4):
                        ring(j, n.split + j, 512)
                    n.split += 4
                else:
                    for j, size in enumerate(LATENT_SIZES):
                        ring(j % SLOTS, n.split + j, size)
                    n.split += len(LATENT_SIZES)
                    with pool.Fori(0, 2) as i:
                        for j in range(12):
                            ring(j % SLOTS, n.split + 12 * i + j, HEAD_SIZES[j % 6])
                    n.split += 24
                    project()
                    n.split += KC
                ffn(layer)

        @block.tensor
        def _(pe):
            n = Counts()

            def product(outs, lhs, rhs, first=True, last=True):
                for z, (lp, rp) in enumerate(((0, 0), (0, 1), (1, 0))):
                    for o, r in zip(outs, rhs[rp]):
                        done = nc.tensor.matmul(o, lhs[lp], r, start=first and z == 0, stop=last and z == 2)
                return done

            def token_halves(hi, lo):
                return [[t[:, 0:HALF], t[:, HALF:W]] for t in (hi, lo)]

            def acc_halves(p, size=HALF):
                return [acc[p][:, b, 0:size] for b in range(2)]

            def weights(slot, k, width=P):
                return [w[slot % 2][:, k * width:(k + 1) * width] for w in (w_hi, w_lo)]

            def ada_unit(slot, use, out, taken=None):
                pe.wait_ge(raw_ready[slot], 16 * use)
                if taken is not None:
                    pe.wait_ge(ada_taken, taken)
                for k in range(KC):
                    done = nc.tensor.matmul(out, raw[slot][:, k * P:(k + 1) * P], cond[:, k, :],
                                            start=k == 0, stop=k == KC - 1)
                done.then_inc(unit_done[slot], 1)

            def ada_rest(layer):
                if layer:
                    for j in range(ADA_REST):
                        u = n.unit + 1 + j
                        ada_unit(u % SLOTS, u // SLOTS + 1, sacc[1][:, j % 2, 0:2], n.ada + j - 1)
                    n.ada += ADA_REST
                    n.unit += ADA_REST

            def statistics(source):
                for b in range(2):
                    done = nc.tensor.matmul(sacc[0][:, b, 0:HALF], ones[:], source[:, b * HALF:(b + 1) * HALF],
                                            start=True, stop=True)
                done.then_inc(stat_ready, 1)
                n.stat += 1

            def norm():
                pe.wait_ge(summed, n.squared)
                statistics(row(SUM))
                n.chunk += KC

            def project(source, kn, ready=None, ready_from=0):
                with pe.Fori(0, 2) as i:
                    for j in range(4):
                        pe.wait_ge(unit_done[j], n.unit // SLOTS + i + 1)
                        pe.wait_ge(result_taken, n.result + 4 * i + j - 1)
                        for k in range(kn):
                            if j == 0 and ready is not None:
                                pe.wait_ge(ready, ready_from + k + 1)
                            done = product(acc_halves(j % 2), weights(j, k),
                                           token_halves(source[0][:, k, :], source[1][:, k, :]),
                                           k == 0, k == kn - 1)
                        done.then_inc(result_ready, 1)

            def ffn(layer):
                norm()
                for part, (_, count) in enumerate(PARTS):
                    turn = 1 if ada_in_ffn(layer) else 2
                    with pe.Fori(0, count // turn) as i:
                        for j in range(2 * turn):
                            pe.wait_ge(unit_done[j], n.unit // SLOTS + i + 1)
                            pe.wait_ge(result_taken, n.result + 2 * turn * i + j - 1)
                            for k in range(KC):
                                if j == 0:
                                    pe.wait_ge(h_ready, n.chunk - KC + k + 1)
                                done = product(acc_halves(j % 2), weights(j, k),
                                               token_halves(h_hi[:, k, :], h_lo[:, k, :]), k == 0, k == KC - 1)
                            done.then_inc(result_ready, 1)
                        if turn == 1:
                            for j in range(2):
                                ada_unit(2 + j, n.unit // SLOTS + i + 1, sacc[1][:, j, 0:2], n.ada + 2 * i + j - 1)
                    after_ffn_in(n, layer, count)
                    project((g_hi, g_lo), count, g_ready, n.pair - count)
                    after_project(n, squares=part == 2)

            def fnet():
                r = n.result
                for g in range(GROUPS):
                    for t in range(5):
                        first = 0 if t == 0 else LAT0 + P * (t - 1)
                        if r >= 2:
                            pe.wait_ge(result_taken, r - 1)
                        if g == 0 and t == 0:
                            for j in range(2):
                                u = n.unit + 1 + j
                                pe.wait_ge(unit_done[u % SLOTS], u // SLOTS + 1)
                        for k in range(2):
                            c = 2 * g + k
                            if t == 0:
                                pe.wait_ge(h_ready, n.chunk - KC + c + 1)
                            done = product([acc[r % 2][:, 0, :]],
                                           [hh[:, c, first:first + P] for hh in (h_hi, h_lo)],
                                           [[chan_t[p][:, k, :]] for p in range(2)], k == 0, k == 1)
                        done.then_inc(result_ready, 1)
                        r += 1
                    if g == 0:
                        for j in range(4):
                            u = n.unit + TABLES - j
                            pe.wait_ge(unit_done[u % SLOTS], u // SLOTS + 1)
                    for m in range(2):
                        pe.wait_ge(result_taken, r if m == 0 else r - 1)
                        for c in range(2):
                            col = c * GROUP + m * P
                            product([acc[r % 2][:, 0, 0:CTX]], [f[:, 0, col:col + P] for f in freq],
                                    [[ctx_t[c][p][:]] for p in range(2)], c == 0, c == 1)
                        for c in range(2):
                            col = c * GROUP + m * P
                            for t in range(4):
                                done = product([acc[r % 2][:, 1, :]],
                                               [f[:, t + 1, col:col + P] for f in freq],
                                               [[seq_t[c][p][:, t, :]] for p in range(2)],
                                               c == 0 and t == 0, c == 1 and t == 3)
                        done.then_inc(result_ready, 1)
                        r += 1
                n.result = r
                n.unit += TABLES
                pe.wait_ge(result_taken, n.result)
                project((h_hi, h_lo), KC)
                after_project(n)

            def pool_mix():
                for j in range(KC):
                    u = j // 2
                    pe.wait_ge(unit_done[u], n.unit // SLOTS + 1)
                    pe.wait_ge(result_taken, n.result - 1 + j)
                    for k in range(2):
                        c = 2 * u + k
                        pe.wait_ge(h_ready, n.chunk - KC + c + 1)
                        done = product(acc_halves(j % 2), weights(u, 2 * (j % 2) + k),
                                       token_halves(h_hi[:, c, :], h_lo[:, c, :]), k == 0, k == 1)
                    done.then_inc(result_ready, 1)
                after_project(n, 4, 4)

            def rotate(source, out):
                for b in range(2):
                    done = nc.tensor.matmul(out[:, b, 0:HALF], perm[:], source[:, b * HALF:(b + 1) * HALF],
                                            start=True, stop=True)
                done.then_inc(result_ready, 1)

            def unit_product(out, unit, size, rhs, first=True, last=True, k0=0, waits=()):
                pe.wait_ge(unit_done[unit % SLOTS], unit // SLOTS + 1)
                for k in range(size):
                    for s, v in waits:
                        pe.wait_ge(s, v(k))
                    done = product(out, weights(unit, k), rhs(k0 + k), first and k == 0, last and k == size - 1)
                return done

            def latents():
                h_of = lambda k: token_halves(h_hi[:, k, :], h_lo[:, k, :])
                r, u = n.result, n.unit
                for m in range(RC):
                    pe.wait_ge(result_taken, r - 1)
                    wait_h = [(h_ready, lambda k: n.chunk - KC + k + 1)] if m == 0 else []
                    unit_product(acc_halves(r % 2), u, KC, h_of, waits=wait_h).then_inc(result_ready, 1)
                    r, u = r + 1, u + 1
                pe.wait_ge(result_taken, r - 1)
                unit_product(acc_halves(r % 2), u, 4, h_of, last=False)
                unit_product(acc_halves(r % 2), u + 1, 4, h_of, first=False, k0=4).then_inc(result_ready, 1)
                r, u = r + 1, u + 2
                for m in range(QC):
                    pe.wait_ge(result_taken, r - 1)
                    unit_product(acc_halves(r % 2), u, KC, h_of).then_inc(result_ready, 1)
                    r, u = r + 1, u + 1
                    if m == 0:
                        pe.wait_ge(result_taken, r - 1)
                        rotate(kpe_raw, acc[r % 2])
                        r += 1
                    if m == 1:
                        pe.wait_ge(result_taken, n.result + RC)
                        statistics(row(SUM))
                pe.wait_ge(result_taken, r)
                pe.wait_ge(rooted, n.stat)
                statistics(sum_q)
                n.result, n.unit = r, u

            def attention():
                with pe.Fori(0, 2) as i:
                    for h2 in range(2):
                        r = n.result + 64 * i + 32 * h2
                        s = n.score + 20 * i + 10 * h2
                        use = lambda j: n.unit // SLOTS + 3 * i + (6 * h2 + j) // SLOTS + 1
                        slot = lambda j: (6 * h2 + j) % SLOTS
                        ru = [0]

                        def accumulator():
                            p = ru[0] % 2
                            pe.wait_ge(result_taken, r + ru[0] - 1)
                            ru[0] += 1
                            return p

                        def unit(j):
                            pe.wait_ge(unit_done[slot(j)], use(j))

                        if h2 == 0:
                            pe.wait_ge(cached, 2)
                            pe.wait_ge(latent_ready, 1 + RC + QC)
                        unit(0)
                        for t in range(6):
                            p = accumulator()
                            first = [0, LAT0, LAT0 + P, LAT0 + 2 * P, LAT0 + 3 * P, LAT1][t]
                            for k in range(RC):
                                done = product([acc[p][:, 0, 0:2 * VH]],
                                               [c[:, k, first:first + P] for c in (ckv_hi, ckv_lo)],
                                               [[w] for w in weights(slot(0), k, 2 * VH)], k == 0, k == RC - 1)
                            done.then_inc(result_ready, 1)
                        unit(1)
                        p = accumulator()
                        for k in range(QC):
                            done = product(acc_halves(p), weights(slot(1), k),
                                           token_halves(cq_hi[:, k, :], cq_lo[:, k, :]), k == 0, k == QC - 1)
                        done.then_inc(result_ready, 1)
                        p = accumulator()
                        pe.wait_ge(result_taken, r + 7)
                        rotate(q_raw, acc[p])
                        for hh in range(2):
                            unit(2 + 2 * hh)
                            p = accumulator()
                            for k in range(RC):
                                done = product(acc_halves(p, KHALF), weights(slot(2 + 2 * hh), k),
                                               [[c[:, k, 0:KHALF], c[:, k, KHALF:KW]] for c in (ckv_hi, ckv_lo)],
                                               k == 0, k == RC - 1)
                            done.then_inc(result_ready, 1)
                            unit(3 + 2 * hh)
                            p = accumulator()
                            for k in range(QC):
                                done = product(acc_halves(p), weights(slot(3 + 2 * hh), k),
                                               token_halves(cq_hi[:, k, :], cq_lo[:, k, :]), k == 0, k == QC - 1)
                            done.then_inc(result_ready, 1)
                            head_rows = slice(ROPE * hh, ROPE * hh + ROPE)

                            def scores(t):
                                q0, k0, width, banks = Q_TILES[t]
                                b = (5 * hh + t) % 2
                                pe.wait_ge(score_taken, s + 5 * hh + t + 1)
                                keys = lambda src, rows_: [[src_[rows_, k0 + width * z:k0 + width * (z + 1)]
                                                            for z in range(banks)] for src_ in src]
                                out = [sacc[b][:, z, 0:width] for z in range(banks)]
                                product(out, [q[:, q0:q0 + P] for q in (q_hi, q_lo)],
                                        keys((k_hi, k_lo), slice(0, P)), True, False)
                                product(out, [q[head_rows, q0:q0 + P] for q in (qpe_hi, qpe_lo)],
                                        keys((kpe_hi, kpe_lo), head_rows), False, True
                                        ).then_inc(score_ready, 1)

                            def weigh(t):
                                q0, k0, width, banks = Q_TILES[t]
                                tiles = width * banks // P
                                pe.wait_ge(score_taken, s + 5 * hh + t + 3)
                                p = accumulator()
                                for z in range(tiles):
                                    done = nc.tensor.transpose(acc[p][:, z // 4, (z % 4) * P:(z % 4 + 1) * P],
                                                               probs[(5 * hh + t) % 2][:, z * P:(z + 1) * P], ident[:])
                                done.then_inc(result_ready, 1)
                                pe.wait_ge(result_taken, r + ru[0])
                                p = accumulator()
                                for z in range(tiles):
                                    v = z + 1 if t < 4 else 0
                                    done = product([acc[p][:, 0, 0:P]],
                                                   [vv[:, v, hh * VH:(hh + 1) * VH] for vv in (v_hi, v_lo)],
                                                   [[pt[:, z, :]] for pt in (pt_hi, pt_lo)],
                                                   z == 0, z == tiles - 1)
                                done.then_inc(result_ready, 1)

                            pe.wait_ge(result_taken, r + ru[0])
                            pe.wait_ge(rope_step, 3 + (2 * i + h2 + 1) * 3)
                            scores(0)
                            for t in range(1, 5):
                                scores(t)
                                weigh(t - 1)
                            weigh(4)
                n.result += 128
                n.score += 40
                n.unit += 24

            pe.wait_ge(cond_ready, 1)
            four_banks = [sacc[j // 2][:, j % 2, 0:2] for j in range(4)]
            for j in range(4):
                ada_unit(j, 1, four_banks[j])
            with pe.Fori(0, MODS // 4 - 1) as i:
                for j in range(4):
                    ada_unit(j, i + 2, four_banks[j], 4 * i + j + 1)
            pe.wait_ge(ada_taken, MODS)
            n.unit, n.ada, n.squared = MODS, MODS, KC
            pe.wait_ge(loaded, SMALL_LOADS)
            pe.wait_ge(setup_done, 1)
            for layer, kind in enumerate(MIXERS):
                norm()
                ada_rest(layer)
                if kind == "fnet":
                    fnet()
                elif kind == "pool":
                    pool_mix()
                else:
                    latents()
                    attention()
                    pe.wait_ge(result_taken, n.result)
                    project((h_hi, h_lo), KC)
                    after_project(n)
                ffn(layer)
            pe.wait_ge(summed, n.squared)
            statistics(row(SUM))

        @block.scalar
        def _(act):
            n = Counts()

            def round_unit(slot, use, hi, size, free=None):
                act.wait_ge(raw_ready[slot], 16 * use)
                if free is not None:
                    act.wait_ge(result_ready, free)
                nc.scalar.activation(hi, raw[slot][:, 0:size], ACT.Copy).then_inc(weights_hi, 1)

            def round_ring(slot, use, free=None, size=UNIT):
                round_unit(slot, use, w_hi[slot % 2][:, 0:size], size, free)

            def take(r, pieces):
                act.wait_ge(result_ready, r + 1)
                for dst, src in pieces:
                    done = nc.scalar.activation(dst, src, ACT.Copy)
                done.then_inc(result_rounded, 1)

            def root(width, to=row(RSTD)):
                act.wait_ge(stat_ready, n.stat + 1)
                nc.scalar.activation(two(to), halves(sacc[0]), ACT.Sqrt, bias=eps[:], scale=1.0 / width
                                     ).then_inc(rooted, 1)
                n.stat += 1

            def norm(layer, shift, scale, target=None, table_after=None):
                root(D)
                for c in range(KC):
                    act.wait_ge(xn_ready, n.chunk + c + 1)
                    if target is None and c >= 2:
                        act.wait_ge(h_ready, n.chunk + c - 1)
                    xn = row(XN + c % 2)
                    out = row(HF + c % 2) if target is None else padded[c % 2]
                    if target is not None and c >= 2:
                        act.wait_ge(h_ready, n.chunk + c - 1)
                    places = (CXS, LTS) if target is None else (slice(PC, PC + CTX), slice(PL, PL + LAT))
                    for z, (cols, to) in enumerate(zip((CXS, LTS), places)):
                        done = nc.scalar.activation(out[:, to], xn[:, cols], ACT.Identity,
                                                    bias=mod[:, layer % 2, shift + c, z:z + 1],
                                                    scale=mod[:, layer % 2, scale + c, z:z + 1])
                    done.then_inc(h_full, 1)
                    if target is None:
                        act.wait_ge(h_full, n.chunk + c + 1)
                        nc.scalar.activation(h_hi[:, c, :], out, ACT.Copy).then_inc(h_rounded, 1)
                    else:
                        target(c)
                    if table_after is not None:
                        table_after(c)
                n.chunk += KC

            def square(source):
                nc.scalar.activation(row(SQ), source, ACT.Square).then_inc(squared, 1)

            def project_steps(i, squares, last):
                for j in range(4):
                    if not (last and j == 3):
                        round_ring((j + 1) % SLOTS, n.unit // SLOTS + i + (j + 1) // SLOTS + 1,
                                   n.result + 4 * i + j)
                    if squares:
                        act.wait_ge(result_taken, n.result + 4 * i + j + 1)
                        square(x[:, ds(4 * i + j, 1), :].rearrange("p o t -> p (o t)"))

            def project(squares=True, last=False):
                with act.Fori(0, 1 if last else 2) as i:
                    project_steps(i, squares, False)
                if last:
                    project_steps(1, squares, True)

            def ffn(layer):
                norm(layer, SH2, SC2)
                act.wait_ge(layer_loaded, layer_loads(layer))
                for part, (_, count) in enumerate(PARTS):
                    turn = 1 if ada_in_ffn(layer) else 2
                    with act.Fori(0, count // turn) as i:
                        for z in range(turn):
                            gate = turn * i + z
                            r = n.result + 2 * gate
                            nxt = 2 * z + 2 if turn == 2 else 4
                            taps = lambda half: (
                                conv_w[:, ds(n.pair - layer * PAIRS + gate + half * PAIRS, 1), 1:2].rearrange("p o t -> p (o t)"),
                                conv_w[:, ds(n.pair - layer * PAIRS + gate + half * PAIRS, 1), 3:4].rearrange("p o t -> p (o t)"))
                            round_ring(2 * z + 1, n.unit // SLOTS + i + 1, r)
                            w1, b1 = taps(0)
                            act.wait_ge(result_ready, r + 1)
                            nc.scalar.activation(two(conv[0][:, 1:W + 1]), halves(acc[0]), ACT.Identity,
                                                 bias=b1, scale=w1).then_inc(centered, 1)
                            round_ring(nxt % SLOTS, n.unit // SLOTS + i + nxt // SLOTS + 1, r + 1)
                            act.wait_ge(result_taken, r + 1)
                            nc.scalar.activation(gated[:], conv[0][:, 1:W + 1], ACT.Silu).then_inc(silu_done, 1)
                            w1, b1 = taps(1)
                            act.wait_ge(result_ready, r + 2)
                            nc.scalar.activation(two(conv[1][:, 1:W + 1]), halves(acc[1]), ACT.Identity,
                                                 bias=b1, scale=w1).then_inc(centered, 1)
                            act.wait_ge(gated_done, n.pair + gate + 1)
                            nc.scalar.activation(g_hi[:, ds(gate, 1), :].rearrange("p o t -> p (o t)"), gated[:],
                                                 ACT.Copy).then_inc(g_rounded, 1)
                    after_ffn_in(n, layer, count)
                    last = part == 2
                    project(last, last and layer == DEPTH - 1)
                    after_project(n, squares=last)

            def fnet(layer):
                tables = fnet_tables()

                def table(j):
                    hi, _, size = tables[j]
                    u = n.unit + 1 + j
                    round_unit(u % SLOTS, u // SLOTS + 1, hi, size)

                if layer:
                    act.wait_ge(result_ready, n.result)
                table(0)
                table(1)
                norm(layer, SH1, SC1, table_after=lambda c: table(c) if c >= 2 else None)
                r = n.result
                for g in range(GROUPS):
                    for t in range(5):
                        take(r, [(freq[0][:, t, :], acc[r % 2][:, 0, :])])
                        r += 1
                    for m in range(2):
                        c = 2 * g + m
                        take(r, [(h_hi[:, c, CXS], acc[r % 2][:, 0, 0:CTX]), (h_hi[:, c, LTS], acc[r % 2][:, 1, :])])
                        r += 1
                n.result = r
                n.unit += TABLES
                project()
                after_project(n)

            def pool_mix(layer):
                def pooled_hi(c):
                    if c >= 1:
                        round_pooled(c - 1)

                def round_pooled(c):
                    act.wait_ge(pooled_full, c + 1)
                    for to, cols in ((CXS, slice(PC, PC + CTX)), (LTS, slice(PL, PL + LAT))):
                        done = nc.scalar.activation(h_hi[:, c, to], window[c % 2][:, cols], ACT.Copy)
                    done.then_inc(h_rounded, 1)

                norm(layer, SH1, SC1, target=pooled_hi)
                round_pooled(KC - 1)
                for j in range(KC):
                    if j % 2 == 0:
                        u = j // 2 + 1
                        round_ring(u % SLOTS, n.unit // SLOTS + u // SLOTS + 1, n.result + j)
                    act.wait_ge(result_taken, n.result + j + 1)
                    square(x[:, j, :])
                after_project(n, 4, 4)

            def mla(layer):
                act.wait_ge(table_loaded, TABLES_MLA)
                nc.scalar.activation(ckv_hi[:, :, LAT1:KEYS], cache[:, 0:RC, :], ACT.Copy)
                nc.scalar.activation(kpe_hi[:, LAT1:KEYS], cache[:, RC, :], ACT.Copy).then_inc(cache_rounded, 1)
                norm(layer, SH1, SC1)
                act.wait_ge(h_ready, n.chunk)
                act.dma_start(rows[:, 5:7, :], a["rope"]).then_inc(table_loaded, 16)
                r0, u0 = n.result, n.unit
                ring = lambda j, free: round_ring((u0 + j) % SLOTS, (u0 + j) // SLOTS + 1, free,
                                                  (LATENT_SIZES + [UNIT])[j])

                def latent(r, raw_, previous):
                    act.wait_ge(result_ready, r + 1)
                    if previous is not None:
                        act.wait_ge(result_taken, previous + 1)
                    nc.scalar.activation(two(raw_), halves(acc[r % 2]), ACT.Copy)
                    nc.scalar.activation(two(row(SQ)), halves(acc[r % 2]), ACT.Square).then_inc(latent_squared, 1)

                ready = [0, 1, 2, 3, 4, 5, 5, 6, 8, 9, 10, 11]
                for m in range(RC):
                    ring(m + 1, r0 + ready[m])
                    latent(r0 + m, ckv_raw[:, m, :], r0 + m - 1 if m else None)
                ring(5, r0 + ready[4])
                ring(6, r0 + ready[5])
                ring(7, r0 + ready[6])
                latent(r0 + 5, cq_raw[:, 0, :], r0 + 3)
                act.wait_ge(rope_step, 3)
                nc.scalar.activation(kpe_hi[:, 0:LAT1], kpe_sin[:, 0:LAT1], ACT.Copy
                                     ).then_inc(latent_rounded, 1)
                ring(8, r0 + ready[7])
                latent(r0 + 7, cq_raw[:, 1, :], r0 + 5)
                root(KV_RANK)
                for m in range(RC):
                    act.wait_ge(latent_normed, m + 1)
                    nc.scalar.activation(ckv_hi[:, m, 0:LAT1], ckv_raw[:, m, 0:LAT1], ACT.Copy
                                         ).then_inc(latent_rounded, 1)
                act.dma_start(a["state_ckv"], ckv_raw[:, :, CXS]).then_inc(stored, 16)
                act.dma_start(a["state_kpe"], kpe_raw[0:ROPE, CXS]).then_inc(stored, 16)
                for m in range(2, QC):
                    ring(m + 7, r0 + ready[m + 6])
                    latent(r0 + m + 6, cq_raw[:, m, :], r0 + m + 5)
                root(Q_RANK, rstd_q)
                act.wait_ge(cached, 2)
                for m in range(QC):
                    act.wait_ge(latent_normed, RC + m + 1)
                    nc.scalar.activation(cq_hi[:, m, :], cq_raw[:, m, :], ACT.Copy).then_inc(latent_rounded, 1)
                act.wait_ge(stored, 32)
                act.wait_ge(latent_ready, 1 + RC + QC)
                n.result += 12
                n.unit += 12
                with act.Fori(0, 2) as i:
                    for h2 in range(2):
                        attend(i, h2)
                n.result += 128
                n.unit += 24
                n.score += 40
                project()
                after_project(n)

            def attend(i, h2):
                r = n.result + 64 * i + 32 * h2
                s = n.score + 20 * i + 10 * h2

                def ring(j, free):
                    at_ = 6 * h2 + j
                    round_ring(at_ % SLOTS, n.unit // SLOTS + 3 * i + at_ // SLOTS + 1, free,
                               (HEAD_SIZES + [UNIT])[j])

                ring(1, r)
                for t in range(6):
                    take(r + t, [(v_hi[:, t, :], acc[t % 2][:, 0, 0:2 * VH])])
                ring(2, r + 6)
                ring(3, r + 7)
                act.wait_ge(rope_step, 5 + (2 * i + h2) * 3)
                nc.scalar.activation(qpe_hi[:], q_rot, ACT.Copy).then_inc(result_rounded, 1)
                for hh in range(2):
                    base = r + 8 + 12 * hh
                    act.wait_ge(result_ready, base + 1)
                    nc.scalar.activation(k_hi[:].rearrange("p (a b) -> p a b", a=2), acc[0][:, :, 0:KHALF],
                                         ACT.Copy).then_inc(result_rounded, 1)
                    ring(4 + 2 * hh, base + 1)
                    act.wait_ge(result_ready, base + 2)
                    nc.scalar.activation(two(q_hi[:]), halves(acc[1]), ACT.Copy).then_inc(result_rounded, 1)
                    if hh == 0:
                        ring(5, base + 2)

                    def exponentials(t):
                        q0, k0, width, banks = Q_TILES[t]
                        b = (5 * hh + t) % 2
                        act.wait_ge(bias_done, s + 5 * hh + t + 1)
                        nc.scalar.activation(
                            probs[b][:, 0:width * banks].rearrange("p (a b) -> p a b", a=banks),
                            sacc[b][:, 0:banks, 0:width], ACT.Exp, bias=negtop[:, b:b + 1], scale=SM_SCALE,
                            accum_out=total[:, b:b + 1]).then_inc(exp_done, 1)

                    def weigh(t):
                        q0, k0, width, banks = Q_TILES[t]
                        rt = base + 2 + 2 * t
                        tiles = width * banks // P
                        take(rt, transposed_pieces(pt_hi, acc[0], tiles))
                        take(rt + 1, [(head_out(h_hi, i, h2, hh, q0), acc[1][:, 0, 0:P])])

                    exponentials(0)
                    for t in range(1, 5):
                        exponentials(t)
                        weigh(t - 1)
                    weigh(4)

            def load_layer(layer):
                if layer:
                    act.wait_ge(result_taken, n.result)
                act.dma_start(conv_w[:], a["conv_w"][layer]).then_inc(layer_loaded, 16)
                if layer + 1 < DEPTH:
                    act.dma_start(b_ada[:, (layer + 1) % 2, :], a["b_ada"][layer + 1]).then_inc(layer_loaded, 16)

            act.dma_start(cond[:], a["cond"]).then_inc(loaded, 16)
            act.dma_start(b_ada[:, 0, :], a["b_ada"][0]).then_inc(loaded, 16)
            for c in range(KC):
                act.dma_start(x[:, c, :], a["x"][c]).then_inc(loaded, 16)
            for dst, name in ((ident, "ident"), (ones, "ones"), (perm, "perm"), (gains, "gains")):
                act.dma_start(dst[:], a[name]).then_inc(loaded, 16)
            act.wait_ge(loaded, SMALL_LOADS)
            act.wait_ge(setup_done, 1)
            nc.scalar.activation(cond[:], cond[:], ACT.Silu).then_inc(cond_ready, 1)
            for c in range(KC):
                if c:
                    act.wait_ge(summed, c)
                square(x[:, c, :])
            n.unit, n.ada, n.squared = MODS, MODS, KC
            load_layer(0)
            round_ring(0, n.unit // SLOTS + 1)
            for layer, kind in enumerate(MIXERS):
                if layer:
                    load_layer(layer)
                    if kind == "pool":
                        act.dma_start(inv_count[:], a["inv_count"]).then_inc(table_loaded, 16)
                    if kind == "mla":
                        act.wait_ge(result_ready, n.result)
                        act.dma_start(cache[:], a["cache"]).then_inc(table_loaded, 16)
                    n.unit += ADA_REST
                act.wait_ge(mod_ready, layer + 1)
                {"fnet": fnet, "pool": pool_mix, "mla": mla}[kind](layer)
                ffn(layer)
            root(D)
            for c in range(KC):
                act.wait_ge(y_ready, c + 1)
                act.dma_start(a["y"][c], y[:, c, :]).then_inc(stored, 16)
            act.wait_ge(stored, 32 + 16 * KC)

        @block.vector
        def _(dve):
            n = Counts()

            def recip(width_row):
                dve.wait_ge(rooted, n.stat + 1)
                nc.vector.reciprocal(width_row, width_row).then_inc(rstd_done, 1)
                n.stat += 1
                dve.wait_ge(rstd_done, n.stat)

            def clear_sum():
                nc.vector.memset(row(SUM), 0.0).then_inc(sum_cleared, 1)
                n.cleared += 1

            def scale_x(c):
                nc.vector.tensor_tensor(row(XN + c % 2), x[:, c, :], row(RSTD), ALU.mult).then_inc(xn_ready, 1)

            def lo_part(ready, hi, lo, full, inc, rounded=h_rounded):
                dve.wait_ge(rounded, ready)
                nc.vector.tensor_tensor(lo, full, hi.bitcast(f32), ALU.subtract).then_inc(inc, 1)

            def norm():
                recip(row(RSTD))
                clear_sum()
                scale_x(0)
                scale_x(1)
                for c in range(KC):
                    lo_part(n.chunk + c + 1, h_hi[:, c, :], h_lo[:, c, :], row(HF + c % 2), h_ready)
                    if c + 2 < KC:
                        scale_x(c + 2)
                n.chunk += KC

            def take(r, rounded, pieces):
                dve.wait_ge(result_rounded, rounded)
                for lo, hi, src in pieces:
                    done = nc.vector.tensor_tensor(lo, src, hi.bitcast(f32), ALU.subtract)
                done.then_inc(result_taken, 1)

            def project(gate, squares=True):
                if squares:
                    dve.wait_ge(sum_cleared, n.cleared)
                with dve.Fori(0, 2) as i:
                    for j in range(4):
                        update_x(4 * i + j, 4 * i + j, gate(4 * i + j), j % 2, squares)

            def update_x(c, j, gate, pair, squares):
                dve.wait_ge(result_ready, n.result + j + 1)
                for cond_, x0, x1, bank, p0 in ((0, 0, CTX, 0, 0), (1, LAT0, HALF, 0, LAT0), (1, HALF, LAT1, 1, 0)):
                    xs = x[:, ds(c, 1), x0:x1].rearrange("p o t -> p (o t)")
                    done = nc.vector.scalar_tensor_tensor(xs, acc[pair][:, bank, p0:p0 + x1 - x0], gate(cond_), xs,
                                                          ALU.mult, ALU.add)
                done.then_inc(result_taken, 1)
                if squares:
                    dve.wait_ge(summed, n.squared + j)
                    add_square(row(SUM), n.squared + j, summed)

            def add_square(total_, index, inc, ready=squared):
                dve.wait_ge(ready, index + 1)
                nc.vector.tensor_tensor(total_, total_, row(SQ), ALU.add).then_inc(inc, 1)

            def mod_gate(layer, which):
                return lambda c: lambda z: mod[:, layer % 2, ds(which + c, 1), z:z + 1].rearrange("p o t -> p (o t)")

            def take_ada(slot, use, source, layer, index):
                dve.wait_ge(unit_done[slot], use)
                nc.vector.tensor_scalar(
                    mod[:, layer % 2, ds(index, 1), :].rearrange("p o t -> p (o t)"), source,
                    b_ada[:, layer % 2, ds(index, 1)], None, ALU.add).then_inc(ada_taken, 1)

            def ffn(layer):
                norm()
                for t in conv:
                    nc.vector.memset(t[:, 0:1], 0.0)
                    nc.vector.memset(t[:, W + 1:W + 2], 0.0).then_inc(conv_padded, 1)
                dve.wait_ge(conv_padded, 2 * layer + 2)
                dve.wait_ge(layer_loaded, layer_loads(layer))
                for part, (_, count) in enumerate(PARTS):
                    turn = 1 if ada_in_ffn(layer) else 2
                    with dve.Fori(0, count // turn) as i:
                        for z in range(turn):
                            pair = n.pair + turn * i + z
                            for half in range(2):
                                k = 2 * pair + half
                                tap = lambda t: conv_w[:, ds(pair - layer * PAIRS + half * PAIRS, 1),
                                                       t:t + 1].rearrange("p o t -> p (o t)")
                                dve.wait_ge(centered, k + 1)
                                to = two(conv[half][:, 2:W + 2])
                                nc.vector.scalar_tensor_tensor(to, halves(acc[half]), tap(0), to, ALU.mult, ALU.add
                                                               ).then_inc(left_done, 1)
                                dve.wait_ge(left_done, k + 1)
                                to = two(conv[half][:, 0:W])
                                nc.vector.scalar_tensor_tensor(to, halves(acc[half]), tap(2), to, ALU.mult, ALU.add
                                                               ).then_inc(result_taken, 1)
                            dve.wait_ge(silu_done, pair + 1)
                            dve.wait_ge(result_taken, n.result + 2 * (turn * i + z) + 2)
                            nc.vector.tensor_tensor(gated[:], gated[:], conv[1][:, 1:W + 1], ALU.mult
                                                    ).then_inc(gated_done, 1)
                            dve.wait_ge(g_rounded, pair + 1)
                            gc = ds(turn * i + z, 1)
                            nc.vector.tensor_tensor(
                                g_lo[:, gc, :].rearrange("p o t -> p (o t)"), gated[:],
                                g_hi[:, gc, :].rearrange("p o t -> p (o t)").bitcast(f32), ALU.subtract
                            ).then_inc(g_ready, 1)
                        if turn == 1:
                            for j in range(2):
                                take_ada(2 + j, n.unit // SLOTS + i + 1, sacc[1][:, j, 0:2], layer + 1,
                                         n.ada - MODS * (layer + 1) + 2 * i + j)
                    after_ffn_in(n, layer, count)
                    project(mod_gate(layer, G2), part == 2)
                    after_project(n, squares=part == 2)

            def fnet(layer):
                norm()
                r = n.result
                for g in range(GROUPS):
                    for t in range(5):
                        n.rounded += 1
                        take(r, n.rounded, [(freq[1][:, t, :], freq[0][:, t, :], acc[r % 2][:, 0, :])])
                        r += 1
                    for m in range(2):
                        c = 2 * g + m
                        n.rounded += 1
                        take(r, n.rounded, [(h_lo[:, c, CXS], h_hi[:, c, CXS], acc[r % 2][:, 0, 0:CTX]),
                                            (h_lo[:, c, LTS], h_hi[:, c, LTS], acc[r % 2][:, 1, :])])
                        r += 1
                n.result = r
                n.unit += TABLES
                project(mod_gate(layer, G1))
                after_project(n)

            def pool_mix(layer):
                steps = [0]

                def step(ins):
                    steps[0] += 1
                    ins.then_inc(pool_step, 1)
                    dve.wait_ge(pool_step, steps[0])

                for t in padded:
                    for lo, hi in ((0, PC), (PC + CTX, PL), (PL + LAT, PADW)):
                        last = nc.vector.memset(t[:, lo:hi], 0.0)
                step(last)
                for z in range(2):
                    last = nc.vector.tensor_tensor(gate_pool[:, :, z], mod[:, layer % 2, G1:G1 + KC, z],
                                                   pool_scale, ALU.mult)
                step(last)
                dve.wait_ge(table_loaded, TABLES_POOL)
                recip(row(RSTD))
                clear_sum()
                scale_x(0)
                scale_x(1)
                for c in range(KC):
                    dve.wait_ge(h_full, n.chunk + c + 1)
                    if c + 2 < KC:
                        scale_x(c + 2)
                    source, lo, hi = padded[c % 2], 0, PADW
                    levels = c // 2 + 1
                    a_, b_ = window[c % 2], scratch
                    outs = [a_ if (levels - l) % 2 == 0 else b_ for l in range(levels)]
                    for level in range(levels):
                        back = 1 if level == 0 else 2 ** (level - 1)
                        ahead = 0 if level == 0 else back
                        lo, hi = lo + back, hi - ahead
                        out = outs[level]
                        step(nc.vector.tensor_tensor(out[:, lo:hi], source[:, lo - back:hi - back],
                                                     source[:, lo + ahead:hi + ahead], ALU.add))
                        source = out
                    out = window[c % 2]
                    step(nc.vector.tensor_tensor(out[:, PC:PL + LAT], source[:, PC:PL + LAT],
                                                 inv_count[:, c // 2, PC:PL + LAT], ALU.mult))
                    nc.vector.tensor_tensor(out[:, PC:PL + LAT], out[:, PC:PL + LAT], padded[c % 2][:, PC:PL + LAT],
                                            ALU.subtract).then_inc(pooled_full, 1)
                    dve.wait_ge(pooled_full, c + 1)
                    if c >= 1:
                        pooled_lo(c - 1)
                pooled_lo(KC - 1)
                n.chunk += KC
                for c in range(KC):
                    update_x(c, c, lambda z: gate_pool[:, c, z:z + 1], c % 2, True)
                after_project(n, 4, 4)

            def pooled_lo(c):
                dve.wait_ge(h_rounded, n.chunk + c + 1)
                for to, cols in ((CXS, slice(PC, PC + CTX)), (LTS, slice(PL, PL + LAT))):
                    done = nc.vector.tensor_tensor(h_lo[:, c, to], window[c % 2][:, cols],
                                                   h_hi[:, c, to].bitcast(f32), ALU.subtract)
                done.then_inc(h_ready, 1)

            def mla(layer):
                for t in (ckv_hi, ckv_lo):
                    nc.vector.memset(t[:, :, KEYS:KW].bitcast(f32), 0.0)
                nc.vector.memset(kpe_lo[:, KEYS:KW].bitcast(f32), 0.0).then_inc(cached, 1)
                dve.wait_ge(cache_rounded, 1)
                nc.vector.tensor_tensor(kpe_lo[:, LAT1:KEYS], cache[:, RC, :], kpe_hi[:, LAT1:KEYS].bitcast(f32),
                                        ALU.subtract)
                nc.vector.tensor_tensor(ckv_lo[:, :, LAT1:KEYS], cache[:, 0:RC, :],
                                        ckv_hi[:, :, LAT1:KEYS].bitcast(f32), ALU.subtract).then_inc(cached, 1)
                norm()
                r0 = n.result
                dve.wait_ge(sum_cleared, n.cleared)
                for m in range(RC):
                    if m:
                        dve.wait_ge(result_taken, r0 + m)
                    add_square(row(SUM), m, result_taken, latent_squared)
                dve.wait_ge(result_ready, r0 + 5)
                nc.vector.tensor_copy(two(kpe_raw[:]), halves(acc[(r0 + 4) % 2])).then_inc(result_taken, 1)
                dve.wait_ge(result_taken, r0 + 5)
                dve.wait_ge(table_loaded, TABLES_ROPE)
                nc.vector.tensor_tensor(kpe_cos[:], kpe_raw[:], tab_cos, ALU.mult).then_inc(rope_step, 1)
                nc.vector.memset(sum_q, 0.0).then_inc(rope_step, 1)
                dve.wait_ge(rope_step, 2)
                add_square(sum_q, RC, result_taken, latent_squared)
                dve.wait_ge(result_ready, r0 + 7)
                nc.vector.tensor_tensor(two(kpe_sin[:]), halves(acc[(r0 + 6) % 2]), two(tab_sin), ALU.mult
                                        ).then_inc(result_taken, 1)
                dve.wait_ge(result_taken, r0 + 7)
                nc.vector.tensor_tensor(kpe_sin[:], kpe_sin[:], kpe_cos[:], ALU.add).then_inc(rope_step, 1)
                dve.wait_ge(rope_step, 3)
                lo_part(1, kpe_hi[:, 0:LAT1], kpe_lo[:, 0:LAT1], kpe_sin[:, 0:LAT1], latent_ready, latent_rounded)
                add_square(sum_q, RC + 1, result_taken, latent_squared)
                recip(row(RSTD))

                def normed(raw_, gain, rstd, width=W):
                    nc.vector.scalar_tensor_tensor(raw_, raw_, gain, rstd, ALU.mult, ALU.mult
                                                   ).then_inc(latent_normed, 1)

                for m in range(RC):
                    normed(ckv_raw[:, m, :], g_kv[:, m:m + 1], row(RSTD))
                dve.wait_ge(latent_normed, RC)
                for m in range(RC):
                    lo_part(2 + m, ckv_hi[:, m, 0:LAT1], ckv_lo[:, m, 0:LAT1], ckv_raw[:, m, 0:LAT1],
                            latent_ready, latent_rounded)
                for m in range(2, QC):
                    dve.wait_ge(result_taken, r0 + 6 + m)
                    add_square(sum_q, RC + m, result_taken, latent_squared)
                recip(rstd_q)
                for m in range(QC):
                    normed(cq_raw[:, m, :], g_q[:, m:m + 1], rstd_q)
                dve.wait_ge(latent_normed, RC + QC)
                for m in range(QC):
                    lo_part(RC + 2 + m, cq_hi[:, m, :], cq_lo[:, m, :], cq_raw[:, m, :], latent_ready, latent_rounded)
                n.result += 12
                n.unit += 12
                for t in (top, total):
                    nc.vector.memset(t[:], 0.0).then_inc(score_taken, 1)
                with dve.Fori(0, 2) as i:
                    for h2 in range(2):
                        attend(i, h2)
                n.result += 128
                n.rounded += 4 * 31
                n.unit += 24
                n.score += 40
                clear_sum()
                dve.wait_ge(sum_cleared, n.cleared)
                project(mod_gate(layer, G1))
                after_project(n)

            def attend(i, h2):
                r = n.result + 64 * i + 32 * h2
                s = n.score + 20 * i + 10 * h2
                rounded = n.rounded + 62 * i + 31 * h2
                ropes = 3 + (2 * i + h2) * 3
                for t in range(6):
                    take(r + t, rounded + t + 1, [(v_lo[:, t, :], v_hi[:, t, :], acc[t % 2][:, 0, 0:2 * VH])])
                dve.wait_ge(result_ready, r + 7)
                nc.vector.tensor_copy(two(q_raw), halves(acc[0])).then_inc(result_taken, 1)
                dve.wait_ge(result_ready, r + 8)
                nc.vector.tensor_tensor(two(q_rot), halves(acc[1]), two(tab_sin), ALU.mult).then_inc(result_taken, 1)
                nc.vector.tensor_tensor(q_raw, q_raw, tab_cos, ALU.mult).then_inc(rope_step, 1)
                dve.wait_ge(result_taken, r + 8)
                dve.wait_ge(rope_step, ropes + 1)
                nc.vector.tensor_tensor(q_rot, q_rot, q_raw, ALU.add).then_inc(rope_step, 1)
                dve.wait_ge(result_rounded, rounded + 7)
                nc.vector.tensor_tensor(qpe_lo[:], q_rot, qpe_hi[:].bitcast(f32), ALU.subtract).then_inc(rope_step, 1)
                for hh in range(2):
                    base = r + 8 + 12 * hh
                    rb = rounded + 7 + 12 * hh
                    take(base, rb + 1, [(k_lo[:].rearrange("p (a b) -> p a b", a=2),
                                         k_hi[:].rearrange("p (a b) -> p a b", a=2), acc[0][:, :, 0:KHALF])])
                    take(base + 1, rb + 2, [(two(q_lo[:]), two(q_hi[:]), halves(acc[1]))])

                    def softmax(t):
                        q0, k0, width, banks = Q_TILES[t]
                        b = (5 * hh + t) % 2
                        k = s + 5 * hh + t + 1
                        dve.wait_ge(score_ready, k)
                        nc.vector.tensor_reduce(top[:, b:b + 1], sacc[b][:, 0:banks, 0:width], AX.XY, ALU.max
                                                ).then_inc(top_done, 1)
                        dve.wait_ge(top_done, k)
                        nc.vector.tensor_scalar(negtop[:, b:b + 1], top[:, b:b + 1], -SM_SCALE, None, ALU.mult
                                                ).then_inc(bias_done, 1)
                        dve.wait_ge(exp_done, k)
                        nc.vector.reciprocal(inverse[:, b:b + 1], total[:, b:b + 1]).then_inc(inverse_done, 1)
                        dve.wait_ge(inverse_done, k)
                        pr = probs[b][:, 0:width * banks]
                        nc.vector.tensor_scalar(pr, pr, inverse[:, b:b + 1], None, ALU.mult).then_inc(score_taken, 1)

                    def weigh(t):
                        q0, k0, width, banks = Q_TILES[t]
                        tiles = width * banks // P
                        take(None, rb + 3 + 2 * t, [(lo, hi, src) for (lo, src), (hi, _) in zip(
                            transposed_pieces(pt_lo, acc[0], tiles), transposed_pieces(pt_hi, acc[0], tiles))])
                        take(None, rb + 4 + 2 * t, [(head_out(h_lo, i, h2, hh, q0), head_out(h_hi, i, h2, hh, q0),
                                                     acc[1][:, 0, 0:P])])

                    softmax(0)
                    for t in range(1, 5):
                        softmax(t)
                        weigh(t - 1)
                    weigh(4)

            nc.vector.memset(rows[:], 0.0)
            nc.vector.memset(eps[:], EPS).then_inc(setup_done, 1)
            dve.wait_ge(loaded, SMALL_LOADS)
            dve.wait_ge(setup_done, 1)
            for c in range(KC):
                if c:
                    dve.wait_ge(summed, c)
                add_square(row(SUM), c, summed)
            with dve.Fori(0, MODS // 4) as i:
                for j in range(4):
                    take_ada(j, i + 1, sacc[j // 2][:, j % 2, 0:2], 0, 4 * i + j)
            n.unit, n.ada, n.squared = MODS, MODS, KC
            for layer, kind in enumerate(MIXERS):
                dve.wait_ge(ada_taken, n.ada)
                nc.vector.tensor_scalar(mod[:, layer % 2, SC1:SC1 + KC, :], mod[:, layer % 2, SC1:SC1 + KC, :],
                                        1.0, None, ALU.add)
                nc.vector.tensor_scalar(mod[:, layer % 2, SC2:SC2 + KC, :], mod[:, layer % 2, SC2:SC2 + KC, :],
                                        1.0, None, ALU.add).then_inc(mod_ready, 1)
                if layer:
                    for j in range(ADA_REST):
                        u = n.unit + 1 + j
                        take_ada(u % SLOTS, u // SLOTS + 1, sacc[1][:, j % 2, 0:2], layer, MODS - ADA_REST + j)
                    n.unit += ADA_REST
                    n.ada += ADA_REST
                {"fnet": fnet, "pool": pool_mix, "mla": mla}[kind](layer)
                ffn(layer)
            recip(row(RSTD))
            for c in range(KC):
                nc.vector.scalar_tensor_tensor(y[:, c, :], x[:, c, :], g_final[:, c:c + 1], row(RSTD),
                                               ALU.mult, ALU.mult).then_inc(y_ready, 1)


def _weight_units(w, rows=None, cols=None):
    k, m = w.shape
    u = w.reshape(k // P, P, m // P, P).transpose(2, 1, 0, 3).reshape(m // P, P, k)
    return _padded(u)


def _padded(u):
    out = np.zeros((u.shape[0], P, UNIT), np.float32)
    out[:, :, :u.shape[2]] = u
    return out


def _fourier_units():
    def angle(size):
        i = np.arange(size)
        return 2 * np.pi * ((i[:, None] * i[None, :]) % size) / size
    ch, cx, sq = angle(GROUP), angle(CTX), angle(LAT)
    chan = np.concatenate([np.cos(ch), np.sin(ch)], 1) / np.sqrt(GROUP)
    units = [chan.reshape(2, P, 2 * GROUP)]
    units += [t[None] / np.sqrt(CTX) for t in (np.cos(cx), -np.sin(cx))]
    for t in (np.cos(sq), -np.sin(sq)):
        units.append((t / np.sqrt(LAT)).reshape(2, 2, P, LAT).transpose(0, 2, 1, 3).reshape(2, P, 2 * LAT))
    return np.concatenate([_padded(u.astype(np.float32)) for u in units])


def _stream(w):
    ada = [_weight_units(w["w_ada"][l]) for l in range(DEPTH)]
    out = [ada[0]]
    f = 0
    for layer, kind in enumerate(MIXERS):
        rest = [ada[layer][MODS - ADA_REST:]] if layer else []
        if kind == "fnet":
            u = _weight_units(w["w_fnet"][f])
            f += 1
            out += [u[:1], *rest, _fourier_units(), u[1:]]
        elif kind == "pool":
            g = w["w_pool"][0].reshape(GROUPS, 2, P, 2, P).transpose(0, 2, 3, 1, 4).reshape(GROUPS, P, 4 * P)
            u = _padded(g)
            out += [u[:1], *rest, u[1:]]
        else:
            dkv = w["w_dkv"][0]
            ckv = _weight_units(dkv[:, :KV_RANK])
            kpe = np.concatenate([dkv[:, KV_RANK:]] * 2, 1)
            kpe = np.concatenate([_weight_units(kpe[:D // 2]), _weight_units(kpe[D // 2:])])
            out += [ckv[:1], *rest, ckv[1:], kpe, _weight_units(w["w_dq"][0])]
            uq = w["w_uq"][0].reshape(Q_RANK, HEADS, NOPE + ROPE)
            ukv = w["w_ukv"][0].reshape(KV_RANK, HEADS, NOPE + VH)
            for h in range(0, HEADS, 2):
                v = ukv[:, h:h + 2, NOPE:].reshape(RC, P, 2 * VH).transpose(1, 0, 2).reshape(1, P, RC * 2 * VH)
                out += [v, _weight_units(uq[:, h:h + 2, NOPE:].reshape(Q_RANK, 2 * ROPE))]
                for k in (h, h + 1):
                    out += [_weight_units(ukv[:, k, :NOPE]), _weight_units(uq[:, k, :NOPE])]
            out += [_weight_units(w["w_o"][0])]
        w_in, w_out = _weight_units(w["w_ffn_in"][layer]), w["w_ffn_out"][layer]
        for first, count in PARTS:
            for p in range(first, first + count):
                out += [w_in[p:p + 1], w_in[PAIRS + p:PAIRS + p + 1]]
                if ada_in_ffn(layer):
                    out.append(ada[layer + 1][2 * p:2 * p + 2])
            out.append(_weight_units(w_out[first * P:(first + count) * P]))
    return np.concatenate(out)


def _tokens(ctx_t, lat_t):
    c = ctx_t.shape[0]
    out = np.zeros((c // P, P, W), np.float32)
    out[:, :, 0:CTX] = ctx_t.reshape(c // P, P, CTX)
    out[:, :, LAT0:LAT1] = lat_t.reshape(c // P, P, LAT)
    return out


def _rope_tables():
    grid_w, axis = 64, ROPE // 2
    inv = (1.0 / (np.float32(10000.0) ** (np.arange(0, axis, 2, dtype=np.float32) / np.float32(axis)))).astype(np.float32)
    t = np.arange(LAT)
    out = np.zeros((P, 2, W), np.float32)
    out[:, 0, 0:CTX] = 1.0
    swap = np.zeros((P, P), np.float32)
    for p in range(P):
        d = p % ROPE
        pos = (t // grid_w if d < axis else t % grid_w).astype(np.float32)
        ang = pos * inv[d % (axis // 2)]
        upper = d % axis >= axis // 2
        out[p, 0, LAT0:LAT1] = np.cos(ang)
        out[p, 1, LAT0:LAT1] = np.sin(ang) if upper else -np.sin(ang)
        swap[p - axis // 2 if upper else p + axis // 2, p] = 1.0
    return out, swap


def _inverse_counts():
    out = np.zeros((4, PADW), np.float32)
    for g in range(4):
        w = 2 ** (g + 1)
        for start, size in ((PC, CTX), (PL, LAT)):
            t = np.arange(size)
            lo, hi = np.clip(t - w // 2, 0, size), np.clip(t - w // 2 + w, 0, size)
            out[g, start:start + size] = 1.0 / (hi - lo)
    return np.ascontiguousarray(np.broadcast_to(out, (P, 4, PADW)))


def _columns(v):
    return np.moveaxis(v.reshape(*v.shape[:-1], -1, P), -1, -2)


def kernel(**inputs):
    import concourse.bacc as bacc
    from concourse.bass_utils import run_bass_kernel_spmd

    w = {k: np.asarray(v) for k, v in inputs.items()}
    rope, swap = _rope_tables()
    conv = np.concatenate([w["w_ffn_conv"], w["b_ffn_conv"][:, None]], 1)
    cache = np.zeros((P, RC + 1, PAST), np.float32)
    cache[:, :RC] = w["cache_ckv"][0, 0].T.reshape(RC, P, PAST).transpose(1, 0, 2)
    cache[:, RC] = np.concatenate([w["cache_kpe"][0, 0].T] * 2, 0)
    arrays = {
        "stream": _stream(w),
        "x": _tokens(w["x_prompt"][0].T, w["x_sample"][0].T),
        "cond": np.stack([_columns(w["c_ctx"]), _columns(w["c"][0])], -1),
        "b_ada": _columns(w["b_ada"]),
        "conv_w": _columns(conv).transpose(0, 2, 3, 1),
        "gains": np.concatenate([_columns(w["g_q"][0]), _columns(w["g_kv"][0]), _columns(w["g_final"]),
                                 _columns(w["pool_scale"][0])], 1),
        "cache": cache,
        "rope": rope,
        "perm": swap,
        "ident": np.eye(P, dtype=np.float32),
        "ones": np.ones((P, P), np.float32),
        "inv_count": _inverse_counts(),
    }
    arrays = {k: np.ascontiguousarray(v) for k, v in arrays.items()}
    outs = {"y": (KC, P, W), "state_ckv": (P, RC, CTX), "state_kpe": (ROPE, CTX)}
    nc = bacc.Bacc("TRN2", target_bir_lowering=False, num_devices=1)
    f32 = mybir.dt.float32
    aps = {k: nc.dram_tensor(f"in_{k}", v.shape, f32, kind="ExternalInput").ap() for k, v in arrays.items()}
    aps |= {k: nc.dram_tensor(f"out_{k}", s, f32, kind="ExternalOutput").ap() for k, s in outs.items()}
    build_backbone(nc, aps)
    r = run_bass_kernel_spmd(nc, [{f"in_{k}": v for k, v in arrays.items()}], core_ids=[0]).results[0]
    y = r["out_y"].reshape(D, W)
    ckv = r["out_state_ckv"].transpose(1, 0, 2).reshape(KV_RANK, CTX)
    return (np.ascontiguousarray(y[:, :CTX].T)[None], np.ascontiguousarray(y[:, LAT0:LAT1].T)[None],
            np.ascontiguousarray(ckv.T)[None, None], np.ascontiguousarray(r["out_state_kpe"].T)[None, None])
```

```python
from contextlib import ExitStack

import concourse.bass as bass
import numpy as np
from concourse import mybir

P = 128
D = 1024
KC = D // P
CTX, LAT, PAST = 128, 512, 128
GAP = 2
LAT0 = CTX + GAP
LAT1 = LAT0 + LAT
W = LAT1 + GAP
HALF = W // 2
DEPTH = 4
N_MOD = 6
MODS = N_MOD * KC
D_FF = 2816
PAIRS = D_FF // P
PARTS = [(0, 8), (8, 8), (16, 6)]
GROUPS, GROUP = 4, 256
HEADS, NOPE, ROPE, VH = 8, 128, 64, 128
Q_RANK, KV_RANK = 768, 512
QC, RC = Q_RANK // P, KV_RANK // P
SM_SCALE = (NOPE + ROPE) ** -0.5
EPS = 1e-6
UNIT = 1024
SLOTS = 4
KEYS = LAT1 + PAST
KW = KEYS + GAP
KHALF = KW // 2
NK = LAT + PAST
SHALF = NK // 2
KTILES = NK // P
PADW = 8 + CTX + 8 + LAT + 8
PC, PL = 8, 8 + CTX + 8
MIXERS = ["fnet", "pool", "mla", "fnet"]
SH1, SC1, G1, SH2, SC2, G2 = (KC * i for i in range(N_MOD))

TABLES = 6
LATENT_SIZES = [UNIT] * RC + [UNIT // 2] * 2 + [UNIT] * QC
HEAD_SIZES = [RC * 2 * VH, QC * P, RC * P, QC * P, RC * P, QC * P]
Q_TILES = [(LAT0 + P * t, LAT0, SHALF, 2) for t in range(4)] + [(0, 0, CTX, 1)]
FIRST_LOADS = 16 * 3
SMALL_LOADS = 16 * (KC + 3)
TABLES_POOL, TABLES_MLA, TABLES_ROPE = 16, 32, 48


def layer_loads(layer):
    return 16 * (2 * layer + min(2, DEPTH - layer))


def ada_in_ffn(layer):
    return layer + 1 < DEPTH


def ada_rest(layer):
    return 2 * (layer > 0) + 2 * (layer + 1 < DEPTH)


class Counts:

    def __init__(self):
        self.unit = 0
        self.result = 0
        self.ada = 0
        self.pair = 0
        self.rounded = 0
        self.norm = 0
        self.stat = 0
        self.chunk = 0
        self.squared = 0
        self.score = 0
        self.cleared = 0


def wait_past(engine, semaphore, count):
    if not (isinstance(count, int) and count == 0):
        engine.wait_ge(semaphore, count)


def build_backbone(nc, a):
    f32, f32r = mybir.dt.float32, mybir.dt.float32r
    ACT = mybir.ActivationFunctionType
    ALU = mybir.AluOpType
    AX = mybir.AxisListType
    ds = bass.ds
    n_units = a["stream"].shape[0]

    with ExitStack() as ctx:
        sem = lambda name: ctx.enter_context(nc.semaphore(name))
        pb = lambda name, shape: ctx.enter_context(nc.psum_tensor(name, shape, f32))
        at = [(nc.sbuf_base + 31) // 32 * 32]

        def place(name, shape, dt=f32, offset=None):
            size = 4 * int(np.prod(shape[1:]))
            where = at[0] if offset is None else offset
            if offset is None:
                at[0] += size
            assert where + size <= nc.sbuf_usable_end, name
            return nc.alloc_sbuf_tensor_at(name, shape, dt, offset=where, align_bytes=4)

        x = place("x", [P, KC, W])
        h_at = at[0]
        h_hi, h_lo = place("h_hi", [P, KC, W], f32r), place("h_lo", [P, KC, W], f32r)
        raw = [place(f"raw{s}", [P, UNIT]) for s in range(SLOTS)]
        w_hi = [place(f"w_hi{s}", [P, UNIT], f32r) for s in range(2)]
        w_lo = [place(f"w_lo{s}", [P, UNIT], f32r) for s in range(2)]
        rows = place("rows", [P, 7, W])
        mod = place("mod", [P, 2, MODS, 2])
        b_ada = place("b_ada", [P, 2, MODS, 2])
        conv_w = place("conv_w", [P, 2 * PAIRS, 4])
        ident, ones, perm = place("ident", [P, P]), place("ones", [P, P]), place("perm", [P, P])
        cond = place("cond", [P, KC, 2])
        cond_parts = place("cond_parts", [P, KC, 4], f32r)
        hi_plus_lo = place("hi_plus_lo", [4, 2])
        gains = place("gains", [P, QC + RC + 2 * KC])
        g_q, g_kv = gains[:, 0:QC], gains[:, QC:QC + RC]
        g_final = gains[:, QC + RC:QC + RC + KC]
        pool_scale = gains[:, QC + RC + KC:]
        eps = place("eps", [P, 1])
        gate_pool = place("gate_pool", [P, KC, 2])
        top, negtop, total, inverse = (place(n, [P, 2]) for n in ("top", "negtop", "total", "inverse"))
        g_at = at[0]
        g_hi, g_lo = place("g_hi", [P, 8, W], f32r), place("g_lo", [P, 8, W], f32r)
        seq_t = [[place(f"seq_t{c}{p}", [P, 4, LAT], f32r, g_at + (2 * c + p) * 8192) for p in range(2)]
                 for c in range(2)]
        ctx_t = [place(f"ctx_t{p}", [P, 2, CTX], f32r, g_at + 32768 + 1024 * p) for p in range(2)]
        cq_hi = place("cq_hi", [P, QC, W], f32r, g_at)
        cq_lo = place("cq_lo", [P, QC, W], f32r, g_at + 4 * QC * W)
        cache = place("cache", [P, RC + 1, PAST], f32, g_at)
        tail = g_at + 8 * QC * W
        ckv_raw = place("ckv_raw", [P, RC, W], f32, tail)
        q_hi, q_lo = place("q_hi", [P, W], f32r, tail), place("q_lo", [P, W], f32r, tail + 4 * W)
        pt_hi = place("pt_hi", [P, KTILES, P], f32r, tail + 8 * W)
        pt_lo = place("pt_lo", [P, KTILES, P], f32r, tail + 8 * W + 4 * NK)
        e_at = at[0]
        conv = [place(f"conv{j}", [P, W + 2], f32, e_at + 4 * (W + 2) * j) for j in range(2)]
        gated = place("gated", [P, W], f32, e_at + 8 * (W + 2))
        chan_t = [place(f"chan_t{p}", [P, 2, 2 * GROUP], f32r, e_at + 4096 * p) for p in range(2)]
        freq = [place(f"freq{p}", [P, 5, 2 * GROUP], f32r, e_at + 8192 + 10240 * p) for p in range(2)]
        inv_count = place("inv_count", [P, 4, PADW], f32, e_at)
        padded = [place(f"padded{j}", [P, PADW], f32, e_at + 4 * PADW * (4 + j)) for j in range(2)]
        window = [place(f"window{j}", [P, PADW], f32, e_at + 4 * PADW * (6 + j)) for j in range(2)]
        scratch = place("scratch", [P, PADW], f32, e_at + 4 * PADW * 8)
        y = place("y", [P, KC, W], f32, g_at)
        ckv_hi, ckv_lo = place("ckv_hi", [P, RC, KW], f32r), place("ckv_lo", [P, RC, KW], f32r)
        kpe_hi, kpe_lo = place("kpe_hi", [P, KW], f32r), place("kpe_lo", [P, KW], f32r)
        v_at = at[0]
        v_hi, v_lo = place("v_hi", [P, 6, 2 * VH], f32r), place("v_lo", [P, 6, 2 * VH], f32r)
        k_hi, k_lo = place("k_hi", [P, KW], f32r), place("k_lo", [P, KW], f32r)
        qpe_hi, qpe_lo = place("qpe_hi", [P, W], f32r), place("qpe_lo", [P, W], f32r)
        cq_raw = place("cq_raw", [P, QC, W], f32, v_at)
        kpe_raw, kpe_cos, kpe_sin = (place(f"kpe_{n}", [P, W], f32, v_at + 4 * W * (QC + j))
                                     for j, n in enumerate(("raw", "cos", "sin")))
        a_at = at[0] - 4 * (4 * UNIT + 2 * P)
        a_hi = [place(f"a_hi{u}", [P, UNIT], f32r, a_at + 4 * UNIT * u) for u in range(2)]
        a_lo = [place(f"a_lo{u}", [P, UNIT], f32r, a_at + 4 * UNIT * (2 + u)) for u in range(2)]
        ada_row = place("ada_row", [4, 2 * P], f32, a_at + 16 * UNIT)
        SUM, SQ, RSTD, XN, HF = 0, 1, 2, 3, 5
        row = lambda i: rows[:, i, :]
        tab_cos, tab_sin = row(5), row(6)
        sum_q, rstd_q = row(3), row(4)
        probs = [row(3), row(4)]
        q_raw, q_rot = row(0), row(1)

        acc = [pb("acc0", [P, 2, 512]), pb("acc1", [P, 2, 512])]
        sacc = [pb("sacc0", [P, 2, 512]), pb("sacc1", [P, 2, 512])]
        halves = lambda t: t[:, :, 0:HALF]
        two = lambda ap: ap.rearrange("p (a b) -> p a b", a=2)

        first_loaded = sem("first_loaded")
        loaded = sem("loaded")
        layer_loaded = sem("layer_loaded")
        table_loaded = sem("table_loaded")
        raw_ready = [sem(f"raw_ready{s}") for s in range(SLOTS)]
        unit_done = [sem(f"unit_done{s}") for s in range(SLOTS)]
        weights_hi = sem("weights_hi")
        result_ready = sem("result_ready")
        result_taken = sem("result_taken")
        result_rounded = sem("result_rounded")
        ada_rows = sem("ada_rows")
        ada_evacuated = sem("ada_evacuated")
        ada_cols = sem("ada_cols")
        ada_taken = sem("ada_taken")
        cond_rounded = sem("cond_rounded")
        cond_parts_ready = sem("cond_parts_ready")
        cond_ready = sem("cond_ready")
        centered = sem("centered")
        left_done = sem("left_done")
        silu_done = sem("silu_done")
        gated_done = sem("gated_done")
        g_rounded = sem("g_rounded")
        g_ready = sem("g_ready")
        squared = sem("squared")
        summed = sem("summed")
        stat_ready = sem("stat_ready")
        rooted = sem("rooted")
        rstd_done = sem("rstd_done")
        xn_ready = sem("xn_ready")
        h_full = sem("h_full")
        h_rounded = sem("h_rounded")
        h_ready = sem("h_ready")
        mod_ready = sem("mod_ready")
        setup_done = sem("setup_done")
        pool_step = sem("pool_step")
        pooled_full = sem("pooled_full")
        rope_step = sem("rope_step")
        raw_copied = sem("raw_copied")
        score_ready = sem("score_ready")
        score_taken = sem("score_taken")
        top_done = sem("top_done")
        bias_done = sem("bias_done")
        exp_done = sem("exp_done")
        inverse_done = sem("inverse_done")
        latent_normed = sem("latent_normed")
        latent_squared = sem("latent_squared")
        latent_rounded = sem("latent_rounded")
        latent_ready = sem("latent_ready")
        sum_cleared = sem("sum_cleared")
        conv_padded = sem("conv_padded")
        cached = sem("cached")
        cache_rounded = sem("cache_rounded")
        stored = sem("stored")
        y_ready = sem("y_ready")

        block = ctx.enter_context(nc.Block())

        CXS, LTS = slice(0, CTX), slice(LAT0, LAT1)

        def fnet_tables():
            out = [(t[0][:].rearrange("p a b -> p (a b)"), t[1][:].rearrange("p a b -> p (a b)"), size)
                   for t, size in ((chan_t, UNIT), (ctx_t, 2 * CTX))]
            flat = lambda t, k: t[:, 2 * k:2 * k + 2, :].rearrange("p a b -> p (a b)")
            out += [(flat(seq_t[c][0], k), flat(seq_t[c][1], k), UNIT) for c in range(2) for k in range(2)]
            return out

        def transposed_pieces(dst, src, tiles):
            flat = lambda z0, z1: dst[:, z0:z1, :].rearrange("p a b -> p (a b)")
            if tiles == 1:
                return [(flat(0, 1), src[:, 0, 0:P])]
            return [(flat(0, 4), src[:, 0, :]), (flat(4, 5), src[:, 1, 0:P])]

        def head_out(dst, i, h2, hh, q0):
            return dst[:, ds(4 * i + 2 * h2 + hh, 1), q0:q0 + P].rearrange("p o t -> p (o t)")

        def after_ffn_in(n, layer, count):
            n.unit += 4 * count if ada_in_ffn(layer) else 2 * count
            n.result += 2 * count
            n.pair += count
            n.ada += count if ada_in_ffn(layer) else 0

        def after_project(n, units=KC, squares=True):
            n.unit += units
            n.result += KC
            n.squared += KC if squares else 0

        def after_norm(n):
            n.norm += 1
            n.stat += 1
            n.chunk += KC

        @block.sync
        def _(sp):
            for s in range(SLOTS):
                sp.dma_start(raw[s][:], a["stream"][s]).then_inc(raw_ready[s], 16)
            with sp.Fori(1, n_units // SLOTS) as i:
                for s in range(SLOTS):
                    sp.wait_ge(unit_done[s], i)
                    sp.dma_start(raw[s][:], a["stream"][ds(i * SLOTS + s, 1)].rearrange("o p n -> (o p) n")
                                 ).then_inc(raw_ready[s], 16)

        @block.gpsimd
        def _(pool):
            n = Counts()

            def cut(slot, split, hi, lo, raw_size):
                pool.wait_ge(weights_hi, split + 1)
                nc.gpsimd.tensor_tensor(lo, raw[slot][:, 0:raw_size], hi.bitcast(f32), ALU.subtract
                                        ).then_inc(unit_done[slot], 1)

            def ring(slot, split, size=UNIT):
                cut(slot, split, w_hi[slot % 2][:, 0:size], w_lo[slot % 2][:, 0:size], size)

            def pair_of_modulation(slot, split):
                for u in range(2):
                    cut(slot + u, split + u, a_hi[u][:], a_lo[u][:], UNIT)

            def project(size, last=False):
                next_size = UNIT
                with pool.Fori(0, 1) as i:
                    for j in range(4):
                        ring((j + 2) % SLOTS, n.unit + 2 + j, size)
                for j in range(2 if last else 4):
                    ring((j + 2) % SLOTS, n.unit + 6 + j, size if j < 2 else next_size)

            def ffn(layer):
                for part, (_, count) in enumerate(PARTS):
                    if ada_in_ffn(layer):
                        with pool.Fori(0, count) as i:
                            base = n.unit + 4 * i + 2
                            ring(0, base)
                            pair_of_modulation(2, base + 1)
                            ring(1, base + 3)
                    else:
                        with pool.Fori(0, count // 2) as i:
                            for j in range(4):
                                ring((j + 2) % SLOTS, n.unit + 4 * i + 2 + j)
                    after_ffn_in(n, layer, count)
                    project(count * P, part == 2 and layer == DEPTH - 1)
                    after_project(n, squares=part == 2)

            with pool.Fori(0, MODS // 4) as i:
                pair_of_modulation(0, 4 * i)
            n.unit = MODS
            ring(0, n.unit)
            ring(1, n.unit + 1)
            for layer, kind in enumerate(MIXERS):
                if kind == "fnet":
                    for j, (hi, lo, size) in enumerate(fnet_tables()):
                        cut((2 + j) % SLOTS, n.unit + 2 + j, hi, lo, size)
                    pair_of_modulation(0, n.unit + 2 + TABLES)
                    n.unit += TABLES + 2
                    project(UNIT)
                    n.unit += KC
                elif kind == "pool":
                    pair_of_modulation(2, n.unit + 2)
                    pair_of_modulation(0, n.unit + 4)
                    n.unit += 4
                    for j in range(2, 6):
                        ring(j % SLOTS, n.unit + j, 512 if j < 4 else UNIT)
                    n.unit += 4
                else:
                    for j in range(2, 14):
                        ring(j % SLOTS, n.unit + j, (LATENT_SIZES + HEAD_SIZES)[j])
                    n.unit += len(LATENT_SIZES)
                    with pool.Fori(0, 2) as i:
                        for j in range(12):
                            ring((j + 2) % SLOTS, n.unit + 12 * i + j + 2, UNIT if j > 9 else HEAD_SIZES[(j + 2) % 6])
                    n.unit += 24
                    ring(2, n.unit + 2)
                    ring(3, n.unit + 3)
                    pair_of_modulation(0, n.unit + 4)
                    ring(0, n.unit + 6)
                    ring(1, n.unit + 7)
                    pair_of_modulation(2, n.unit + 8)
                    for j in range(2, 6):
                        ring(j % SLOTS, n.unit + 8 + j)
                    n.unit += KC + 4
                ffn(layer)

        @block.tensor
        def _(pe):
            n = Counts()

            def product(outs, lhs, rhs, first=True, last=True):
                for z, (lp, rp) in enumerate(((0, 0), (0, 1), (1, 0))):
                    for o, r in zip(outs, rhs[rp]):
                        done = nc.tensor.matmul(o, lhs[lp], r, start=first and z == 0, stop=last and z == 2)
                return done

            def token_halves(hi, lo):
                return [[t[:, 0:HALF], t[:, HALF:W]] for t in (hi, lo)]

            def acc_halves(p, size=HALF):
                return [acc[p][:, b, 0:size] for b in range(2)]

            def weights(slot, k, width=P):
                return [w[slot % 2][:, k * width:(k + 1) * width] for w in (w_hi, w_lo)]

            def modulation_rows(pair, units, parts=(a_hi, a_lo)):
                wait_past(pe, ada_evacuated, pair)
                for u, (slot, use) in enumerate(units):
                    pe.wait_ge(unit_done[slot], use)
                    for k in range(KC):
                        for z in range(2):
                            done = nc.tensor.matmul(sacc[1][0:4, 0, u * P:(u + 1) * P], cond_parts[:, k, :],
                                                    parts[z][u][:, k * P:(k + 1) * P],
                                                    start=k == 0 and z == 0, stop=k == KC - 1 and z == 1)
                done.then_inc(ada_rows, 1)

            def modulation_columns(pair):
                pe.wait_ge(ada_evacuated, pair + 1)
                wait_past(pe, ada_taken, pair)
                for u in range(2):
                    done = nc.tensor.matmul(sacc[1][:, 1, 2 * u:2 * u + 2], ada_row[:, u * P:(u + 1) * P], hi_plus_lo[:],
                                            start=True, stop=True)
                done.then_inc(ada_cols, 1)

            def uses(*units):
                return [(u % SLOTS, u // SLOTS + 1) for u in units]

            def statistics(source):
                for b in range(2):
                    done = nc.tensor.matmul(sacc[0][:, b, 0:HALF], ones[:], source[:, b * HALF:(b + 1) * HALF],
                                            start=True, stop=True)
                done.then_inc(stat_ready, 1)
                n.stat += 1

            def norm():
                pe.wait_ge(summed, n.squared)
                statistics(row(SUM))
                n.chunk += KC

            def project(source, kn, ready=None, ready_from=0, turns=(0, 2)):
                with pe.Fori(*turns) as i:
                    for j in range(4):
                        pe.wait_ge(unit_done[j], n.unit // SLOTS + i + 1)
                        pe.wait_ge(result_taken, n.result + 4 * i + j - 1)
                        for k in range(kn):
                            if j == 0 and ready is not None:
                                pe.wait_ge(ready, ready_from + k + 1)
                            done = product(acc_halves(j % 2), weights(j, k),
                                           token_halves(source[0][:, k, :], source[1][:, k, :]),
                                           k == 0, k == kn - 1)
                        done.then_inc(result_ready, 1)

            def ffn(layer):
                norm()
                for part, (_, count) in enumerate(PARTS):
                    turn = 1 if ada_in_ffn(layer) else 2
                    with pe.Fori(0, count // turn) as i:
                        for j in range(2 * turn):
                            pe.wait_ge(unit_done[j], n.unit // SLOTS + i + 1)
                            pe.wait_ge(result_taken, n.result + 2 * turn * i + j - 1)
                            for k in range(KC):
                                if j == 0:
                                    pe.wait_ge(h_ready, n.chunk - KC + k + 1)
                                done = product(acc_halves(j % 2), weights(j, k),
                                               token_halves(h_hi[:, k, :], h_lo[:, k, :]), k == 0, k == KC - 1)
                            done.then_inc(result_ready, 1)
                            if turn == 1 and j == 0:
                                modulation_rows(n.ada + i, [(2 + u, n.unit // SLOTS + i) for u in range(2)])
                            elif turn == 1:
                                modulation_columns(n.ada + i)
                    after_ffn_in(n, layer, count)
                    project((g_hi, g_lo), count, g_ready, n.pair - count)
                    after_project(n, squares=part == 2)

            def fnet(layer):
                r = n.result
                for g in range(GROUPS):
                    for t in range(5):
                        first = 0 if t == 0 else LAT0 + P * (t - 1)
                        if r >= 2:
                            pe.wait_ge(result_taken, r - 1)
                        if g == 0 and t == 0:
                            pe.wait_ge(unit_done[2], n.unit // SLOTS + 1)
                        for k in range(2):
                            c = 2 * g + k
                            if t == 0:
                                pe.wait_ge(h_ready, n.chunk - KC + c + 1)
                            done = product([acc[r % 2][:, 0, :]],
                                           [hh[:, c, first:first + P] for hh in (h_hi, h_lo)],
                                           [[chan_t[p][:, k, :]] for p in range(2)], k == 0, k == 1)
                        done.then_inc(result_ready, 1)
                        r += 1
                    if g == 0:
                        for slot, use in uses(*range(n.unit + 3, n.unit + 2 + TABLES)):
                            pe.wait_ge(unit_done[slot], use)
                    if layer and g == 1:
                        modulation_rows(n.ada, uses(n.unit + 2 + TABLES, n.unit + 3 + TABLES))
                    if layer and g == 2:
                        modulation_columns(n.ada)
                        n.ada += 1
                    for m in range(2):
                        pe.wait_ge(result_taken, r if m == 0 else r - 1)
                        for c in range(2):
                            col = c * GROUP + m * P
                            product([acc[r % 2][:, 0, 0:CTX]], [f[:, 0, col:col + P] for f in freq],
                                    [[ctx_t[p][:, c, :]] for p in range(2)], c == 0, c == 1)
                        for c in range(2):
                            col = c * GROUP + m * P
                            for t in range(4):
                                done = product([acc[r % 2][:, 1, :]],
                                               [f[:, t + 1, col:col + P] for f in freq],
                                               [[seq_t[c][p][:, t, :]] for p in range(2)],
                                               c == 0 and t == 0, c == 1 and t == 3)
                        done.then_inc(result_ready, 1)
                        r += 1
                n.result = r
                n.unit += TABLES + 2
                pe.wait_ge(result_taken, n.result)
                project((h_hi, h_lo), KC)
                after_project(n)

            def pool_mix():
                for j in range(KC):
                    u = j // 2
                    pe.wait_ge(unit_done[u], n.unit // SLOTS + 1)
                    pe.wait_ge(result_taken, n.result - 1 + j)
                    for k in range(2):
                        c = 2 * u + k
                        pe.wait_ge(h_ready, n.chunk - KC + c + 1)
                        done = product(acc_halves(j % 2), weights(u, 2 * (j % 2) + k),
                                       token_halves(h_hi[:, c, :], h_lo[:, c, :]), k == 0, k == 1)
                    done.then_inc(result_ready, 1)
                after_project(n, 4)

            def rotate(source, out):
                for b in range(2):
                    done = nc.tensor.matmul(out[:, b, 0:HALF], perm[:], source[:, b * HALF:(b + 1) * HALF],
                                            start=True, stop=True)
                done.then_inc(result_ready, 1)

            def unit_product(out, unit, size, rhs, first=True, last=True, k0=0, waits=()):
                pe.wait_ge(unit_done[unit % SLOTS], unit // SLOTS + 1)
                for k in range(size):
                    for s, v in waits:
                        pe.wait_ge(s, v(k))
                    done = product(out, weights(unit, k), rhs(k0 + k), first and k == 0, last and k == size - 1)
                return done

            def latents():
                h_of = lambda k: token_halves(h_hi[:, k, :], h_lo[:, k, :])
                r, u = n.result, n.unit
                for m in range(RC):
                    pe.wait_ge(result_taken, r - 1)
                    wait_h = [(h_ready, lambda k: n.chunk - KC + k + 1)] if m == 0 else []
                    unit_product(acc_halves(r % 2), u, KC, h_of, waits=wait_h).then_inc(result_ready, 1)
                    r, u = r + 1, u + 1
                pe.wait_ge(result_taken, r - 1)
                unit_product(acc_halves(r % 2), u, 4, h_of, last=False)
                unit_product(acc_halves(r % 2), u + 1, 4, h_of, first=False, k0=4).then_inc(result_ready, 1)
                r, u = r + 1, u + 2
                for m in range(QC):
                    pe.wait_ge(result_taken, r - 1)
                    unit_product(acc_halves(r % 2), u, KC, h_of).then_inc(result_ready, 1)
                    r, u = r + 1, u + 1
                    if m == 0:
                        pe.wait_ge(result_taken, r - 1)
                        rotate(kpe_raw, acc[r % 2])
                        r += 1
                    if m == 1:
                        pe.wait_ge(result_taken, n.result + RC)
                        statistics(row(SUM))
                pe.wait_ge(result_taken, r)
                pe.wait_ge(rooted, n.stat)
                statistics(sum_q)
                n.result, n.unit = r, u

            def attention():
                with pe.Fori(0, 2) as i:
                    for h2 in range(2):
                        r = n.result + 64 * i + 32 * h2
                        s = n.score + 20 * i + 10 * h2
                        use = lambda j: n.unit // SLOTS + 3 * i + (6 * h2 + j) // SLOTS + 1
                        slot = lambda j: (6 * h2 + j) % SLOTS
                        ru = [0]

                        def accumulator():
                            p = ru[0] % 2
                            pe.wait_ge(result_taken, r + ru[0] - 1)
                            ru[0] += 1
                            return p

                        def unit(j):
                            pe.wait_ge(unit_done[slot(j)], use(j))

                        if h2 == 0:
                            pe.wait_ge(cached, 2)
                            pe.wait_ge(latent_ready, 1 + RC + QC)
                        unit(0)
                        for t in range(6):
                            p = accumulator()
                            first = [0, LAT0, LAT0 + P, LAT0 + 2 * P, LAT0 + 3 * P, LAT1][t]
                            for k in range(RC):
                                done = product([acc[p][:, 0, 0:2 * VH]],
                                               [c[:, k, first:first + P] for c in (ckv_hi, ckv_lo)],
                                               [[w] for w in weights(slot(0), k, 2 * VH)], k == 0, k == RC - 1)
                            done.then_inc(result_ready, 1)
                        unit(1)
                        p = accumulator()
                        for k in range(QC):
                            done = product(acc_halves(p), weights(slot(1), k),
                                           token_halves(cq_hi[:, k, :], cq_lo[:, k, :]), k == 0, k == QC - 1)
                        done.then_inc(result_ready, 1)
                        p = accumulator()
                        pe.wait_ge(result_taken, r + 7)
                        rotate(q_raw, acc[p])
                        for hh in range(2):
                            unit(2 + 2 * hh)
                            p = accumulator()
                            for k in range(RC):
                                done = product(acc_halves(p, KHALF), weights(slot(2 + 2 * hh), k),
                                               [[c[:, k, 0:KHALF], c[:, k, KHALF:KW]] for c in (ckv_hi, ckv_lo)],
                                               k == 0, k == RC - 1)
                            done.then_inc(result_ready, 1)
                            unit(3 + 2 * hh)
                            p = accumulator()
                            for k in range(QC):
                                done = product(acc_halves(p), weights(slot(3 + 2 * hh), k),
                                               token_halves(cq_hi[:, k, :], cq_lo[:, k, :]), k == 0, k == QC - 1)
                            done.then_inc(result_ready, 1)
                            head_rows = slice(ROPE * hh, ROPE * hh + ROPE)

                            def scores(t):
                                q0, k0, width, banks = Q_TILES[t]
                                b = (5 * hh + t) % 2
                                pe.wait_ge(score_taken, s + 5 * hh + t + 1)
                                keys = lambda src, rows_: [[src_[rows_, k0 + width * z:k0 + width * (z + 1)]
                                                            for z in range(banks)] for src_ in src]
                                out = [sacc[b][:, z, 0:width] for z in range(banks)]
                                product(out, [q[:, q0:q0 + P] for q in (q_hi, q_lo)],
                                        keys((k_hi, k_lo), slice(0, P)), True, False)
                                product(out, [q[head_rows, q0:q0 + P] for q in (qpe_hi, qpe_lo)],
                                        keys((kpe_hi, kpe_lo), head_rows), False, True
                                        ).then_inc(score_ready, 1)

                            def weigh(t):
                                q0, k0, width, banks = Q_TILES[t]
                                tiles = width * banks // P
                                pe.wait_ge(score_taken, s + 5 * hh + t + 3)
                                p = accumulator()
                                for z in range(tiles):
                                    done = nc.tensor.transpose(acc[p][:, z // 4, (z % 4) * P:(z % 4 + 1) * P],
                                                               probs[(5 * hh + t) % 2][:, z * P:(z + 1) * P], ident[:])
                                done.then_inc(result_ready, 1)
                                pe.wait_ge(result_taken, r + ru[0])
                                p = accumulator()
                                for z in range(tiles):
                                    v = z + 1 if t < 4 else 0
                                    done = product([acc[p][:, 0, 0:P]],
                                                   [vv[:, v, hh * VH:(hh + 1) * VH] for vv in (v_hi, v_lo)],
                                                   [[pt[:, z, :]] for pt in (pt_hi, pt_lo)],
                                                   z == 0, z == tiles - 1)
                                done.then_inc(result_ready, 1)

                            pe.wait_ge(result_taken, r + ru[0])
                            pe.wait_ge(rope_step, 3 + (2 * i + h2 + 1) * 3)
                            scores(0)
                            for t in range(1, 5):
                                scores(t)
                                weigh(t - 1)
                            weigh(4)
                n.result += 128
                n.score += 40
                n.unit += 24

            pe.wait_ge(first_loaded, FIRST_LOADS)
            pe.wait_ge(cond_parts_ready, 1)

            def two_pairs(i):
                for j in range(2):
                    modulation_rows(2 * i + j, [(2 * j + u, i + 1) for u in range(2)], ((a_hi, a_lo), (w_hi, w_lo))[j])
                    modulation_columns(2 * i + j)

            two_pairs(0)
            with pe.Fori(1, MODS // 4) as i:
                two_pairs(i)
            n.unit, n.ada, n.squared = MODS, MODS // 2, KC
            pe.wait_ge(loaded, SMALL_LOADS)
            pe.wait_ge(setup_done, 1)
            for layer, kind in enumerate(MIXERS):
                if layer:
                    modulation_rows(n.ada, [(2 + u, n.unit // SLOTS) for u in range(2)])
                norm()
                if layer:
                    modulation_columns(n.ada)
                    n.ada += 1
                if kind == "fnet":
                    fnet(layer)
                elif kind == "pool":
                    modulation_rows(n.ada, uses(n.unit + 2, n.unit + 3))
                    modulation_columns(n.ada)
                    n.ada += 1
                    n.unit += 4
                    pool_mix()
                else:
                    latents()
                    attention()
                    pe.wait_ge(result_taken, n.result)
                    project((h_hi, h_lo), KC, turns=(0, 1))
                    modulation_rows(n.ada, uses(n.unit + 4, n.unit + 5))
                    n.unit += 4
                    project((h_hi, h_lo), KC, turns=(1, 2))
                    modulation_columns(n.ada)
                    n.ada += 1
                    after_project(n)
                ffn(layer)
            pe.wait_ge(summed, n.squared)
            statistics(row(SUM))

        @block.scalar
        def _(act):
            n = Counts()

            def round_unit(slot, use, hi, size, free=None):
                act.wait_ge(raw_ready[slot], 16 * use)
                if free is not None:
                    act.wait_ge(result_ready, free)
                nc.scalar.activation(hi, raw[slot][:, 0:size], ACT.Copy).then_inc(weights_hi, 1)

            def round_ring(slot, use, free=None, size=UNIT):
                round_unit(slot, use, w_hi[slot % 2][:, 0:size], size, free)

            def take(r, pieces):
                act.wait_ge(result_ready, r + 1)
                for dst, src in pieces:
                    done = nc.scalar.activation(dst, src, ACT.Copy)
                done.then_inc(result_rounded, 1)

            def cut_modulation(pair, units):
                act.wait_ge(ada_rows, pair)
                for u, (slot, use) in enumerate(units):
                    round_unit(slot, use, a_hi[u][:], UNIT)

            def uses(*units):
                return [(u % SLOTS, u // SLOTS + 1) for u in units]

            def evacuate(pair):
                act.wait_ge(ada_rows, pair + 1)
                wait_past(act, ada_cols, pair)
                nc.scalar.activation(ada_row[:], sacc[1][0:4, 0, 0:2 * P], ACT.Copy).then_inc(ada_evacuated, 1)

            def root(width, to=row(RSTD)):
                act.wait_ge(stat_ready, n.stat + 1)
                nc.scalar.activation(two(to), halves(sacc[0]), ACT.Sqrt, bias=eps[:], scale=1.0 / width
                                     ).then_inc(rooted, 1)
                n.stat += 1

            def norm(layer, shift, scale, target=None, after_chunk=None):
                root(D)
                if layer and scale == SC1:
                    evacuate(n.ada)
                    n.ada += 1
                for c in range(KC):
                    act.wait_ge(xn_ready, n.chunk + c + 1)
                    if target is None and c >= 2:
                        act.wait_ge(h_ready, n.chunk + c - 1)
                    xn = row(XN + c % 2)
                    out = row(HF + c % 2) if target is None else padded[c % 2]
                    if target is not None and c >= 2:
                        act.wait_ge(h_ready, n.chunk + c - 1)
                    places = (CXS, LTS) if target is None else (slice(PC, PC + CTX), slice(PL, PL + LAT))
                    for z, (cols, to) in enumerate(zip((CXS, LTS), places)):
                        done = nc.scalar.activation(out[:, to], xn[:, cols], ACT.Identity,
                                                    bias=mod[:, layer % 2, shift + c, z:z + 1],
                                                    scale=mod[:, layer % 2, scale + c, z:z + 1])
                    done.then_inc(h_full, 1)
                    if target is None:
                        act.wait_ge(h_full, n.chunk + c + 1)
                        nc.scalar.activation(h_hi[:, c, :], out, ACT.Copy).then_inc(h_rounded, 1)
                    else:
                        target(c)
                    if after_chunk is not None:
                        after_chunk(c)
                n.chunk += KC

            def square(source):
                nc.scalar.activation(row(SQ), source, ACT.Square).then_inc(squared, 1)

            def project_steps(i, squares, rounds=4, between=None):
                for j in range(4):
                    if j == 2 and between is not None:
                        between()
                    if j < rounds:
                        round_ring((j + 2) % SLOTS, n.unit // SLOTS + i + (j + 2) // SLOTS + 1, n.result + 4 * i + j + 1)
                    if squares:
                        act.wait_ge(result_taken, n.result + 4 * i + j + 1)
                        square(x[:, ds(4 * i + j, 1), :].rearrange("p o t -> p (o t)"))

            def project(squares=True, last=False):
                with act.Fori(0, 1 if last else 2) as i:
                    project_steps(i, squares)
                if last:
                    project_steps(1, squares, 2)

            def ffn(layer):
                norm(layer, SH2, SC2)
                nc.scalar.preload_act_table(ACT.Silu)
                act.wait_ge(layer_loaded, layer_loads(layer))
                for part, (_, count) in enumerate(PARTS):
                    turn = 1 if ada_in_ffn(layer) else 2
                    with act.Fori(0, count // turn) as i:
                        for z in range(turn):
                            gate = turn * i + z
                            r = n.result + 2 * gate

                            def ahead_ring(k, free):
                                j = k + (2 * z if turn == 2 else 2)
                                round_ring(j % SLOTS, n.unit // SLOTS + i + j // SLOTS + 1, free)

                            taps = lambda half: (
                                conv_w[:, ds(n.pair - layer * PAIRS + gate + half * PAIRS, 1), 1:2].rearrange("p o t -> p (o t)"),
                                conv_w[:, ds(n.pair - layer * PAIRS + gate + half * PAIRS, 1), 3:4].rearrange("p o t -> p (o t)"))
                            ahead_ring(2, r + 1)
                            w1, b1 = taps(0)
                            nc.scalar.activation(two(conv[0][:, 1:W + 1]), halves(acc[0]), ACT.Identity,
                                                 bias=b1, scale=w1).then_inc(centered, 1)
                            act.wait_ge(result_taken, r + 1)
                            nc.scalar.activation(gated[:], conv[0][:, 1:W + 1], ACT.Silu).then_inc(silu_done, 1)
                            if turn == 1:
                                evacuate(n.ada + i)
                                cut_modulation(n.ada + i + 1, [(2 + u, n.unit // SLOTS + i + 1) for u in range(2)])
                            ahead_ring(3, r + 2)
                            w1, b1 = taps(1)
                            nc.scalar.activation(two(conv[1][:, 1:W + 1]), halves(acc[1]), ACT.Identity,
                                                 bias=b1, scale=w1).then_inc(centered, 1)
                            act.wait_ge(gated_done, n.pair + gate + 1)
                            nc.scalar.activation(g_hi[:, ds(gate, 1), :].rearrange("p o t -> p (o t)"), gated[:],
                                                 ACT.Copy).then_inc(g_rounded, 1)
                    after_ffn_in(n, layer, count)
                    last = part == 2
                    if last:
                        nc.scalar.preload_act_table(ACT.Sqrt)
                    project(last, last and layer == DEPTH - 1)
                    after_project(n, squares=last)

            def fnet(layer):
                tables = fnet_tables()

                def table(j):
                    hi, _, size = tables[j]
                    u = n.unit + 2 + j
                    round_unit(u % SLOTS, u // SLOTS + 1, hi, size)

                if layer:
                    act.wait_ge(result_ready, n.result)
                table(0)
                table(1)

                def after_chunk(c):
                    if 2 <= c < TABLES:
                        table(c)
                    if c == TABLES:
                        cut_modulation(n.ada, uses(n.unit + 2 + TABLES, n.unit + 3 + TABLES))

                norm(layer, SH1, SC1, after_chunk=after_chunk)
                r = n.result
                for g in range(GROUPS):
                    for t in range(5):
                        take(r, [(freq[0][:, t, :], acc[r % 2][:, 0, :])])
                        r += 1
                    for m in range(2):
                        c = 2 * g + m
                        take(r, [(h_hi[:, c, CXS], acc[r % 2][:, 0, 0:CTX]), (h_hi[:, c, LTS], acc[r % 2][:, 1, :])])
                        r += 1
                    if layer and g == 1:
                        evacuate(n.ada)
                        n.ada += 1
                n.result = r
                n.unit += TABLES + 2
                project()
                after_project(n)

            def pool_mix(layer):
                def pooled_hi(c):
                    if c >= 1:
                        round_pooled(c - 1)

                def round_pooled(c):
                    act.wait_ge(pooled_full, c + 1)
                    for to, cols in ((CXS, slice(PC, PC + CTX)), (LTS, slice(PL, PL + LAT))):
                        done = nc.scalar.activation(h_hi[:, c, to], window[c % 2][:, cols], ACT.Copy)
                    done.then_inc(h_rounded, 1)

                def after_chunk(c):
                    if c == 0:
                        cut_modulation(n.ada, uses(n.unit + 2, n.unit + 3))
                    if c == 3:
                        evacuate(n.ada)
                        n.ada += 1
                        cut_modulation(n.ada, uses(n.unit + 4, n.unit + 5))

                norm(layer, SH1, SC1, target=pooled_hi, after_chunk=after_chunk)
                n.unit += 4
                round_pooled(KC - 1)
                for j in range(KC):
                    if j % 2 == 1:
                        u = j // 2 + 2
                        round_ring(u % SLOTS, n.unit // SLOTS + u // SLOTS + 1, n.result + j + 1,
                                   2 * GROUP if u < 4 else UNIT)
                    act.wait_ge(result_taken, n.result + j + 1)
                    square(x[:, j, :])
                after_project(n, 4)

            def mla(layer):
                act.wait_ge(table_loaded, TABLES_MLA)
                nc.scalar.activation(ckv_hi[:, :, LAT1:KEYS], cache[:, 0:RC, :], ACT.Copy)
                nc.scalar.activation(kpe_hi[:, LAT1:KEYS], cache[:, RC, :], ACT.Copy).then_inc(cache_rounded, 1)
                norm(layer, SH1, SC1)
                act.wait_ge(h_ready, n.chunk)
                act.dma_start(rows[:, 5:7, :], a["rope"]).then_inc(table_loaded, 16)
                r0, u0 = n.result, n.unit
                ring = lambda j, free: round_ring((u0 + j) % SLOTS, (u0 + j) // SLOTS + 1, free,
                                                  (LATENT_SIZES + HEAD_SIZES)[j])

                def latent(r, raw_, previous):
                    act.wait_ge(result_ready, r + 1)
                    if previous is not None:
                        act.wait_ge(result_taken, previous + 1)
                    nc.scalar.activation(two(raw_), halves(acc[r % 2]), ACT.Copy)
                    nc.scalar.activation(two(row(SQ)), halves(acc[r % 2]), ACT.Square).then_inc(latent_squared, 1)

                for m in range(RC):
                    ring(m + 2, r0 + m + 1)
                    latent(r0 + m, ckv_raw[:, m, :], r0 + m - 1 if m else None)
                ring(6, r0 + 5)
                ring(7, r0 + 5)
                ring(8, r0 + 6)
                latent(r0 + 5, cq_raw[:, 0, :], r0 + 3)
                act.wait_ge(rope_step, 3)
                nc.scalar.activation(kpe_hi[:, 0:LAT1], kpe_sin[:, 0:LAT1], ACT.Copy
                                     ).then_inc(latent_rounded, 1)
                ring(9, r0 + 8)
                latent(r0 + 7, cq_raw[:, 1, :], r0 + 5)
                root(KV_RANK)
                for m in range(RC):
                    act.wait_ge(latent_normed, m + 1)
                    nc.scalar.activation(ckv_hi[:, m, 0:LAT1], ckv_raw[:, m, 0:LAT1], ACT.Copy
                                         ).then_inc(latent_rounded, 1)
                act.dma_start(a["state_ckv"], ckv_raw[:, :, CXS]).then_inc(stored, 16)
                act.dma_start(a["state_kpe"], kpe_raw[0:ROPE, CXS]).then_inc(stored, 16)
                for m in range(2, QC):
                    ring(m + 8, r0 + m + 7)
                    latent(r0 + m + 6, cq_raw[:, m, :], r0 + m + 5)
                root(Q_RANK, rstd_q)
                act.wait_ge(cached, 2)
                for m in range(QC):
                    act.wait_ge(latent_normed, RC + m + 1)
                    nc.scalar.activation(cq_hi[:, m, :], cq_raw[:, m, :], ACT.Copy).then_inc(latent_rounded, 1)
                act.wait_ge(stored, 32)
                act.wait_ge(latent_ready, 1 + RC + QC)
                n.result += 12
                n.unit += 12
                nc.scalar.preload_act_table(ACT.Exp)
                with act.Fori(0, 2) as i:
                    for h2 in range(2):
                        attend(i, h2)
                n.result += 128
                n.unit += 24
                n.score += 40

                def cut_last_pair():
                    cut_modulation(n.ada, uses(n.unit + 4, n.unit + 5))
                    n.unit += 4

                project_steps(0, True, between=cut_last_pair)
                evacuate(n.ada)
                n.ada += 1
                cut_modulation(n.ada, uses(n.unit + 2, n.unit + 3))
                project_steps(1, True)
                after_project(n)

            def attend(i, h2):
                r = n.result + 64 * i + 32 * h2
                s = n.score + 20 * i + 10 * h2

                def ring(j, free):
                    at_ = 6 * h2 + j
                    round_ring(at_ % SLOTS, n.unit // SLOTS + 3 * i + at_ // SLOTS + 1, free,
                               HEAD_SIZES[j] if j < 6 else UNIT)

                for t in range(6):
                    take(r + t, [(v_hi[:, t, :], acc[t % 2][:, 0, 0:2 * VH])])
                ring(2, r + 6)
                ring(3, r + 7)
                act.wait_ge(rope_step, 5 + (2 * i + h2) * 3)
                nc.scalar.activation(qpe_hi[:], q_rot, ACT.Copy).then_inc(result_rounded, 1)
                for hh in range(2):
                    base = r + 8 + 12 * hh
                    ring(4 + 2 * hh, base + 1)
                    nc.scalar.activation(k_hi[:].rearrange("p (a b) -> p a b", a=2), acc[0][:, :, 0:KHALF],
                                         ACT.Copy).then_inc(result_rounded, 1)
                    ring(5 + 2 * hh, base + 2)
                    nc.scalar.activation(two(q_hi[:]), halves(acc[1]), ACT.Copy).then_inc(result_rounded, 1)

                    def exponentials(t):
                        q0, k0, width, banks = Q_TILES[t]
                        b = (5 * hh + t) % 2
                        act.wait_ge(bias_done, s + 5 * hh + t + 1)
                        nc.scalar.activation(
                            probs[b][:, 0:width * banks].rearrange("p (a b) -> p a b", a=banks),
                            sacc[b][:, 0:banks, 0:width], ACT.Exp, bias=negtop[:, b:b + 1], scale=SM_SCALE,
                            accum_out=total[:, b:b + 1]).then_inc(exp_done, 1)

                    def weigh(t):
                        q0, k0, width, banks = Q_TILES[t]
                        rt = base + 2 + 2 * t
                        tiles = width * banks // P
                        take(rt, transposed_pieces(pt_hi, acc[0], tiles))
                        take(rt + 1, [(head_out(h_hi, i, h2, hh, q0), acc[1][:, 0, 0:P])])

                    exponentials(0)
                    for t in range(1, 5):
                        exponentials(t)
                        weigh(t - 1)
                    weigh(4)

            def load_layer(layer):
                if layer:
                    act.wait_ge(result_taken, n.result)
                act.dma_start(conv_w[:], a["conv_w"][layer]).then_inc(layer_loaded, 16)
                if layer + 1 < DEPTH:
                    act.dma_start(b_ada[:, (layer + 1) % 2, :, :], a["b_ada"][layer + 1]).then_inc(layer_loaded, 16)

            act.dma_start(cond[:], a["cond"]).then_inc(first_loaded, 16)
            act.dma_start(b_ada[:, 0, :, :], a["b_ada"][0]).then_inc(first_loaded, 16)
            act.dma_start(ident[:], a["ident"]).then_inc(first_loaded, 16)
            for c in range(KC):
                act.dma_start(x[:, c, :], a["x"][c]).then_inc(loaded, 16)
            for dst, name in ((ones, "ones"), (perm, "perm"), (gains, "gains")):
                act.dma_start(dst[:], a[name]).then_inc(loaded, 16)
            act.wait_ge(first_loaded, FIRST_LOADS)
            nc.scalar.activation(cond[:], cond[:], ACT.Silu).then_inc(cond_ready, 1)
            act.wait_ge(cond_ready, 1)
            nc.scalar.activation(cond_parts[:, :, 0:2], cond[:], ACT.Copy).then_inc(cond_rounded, 1)
            for u in range(2):
                round_unit(u, 1, a_hi[u][:], UNIT)
            def two_pairs(i, more):
                wait_past(act, ada_rows, 2 * i)
                for u in range(2):
                    round_unit(2 + u, i + 1, w_hi[u][:], UNIT)
                evacuate(2 * i)
                if more:
                    for u in range(2):
                        round_unit(u, i + 2, a_hi[u][:], UNIT)
                evacuate(2 * i + 1)

            two_pairs(0, True)
            with act.Fori(1, MODS // 4 - 1) as i:
                two_pairs(i, True)
            two_pairs(MODS // 4 - 1, False)
            act.wait_ge(setup_done, 1)
            act.wait_ge(loaded, SMALL_LOADS)
            n.unit, n.ada, n.squared = MODS, MODS // 2, KC
            for c in range(KC):
                if c:
                    act.wait_ge(summed, c)
                square(x[:, c, :])
            load_layer(0)
            round_ring(0, n.unit // SLOTS + 1)
            round_ring(1, n.unit // SLOTS + 1)
            for layer, kind in enumerate(MIXERS):
                if layer:
                    load_layer(layer)
                    if kind == "pool":
                        act.dma_start(inv_count[:], a["inv_count"]).then_inc(table_loaded, 16)
                    if kind == "mla":
                        act.wait_ge(result_ready, n.result)
                        act.dma_start(cache[:], a["cache"]).then_inc(table_loaded, 16)
                act.wait_ge(mod_ready, layer + 1)
                {"fnet": fnet, "pool": pool_mix, "mla": mla}[kind](layer)
                ffn(layer)
            root(D)
            for c in range(KC):
                act.wait_ge(y_ready, c + 1)
                act.dma_start(a["y"][c], y[:, c, :]).then_inc(stored, 16)
            act.wait_ge(stored, 32 + 16 * KC)

        @block.vector
        def _(dve):
            n = Counts()

            def recip(width_row):
                dve.wait_ge(rooted, n.stat + 1)
                nc.vector.reciprocal(width_row, width_row).then_inc(rstd_done, 1)
                n.stat += 1
                dve.wait_ge(rstd_done, n.stat)

            def clear_sum():
                nc.vector.memset(row(SUM), 0.0).then_inc(sum_cleared, 1)
                n.cleared += 1

            def scale_x(c):
                nc.vector.tensor_tensor(row(XN + c % 2), x[:, c, :], row(RSTD), ALU.mult).then_inc(xn_ready, 1)

            def lo_part(ready, hi, lo, full, inc, rounded=h_rounded):
                dve.wait_ge(rounded, ready)
                nc.vector.tensor_tensor(lo, full, hi.bitcast(f32), ALU.subtract).then_inc(inc, 1)

            def norm(mixer_of=0):
                recip(row(RSTD))
                clear_sum()
                scale_x(0)
                scale_x(1)
                if mixer_of:
                    take_late_modulation(mixer_of)
                for c in range(KC):
                    lo_part(n.chunk + c + 1, h_hi[:, c, :], h_lo[:, c, :], row(HF + c % 2), h_ready)
                    if c + 2 < KC:
                        scale_x(c + 2)
                n.chunk += KC

            def take(r, rounded, pieces):
                dve.wait_ge(result_rounded, rounded)
                for lo, hi, src in pieces:
                    done = nc.vector.tensor_tensor(lo, src, hi.bitcast(f32), ALU.subtract)
                done.then_inc(result_taken, 1)

            def project(gate, squares=True):
                if squares:
                    dve.wait_ge(sum_cleared, n.cleared)
                with dve.Fori(0, 2) as i:
                    for j in range(4):
                        update_x(4 * i + j, 4 * i + j, gate(4 * i + j), j % 2, squares)

            def update_x(c, j, gate, pair, squares):
                dve.wait_ge(result_ready, n.result + j + 1)
                for cond_, x0, x1, bank, p0 in ((0, 0, CTX, 0, 0), (1, LAT0, HALF, 0, LAT0), (1, HALF, LAT1, 1, 0)):
                    xs = x[:, ds(c, 1), x0:x1].rearrange("p o t -> p (o t)")
                    done = nc.vector.scalar_tensor_tensor(xs, acc[pair][:, bank, p0:p0 + x1 - x0], gate(cond_), xs,
                                                          ALU.mult, ALU.add)
                done.then_inc(result_taken, 1)
                if squares:
                    dve.wait_ge(summed, n.squared + j)
                    add_square(row(SUM), n.squared + j, summed)

            def add_square(total_, index, inc, ready=squared):
                dve.wait_ge(ready, index + 1)
                nc.vector.tensor_tensor(total_, total_, row(SQ), ALU.add).then_inc(inc, 1)

            def mod_gate(layer, which):
                return lambda c: lambda z: mod[:, layer % 2, ds(which + c, 1), z:z + 1].rearrange("p o t -> p (o t)")

            def take_modulation(layer, pair, count):
                columns = sacc[1][:, 1, 0:4].rearrange("p (u c) -> p u c", u=2)
                chunks = ds(2 * pair, 2)
                dve.wait_ge(ada_cols, count + 1)
                nc.vector.tensor_tensor(mod[:, layer % 2, chunks, :], columns, b_ada[:, layer % 2, chunks, :], ALU.add
                                        ).then_inc(ada_taken, 1)

            def take_late_modulation(layer):
                take_modulation(layer, n.ada - layer * (MODS // 2), n.ada)
                n.ada += 1

            def ffn(layer):
                norm()
                for t in conv:
                    nc.vector.memset(t[:, 0:1], 0.0)
                    nc.vector.memset(t[:, W + 1:W + 2], 0.0).then_inc(conv_padded, 1)
                dve.wait_ge(conv_padded, 2 * layer + 2)
                dve.wait_ge(layer_loaded, layer_loads(layer))
                for part, (_, count) in enumerate(PARTS):
                    turn = 1 if ada_in_ffn(layer) else 2
                    with dve.Fori(0, count // turn) as i:
                        for z in range(turn):
                            pair = n.pair + turn * i + z
                            for half in range(2):
                                k = 2 * pair + half
                                tap = lambda t: conv_w[:, ds(pair - layer * PAIRS + half * PAIRS, 1),
                                                       t:t + 1].rearrange("p o t -> p (o t)")
                                dve.wait_ge(centered, k + 1)
                                to = two(conv[half][:, 2:W + 2])
                                nc.vector.scalar_tensor_tensor(to, halves(acc[half]), tap(0), to, ALU.mult, ALU.add
                                                               ).then_inc(left_done, 1)
                                dve.wait_ge(left_done, k + 1)
                                to = two(conv[half][:, 0:W])
                                nc.vector.scalar_tensor_tensor(to, halves(acc[half]), tap(2), to, ALU.mult, ALU.add
                                                               ).then_inc(result_taken, 1)
                            dve.wait_ge(silu_done, pair + 1)
                            dve.wait_ge(result_taken, n.result + 2 * (turn * i + z) + 2)
                            nc.vector.tensor_tensor(gated[:], gated[:], conv[1][:, 1:W + 1], ALU.mult
                                                    ).then_inc(gated_done, 1)
                            dve.wait_ge(g_rounded, pair + 1)
                            gc = ds(turn * i + z, 1)
                            nc.vector.tensor_tensor(
                                g_lo[:, gc, :].rearrange("p o t -> p (o t)"), gated[:],
                                g_hi[:, gc, :].rearrange("p o t -> p (o t)").bitcast(f32), ALU.subtract
                            ).then_inc(g_ready, 1)
                        if turn == 1:
                            take_modulation(layer + 1, n.ada - (MODS // 2) * (layer + 1) + i, n.ada + i)
                    after_ffn_in(n, layer, count)
                    project(mod_gate(layer, G2), part == 2)
                    after_project(n, squares=part == 2)

            def fnet(layer):
                norm(layer)
                r = n.result
                for g in range(GROUPS):
                    if layer and g == 3:
                        take_late_modulation(layer)
                    for t in range(5):
                        n.rounded += 1
                        take(r, n.rounded, [(freq[1][:, t, :], freq[0][:, t, :], acc[r % 2][:, 0, :])])
                        r += 1
                    for m in range(2):
                        c = 2 * g + m
                        n.rounded += 1
                        take(r, n.rounded, [(h_lo[:, c, CXS], h_hi[:, c, CXS], acc[r % 2][:, 0, 0:CTX]),
                                            (h_lo[:, c, LTS], h_hi[:, c, LTS], acc[r % 2][:, 1, :])])
                        r += 1
                n.result = r
                project(mod_gate(layer, G1))
                after_project(n)

            def pool_mix(layer):
                steps = [0]

                def step(ins):
                    steps[0] += 1
                    ins.then_inc(pool_step, 1)
                    dve.wait_ge(pool_step, steps[0])

                for t in padded:
                    for lo, hi in ((0, PC), (PC + CTX, PL), (PL + LAT, PADW)):
                        last = nc.vector.memset(t[:, lo:hi], 0.0)
                step(last)
                for z in range(2):
                    last = nc.vector.tensor_tensor(gate_pool[:, :, z], mod[:, layer % 2, G1:G1 + KC, z],
                                                   pool_scale, ALU.mult)
                step(last)
                dve.wait_ge(table_loaded, TABLES_POOL)
                recip(row(RSTD))
                clear_sum()
                scale_x(0)
                scale_x(1)
                take_late_modulation(layer)
                for c in range(KC):
                    if c == 6:
                        take_late_modulation(layer)
                    dve.wait_ge(h_full, n.chunk + c + 1)
                    if c + 2 < KC:
                        scale_x(c + 2)
                    source, lo, hi = padded[c % 2], 0, PADW
                    levels = c // 2 + 1
                    a_, b_ = window[c % 2], scratch
                    outs = [a_ if (levels - l) % 2 == 0 else b_ for l in range(levels)]
                    for level in range(levels):
                        back = 1 if level == 0 else 2 ** (level - 1)
                        ahead = 0 if level == 0 else back
                        lo, hi = lo + back, hi - ahead
                        out = outs[level]
                        step(nc.vector.tensor_tensor(out[:, lo:hi], source[:, lo - back:hi - back],
                                                     source[:, lo + ahead:hi + ahead], ALU.add))
                        source = out
                    out = window[c % 2]
                    step(nc.vector.tensor_tensor(out[:, PC:PL + LAT], source[:, PC:PL + LAT],
                                                 inv_count[:, c // 2, PC:PL + LAT], ALU.mult))
                    nc.vector.tensor_tensor(out[:, PC:PL + LAT], out[:, PC:PL + LAT], padded[c % 2][:, PC:PL + LAT],
                                            ALU.subtract).then_inc(pooled_full, 1)
                    dve.wait_ge(pooled_full, c + 1)
                    if c >= 1:
                        pooled_lo(c - 1)
                pooled_lo(KC - 1)
                n.chunk += KC
                for c in range(KC):
                    update_x(c, c, lambda z: gate_pool[:, c, z:z + 1], c % 2, True)
                after_project(n, 4)

            def pooled_lo(c):
                dve.wait_ge(h_rounded, n.chunk + c + 1)
                for to, cols in ((CXS, slice(PC, PC + CTX)), (LTS, slice(PL, PL + LAT))):
                    done = nc.vector.tensor_tensor(h_lo[:, c, to], window[c % 2][:, cols],
                                                   h_hi[:, c, to].bitcast(f32), ALU.subtract)
                done.then_inc(h_ready, 1)

            def mla(layer):
                for t in (ckv_hi, ckv_lo):
                    nc.vector.memset(t[:, :, KEYS:KW].bitcast(f32), 0.0)
                nc.vector.memset(kpe_lo[:, KEYS:KW].bitcast(f32), 0.0).then_inc(cached, 1)
                dve.wait_ge(cache_rounded, 1)
                nc.vector.tensor_tensor(kpe_lo[:, LAT1:KEYS], cache[:, RC, :], kpe_hi[:, LAT1:KEYS].bitcast(f32),
                                        ALU.subtract)
                nc.vector.tensor_tensor(ckv_lo[:, :, LAT1:KEYS], cache[:, 0:RC, :],
                                        ckv_hi[:, :, LAT1:KEYS].bitcast(f32), ALU.subtract).then_inc(cached, 1)
                norm(layer)
                r0 = n.result
                dve.wait_ge(sum_cleared, n.cleared)
                for m in range(RC):
                    if m:
                        dve.wait_ge(result_taken, r0 + m)
                    add_square(row(SUM), m, result_taken, latent_squared)
                dve.wait_ge(result_ready, r0 + 5)
                nc.vector.tensor_copy(two(kpe_raw[:]), halves(acc[(r0 + 4) % 2])).then_inc(result_taken, 1)
                dve.wait_ge(result_taken, r0 + 5)
                dve.wait_ge(table_loaded, TABLES_ROPE)
                nc.vector.tensor_tensor(kpe_cos[:], kpe_raw[:], tab_cos, ALU.mult).then_inc(rope_step, 1)
                nc.vector.memset(sum_q, 0.0).then_inc(rope_step, 1)
                dve.wait_ge(rope_step, 2)
                add_square(sum_q, RC, result_taken, latent_squared)
                dve.wait_ge(result_ready, r0 + 7)
                nc.vector.tensor_tensor(two(kpe_sin[:]), halves(acc[(r0 + 6) % 2]), two(tab_sin), ALU.mult
                                        ).then_inc(result_taken, 1)
                dve.wait_ge(result_taken, r0 + 7)
                nc.vector.tensor_tensor(kpe_sin[:], kpe_sin[:], kpe_cos[:], ALU.add).then_inc(rope_step, 1)
                dve.wait_ge(rope_step, 3)
                lo_part(1, kpe_hi[:, 0:LAT1], kpe_lo[:, 0:LAT1], kpe_sin[:, 0:LAT1], latent_ready, latent_rounded)
                add_square(sum_q, RC + 1, result_taken, latent_squared)
                recip(row(RSTD))

                def normed(raw_, gain, rstd, width=W):
                    nc.vector.scalar_tensor_tensor(raw_, raw_, gain, rstd, ALU.mult, ALU.mult
                                                   ).then_inc(latent_normed, 1)

                for m in range(RC):
                    normed(ckv_raw[:, m, :], g_kv[:, m:m + 1], row(RSTD))
                dve.wait_ge(latent_normed, RC)
                for m in range(RC):
                    lo_part(2 + m, ckv_hi[:, m, 0:LAT1], ckv_lo[:, m, 0:LAT1], ckv_raw[:, m, 0:LAT1],
                            latent_ready, latent_rounded)
                for m in range(2, QC):
                    dve.wait_ge(result_taken, r0 + 6 + m)
                    add_square(sum_q, RC + m, result_taken, latent_squared)
                recip(rstd_q)
                for m in range(QC):
                    normed(cq_raw[:, m, :], g_q[:, m:m + 1], rstd_q)
                dve.wait_ge(latent_normed, RC + QC)
                for m in range(QC):
                    lo_part(RC + 2 + m, cq_hi[:, m, :], cq_lo[:, m, :], cq_raw[:, m, :], latent_ready, latent_rounded)
                n.result += 12
                n.unit += 12
                for t in (top, total):
                    nc.vector.memset(t[:], 0.0).then_inc(score_taken, 1)
                with dve.Fori(0, 2) as i:
                    for h2 in range(2):
                        attend(i, h2)
                n.result += 128
                n.rounded += 4 * 31
                n.unit += 24
                n.score += 40
                clear_sum()
                dve.wait_ge(sum_cleared, n.cleared)
                project(mod_gate(layer, G1))
                take_late_modulation(layer)
                after_project(n)

            def attend(i, h2):
                r = n.result + 64 * i + 32 * h2
                s = n.score + 20 * i + 10 * h2
                rounded = n.rounded + 62 * i + 31 * h2
                ropes = 3 + (2 * i + h2) * 3
                for t in range(6):
                    take(r + t, rounded + t + 1, [(v_lo[:, t, :], v_hi[:, t, :], acc[t % 2][:, 0, 0:2 * VH])])
                dve.wait_ge(result_ready, r + 7)
                nc.vector.tensor_copy(two(q_raw), halves(acc[0])).then_inc(result_taken, 1)
                dve.wait_ge(result_ready, r + 8)
                nc.vector.tensor_tensor(two(q_rot), halves(acc[1]), two(tab_sin), ALU.mult).then_inc(result_taken, 1)
                nc.vector.tensor_tensor(q_raw, q_raw, tab_cos, ALU.mult).then_inc(rope_step, 1)
                dve.wait_ge(result_taken, r + 8)
                dve.wait_ge(rope_step, ropes + 1)
                nc.vector.tensor_tensor(q_rot, q_rot, q_raw, ALU.add).then_inc(rope_step, 1)
                dve.wait_ge(result_rounded, rounded + 7)
                nc.vector.tensor_tensor(qpe_lo[:], q_rot, qpe_hi[:].bitcast(f32), ALU.subtract).then_inc(rope_step, 1)
                for hh in range(2):
                    base = r + 8 + 12 * hh
                    rb = rounded + 7 + 12 * hh
                    take(base, rb + 1, [(k_lo[:].rearrange("p (a b) -> p a b", a=2),
                                         k_hi[:].rearrange("p (a b) -> p a b", a=2), acc[0][:, :, 0:KHALF])])
                    take(base + 1, rb + 2, [(two(q_lo[:]), two(q_hi[:]), halves(acc[1]))])

                    def softmax(t):
                        q0, k0, width, banks = Q_TILES[t]
                        b = (5 * hh + t) % 2
                        k = s + 5 * hh + t + 1
                        dve.wait_ge(score_ready, k)
                        nc.vector.tensor_reduce(top[:, b:b + 1], sacc[b][:, 0:banks, 0:width], AX.XY, ALU.max
                                                ).then_inc(top_done, 1)
                        dve.wait_ge(top_done, k)
                        nc.vector.tensor_scalar(negtop[:, b:b + 1], top[:, b:b + 1], -SM_SCALE, None, ALU.mult
                                                ).then_inc(bias_done, 1)
                        dve.wait_ge(exp_done, k)
                        nc.vector.reciprocal(inverse[:, b:b + 1], total[:, b:b + 1]).then_inc(inverse_done, 1)
                        dve.wait_ge(inverse_done, k)
                        pr = probs[b][:, 0:width * banks]
                        nc.vector.tensor_scalar(pr, pr, inverse[:, b:b + 1], None, ALU.mult).then_inc(score_taken, 1)

                    def weigh(t):
                        q0, k0, width, banks = Q_TILES[t]
                        tiles = width * banks // P
                        take(None, rb + 3 + 2 * t, [(lo, hi, src) for (lo, src), (hi, _) in zip(
                            transposed_pieces(pt_lo, acc[0], tiles), transposed_pieces(pt_hi, acc[0], tiles))])
                        take(None, rb + 4 + 2 * t, [(head_out(h_lo, i, h2, hh, q0), head_out(h_hi, i, h2, hh, q0),
                                                     acc[1][:, 0, 0:P])])

                    softmax(0)
                    for t in range(1, 5):
                        softmax(t)
                        weigh(t - 1)
                    weigh(4)

            nc.vector.memset(rows[:], 0.0)
            nc.vector.memset(eps[:], EPS).then_inc(setup_done, 1)
            dve.wait_ge(first_loaded, FIRST_LOADS)
            dve.wait_ge(setup_done, 1)
            dve.wait_ge(cond_rounded, 1)
            nc.vector.tensor_tensor(hi_plus_lo[:], ident[0:4, 0:2], ident[0:4, 2:4], ALU.add)
            nc.vector.tensor_tensor(cond_parts[:, :, 2:4], cond[:], cond_parts[:, :, 0:2].bitcast(f32), ALU.subtract
                                    ).then_inc(cond_parts_ready, 1)
            with dve.Fori(0, MODS // 4) as i:
                for u in range(2):
                    dve.wait_ge(weights_hi, 4 * i + 3 + u)
                    nc.vector.tensor_tensor(w_lo[u][:], raw[2 + u][:], w_hi[u][:].bitcast(f32), ALU.subtract
                                            ).then_inc(unit_done[2 + u], 1)
                for j in range(2):
                    take_modulation(0, 2 * i + j, 2 * i + j)
            for c in range(KC):
                if c:
                    dve.wait_ge(summed, c)
                add_square(row(SUM), c, summed)
            n.ada, n.squared = MODS // 2, KC
            for layer, kind in enumerate(MIXERS):
                dve.wait_ge(ada_taken, n.ada)
                nc.vector.tensor_scalar(mod[:, layer % 2, SC1:SC1 + KC, :], mod[:, layer % 2, SC1:SC1 + KC, :],
                                        1.0, None, ALU.add)
                nc.vector.tensor_scalar(mod[:, layer % 2, SC2:SC2 + KC, :], mod[:, layer % 2, SC2:SC2 + KC, :],
                                        1.0, None, ALU.add).then_inc(mod_ready, 1)
                {"fnet": fnet, "pool": pool_mix, "mla": mla}[kind](layer)
                ffn(layer)
            recip(row(RSTD))
            for c in range(KC):
                nc.vector.scalar_tensor_tensor(y[:, c, :], x[:, c, :], g_final[:, c:c + 1], row(RSTD),
                                               ALU.mult, ALU.mult).then_inc(y_ready, 1)


def _weight_units(w, rows=None, cols=None):
    k, m = w.shape
    u = w.reshape(k // P, P, m // P, P).transpose(2, 1, 0, 3).reshape(m // P, P, k)
    return _padded(u)


def _padded(u):
    out = np.zeros((u.shape[0], P, UNIT), np.float32)
    out[:, :, :u.shape[2]] = u
    return out


def _fourier_units():
    def angle(size):
        i = np.arange(size)
        return 2 * np.pi * ((i[:, None] * i[None, :]) % size) / size
    ch, cx, sq = angle(GROUP), angle(CTX), angle(LAT)
    chan = np.concatenate([np.cos(ch), np.sin(ch)], 1) / np.sqrt(GROUP)
    units = [chan.reshape(2, P, 2 * GROUP).transpose(1, 0, 2).reshape(1, P, 4 * GROUP)]
    units.append(np.concatenate([np.cos(cx), -np.sin(cx)], 1)[None] / np.sqrt(CTX))
    for t in (np.cos(sq), -np.sin(sq)):
        units.append((t / np.sqrt(LAT)).reshape(2, 2, P, LAT).transpose(0, 2, 1, 3).reshape(2, P, 2 * LAT))
    return np.concatenate([_padded(u.astype(np.float32)) for u in units])


def _stream(w):
    ada = np.concatenate([_weight_units(w["w_ada"][l]) for l in range(DEPTH)])
    out = [ada[:MODS]]
    f = 0
    for layer, kind in enumerate(MIXERS):
        rest = ada[MODS * (layer + 1) - (2 if layer else 0):MODS * (layer + 1) + 2]
        if kind == "fnet":
            u = _weight_units(w["w_fnet"][f])
            f += 1
            out += [u[:2], _fourier_units(), rest, u[2:]]
        elif kind == "pool":
            g = w["w_pool"][0].reshape(GROUPS, 2, P, 2, P).transpose(0, 2, 3, 1, 4).reshape(GROUPS, P, 4 * P)
            u = _padded(g)
            out += [u[:2], rest, u[2:]]
        else:
            dkv = w["w_dkv"][0]
            ckv = _weight_units(dkv[:, :KV_RANK])
            kpe = np.concatenate([dkv[:, KV_RANK:]] * 2, 1)
            kpe = np.concatenate([_weight_units(kpe[:D // 2]), _weight_units(kpe[D // 2:])])
            out += [ckv, kpe, _weight_units(w["w_dq"][0])]
            uq = w["w_uq"][0].reshape(Q_RANK, HEADS, NOPE + ROPE)
            ukv = w["w_ukv"][0].reshape(KV_RANK, HEADS, NOPE + VH)
            for h in range(0, HEADS, 2):
                v = ukv[:, h:h + 2, NOPE:].reshape(RC, P, 2 * VH).transpose(1, 0, 2).reshape(1, P, RC * 2 * VH)
                out += [v, _weight_units(uq[:, h:h + 2, NOPE:].reshape(Q_RANK, 2 * ROPE))]
                for k in (h, h + 1):
                    out += [_weight_units(ukv[:, k, :NOPE]), _weight_units(uq[:, k, :NOPE])]
            u = _weight_units(w["w_o"][0])
            out += [u[:4], rest, u[4:]]
        w_in, w_out = _weight_units(w["w_ffn_in"][layer]), w["w_ffn_out"][layer]
        for first, count in PARTS:
            for p in range(first, first + count):
                out += [w_in[p:p + 1], w_in[PAIRS + p:PAIRS + p + 1]]
                if ada_in_ffn(layer):
                    first_unit = MODS * (layer + 1) + 2 * (p + 1)
                    out.append(ada[first_unit:first_unit + 2])
            out.append(_weight_units(w_out[first * P:(first + count) * P]))
    return np.concatenate(out)


def _tokens(ctx_t, lat_t):
    c = ctx_t.shape[0]
    out = np.zeros((c // P, P, W), np.float32)
    out[:, :, 0:CTX] = ctx_t.reshape(c // P, P, CTX)
    out[:, :, LAT0:LAT1] = lat_t.reshape(c // P, P, LAT)
    return out


def _rope_tables():
    grid_w, axis = 64, ROPE // 2
    inv = (1.0 / (np.float32(10000.0) ** (np.arange(0, axis, 2, dtype=np.float32) / np.float32(axis)))).astype(np.float32)
    t = np.arange(LAT)
    out = np.zeros((P, 2, W), np.float32)
    out[:, 0, 0:CTX] = 1.0
    swap = np.zeros((P, P), np.float32)
    for p in range(P):
        d = p % ROPE
        pos = (t // grid_w if d < axis else t % grid_w).astype(np.float32)
        ang = pos * inv[d % (axis // 2)]
        upper = d % axis >= axis // 2
        out[p, 0, LAT0:LAT1] = np.cos(ang)
        out[p, 1, LAT0:LAT1] = np.sin(ang) if upper else -np.sin(ang)
        swap[p - axis // 2 if upper else p + axis // 2, p] = 1.0
    return out, swap


def _inverse_counts():
    out = np.zeros((4, PADW), np.float32)
    for g in range(4):
        w = 2 ** (g + 1)
        for start, size in ((PC, CTX), (PL, LAT)):
            t = np.arange(size)
            lo, hi = np.clip(t - w // 2, 0, size), np.clip(t - w // 2 + w, 0, size)
            out[g, start:start + size] = 1.0 / (hi - lo)
    return np.ascontiguousarray(np.broadcast_to(out, (P, 4, PADW)))


def _columns(v):
    return np.moveaxis(v.reshape(*v.shape[:-1], -1, P), -1, -2)


def kernel(**inputs):
    import concourse.bacc as bacc
    from concourse.bass_utils import run_bass_kernel_spmd

    w = {k: np.asarray(v) for k, v in inputs.items()}
    rope, swap = _rope_tables()
    conv = np.concatenate([w["w_ffn_conv"], w["b_ffn_conv"][:, None]], 1)
    cache = np.zeros((P, RC + 1, PAST), np.float32)
    cache[:, :RC] = w["cache_ckv"][0, 0].T.reshape(RC, P, PAST).transpose(1, 0, 2)
    cache[:, RC] = np.concatenate([w["cache_kpe"][0, 0].T] * 2, 0)
    arrays = {
        "stream": _stream(w),
        "x": _tokens(w["x_prompt"][0].T, w["x_sample"][0].T),
        "cond": np.stack([_columns(w["c_ctx"]), _columns(w["c"][0])], -1),
        "b_ada": np.stack([_columns(w["b_ada"])] * 2, -1),
        "conv_w": _columns(conv).transpose(0, 2, 3, 1),
        "gains": np.concatenate([_columns(w["g_q"][0]), _columns(w["g_kv"][0]), _columns(w["g_final"]),
                                 _columns(w["pool_scale"][0])], 1),
        "cache": cache,
        "rope": rope,
        "perm": swap,
        "ident": np.eye(P, dtype=np.float32),
        "ones": np.ones((P, P), np.float32),
        "inv_count": _inverse_counts(),
    }
    arrays = {k: np.ascontiguousarray(v) for k, v in arrays.items()}
    outs = {"y": (KC, P, W), "state_ckv": (P, RC, CTX), "state_kpe": (ROPE, CTX)}
    nc = bacc.Bacc("TRN2", target_bir_lowering=False, num_devices=1)
    f32 = mybir.dt.float32
    aps = {k: nc.dram_tensor(f"in_{k}", v.shape, f32, kind="ExternalInput").ap() for k, v in arrays.items()}
    aps |= {k: nc.dram_tensor(f"out_{k}", s, f32, kind="ExternalOutput").ap() for k, s in outs.items()}
    build_backbone(nc, aps)
    r = run_bass_kernel_spmd(nc, [{f"in_{k}": v for k, v in arrays.items()}], core_ids=[0]).results[0]
    y = r["out_y"].reshape(D, W)
    ckv = r["out_state_ckv"].transpose(1, 0, 2).reshape(KV_RANK, CTX)
    return (np.ascontiguousarray(y[:, :CTX].T)[None], np.ascontiguousarray(y[:, LAT0:LAT1].T)[None],
            np.ascontiguousarray(ckv.T)[None, None], np.ascontiguousarray(r["out_state_kpe"].T)[None, None])
```

```python
from contextlib import ExitStack

import concourse.bass as bass
import numpy as np
from concourse import mybir

P = 128
D = 1024
KC = D // P
CTX, LAT, PAST = 128, 512, 128
GAP = 2
LAT0 = CTX + GAP
LAT1 = LAT0 + LAT
W = LAT1 + GAP
HALF = W // 2
DEPTH = 4
N_MOD = 6
MODS = N_MOD * KC
D_FF = 2816
PAIRS = D_FF // P
PARTS = [(0, 8), (8, 8), (16, 6)]
GROUPS, GROUP = 4, 256
HEADS, NOPE, ROPE, VH = 8, 128, 64, 128
Q_RANK, KV_RANK = 768, 512
QC, RC = Q_RANK // P, KV_RANK // P
SM_SCALE = (NOPE + ROPE) ** -0.5
EPS = 1e-6
UNIT = 1024
SLOTS = 4
KEYS = LAT1 + PAST
KW = KEYS + GAP
KHALF = KW // 2
NK = LAT + PAST
SHALF = NK // 2
KTILES = NK // P
PADW = 8 + CTX + 8 + LAT + 8
PC, PL = 8, 8 + CTX + 8
MIXERS = ["fnet", "pool", "mla", "fnet"]
SH1, SC1, G1, SH2, SC2, G2 = (KC * i for i in range(N_MOD))

TABLES, EARLY_TABLES = 8, 6
LATENT_SIZES = [UNIT] * RC + [UNIT // 2] * 2 + [UNIT] * QC
HEAD_SIZES = [RC * P, QC * P, QC * P, RC * 2 * VH, RC * P, QC * P]
T_RESULTS = [[10, 12, 14, 18, 20], [22, 24, 26, 28, 30]]
O_RESULTS = [[11, 13, 15, 19, 21], [23, 25, 27, 29, 31]]
K_RESULTS, QPE_RESULT, Q_RESULTS, ROTATION = [0, 16], 1, [2, 17], 3
V_RESULT = 4
Q_TILES = [(LAT0 + P * t, LAT0, SHALF, 2) for t in range(4)] + [(0, 0, CTX, 1)]
FIRST_LOADS = 16 * 3
SMALL_LOADS = 16 * (KC + 4)
TABLES_POOL, TABLES_MLA, TABLES_ROPE = 16, 32, 48


def layer_loads(layer):
    return 16 * (2 * layer + min(2, DEPTH - layer))


def ada_in_ffn(layer):
    return layer + 1 < DEPTH


ADA_EXTRA, EXTRA_PART = MODS - 2 * PAIRS, 1

FIRST_MODS, PRODUCT_MODS = 2 * KC, KC
PE_PLACES = (1, 4, 7, 10, 13, 15)
PE_MODS = len(PE_PLACES)
DVE_MODS = FIRST_MODS - PE_MODS
LATE_STEPS = (0, 0, 0, 0, 2, 2, 2)
PRODUCT_STEPS = (0, 1, 2, 2, 2, 1, 0, 0)


def late_mods(layer):
    return MODS - FIRST_MODS - PRODUCT_MODS if layer == 0 else 0


def product_mods(layer):
    return PRODUCT_MODS if layer == 0 else 0


def extra(layer, part):
    return ADA_EXTRA if ada_in_ffn(layer) and part == EXTRA_PART else 0


class Counts:

    def __init__(self):
        self.unit = 0
        self.result = 0
        self.split = 0
        self.ada = 0
        self.pair = 0
        self.rounded = 0
        self.stat = 0
        self.chunk = 0
        self.full = 0
        self.affine = 0
        self.squared = 0
        self.score = 0
        self.cleared = 0


def wait_past(engine, semaphore, count):
    if not (isinstance(count, int) and count == 0):
        engine.wait_ge(semaphore, count)


def build_backbone(nc, a):
    f32, f32r = mybir.dt.float32, mybir.dt.float32r
    ACT = mybir.ActivationFunctionType
    ALU = mybir.AluOpType
    AX = mybir.AxisListType
    ds = bass.ds
    n_units = a["stream"].shape[0]

    with ExitStack() as ctx:
        sem = lambda name: ctx.enter_context(nc.semaphore(name))
        pb = lambda name, shape: ctx.enter_context(nc.psum_tensor(name, shape, f32))
        at = [(nc.sbuf_base + 31) // 32 * 32]

        def place(name, shape, dt=f32, offset=None):
            size = 4 * int(np.prod(shape[1:]))
            where = at[0] if offset is None else offset
            if offset is None:
                at[0] += size
            assert where + size <= nc.sbuf_usable_end, name
            return nc.alloc_sbuf_tensor_at(name, shape, dt, offset=where, align_bytes=4)

        x = place("x", [P, KC, W])
        h_hi, h_lo = place("h_hi", [P, KC, W], f32r), place("h_lo", [P, KC, W], f32r)
        raw = [place(f"raw{s}", [P, UNIT]) for s in range(SLOTS)]
        w_hi = [place(f"w_hi{s}", [P, UNIT], f32r) for s in range(2)]
        w_lo = [place(f"w_lo{s}", [P, UNIT], f32r) for s in range(2)]
        rows = place("rows", [P, 7, W])
        mod = place("mod", [P, 2, MODS, 2])
        b_ada = place("b_ada", [P, 2, MODS, 2])
        conv_w = place("conv_w", [P, 2 * PAIRS, 4])
        ident, ones, perm = place("ident", [P, P]), place("ones", [P, P]), place("perm", [P, P])
        cond_columns = place("cond_columns", [P, KC, 2])
        gains = place("gains", [P, QC + RC + 2 * KC])
        g_q, g_kv = gains[:, 0:QC], gains[:, QC:QC + RC]
        g_final = gains[:, QC + RC:QC + RC + KC]
        pool_scale = gains[:, QC + RC + KC:]
        eps = place("eps", [P, 1])
        gate_pool = place("gate_pool", [P, KC, 2])
        top, negtop, total, inverse = (place(n, [P, 2]) for n in ("top", "negtop", "total", "inverse"))
        g_at = at[0]
        g_hi, g_lo = place("g_hi", [P, 8, W], f32r), place("g_lo", [P, 8, W], f32r)
        seq_t = [[place(f"seq_t{c}{p}", [P, 4, LAT], f32r, g_at + (2 * c + p) * 8192) for p in range(2)]
                 for c in range(2)]
        ctx_t = [place(f"ctx_t{p}", [P, 2, CTX], f32r, g_at + 32768 + 1024 * p) for p in range(2)]
        cq_hi = place("cq_hi", [P, QC, W], f32r, g_at)
        cq_lo = place("cq_lo", [P, QC, W], f32r, g_at + 4 * QC * W)
        cache = place("cache", [P, RC + 1, PAST], f32, g_at)
        tail = g_at + 8 * QC * W
        ckv_raw = place("ckv_raw", [P, RC, W], f32, tail)
        q_hi, q_lo = place("q_hi", [P, W], f32r, tail), place("q_lo", [P, W], f32r, tail + 4 * W)
        pt_hi = place("pt_hi", [P, KTILES, P], f32r, tail + 8 * W)
        pt_lo = place("pt_lo", [P, KTILES, P], f32r, tail + 8 * W + 4 * NK)
        e_at = at[0]
        conv = [place(f"conv{j}", [P, W + 2], f32, e_at + 4 * (W + 2) * j) for j in range(2)]
        gated = place("gated", [P, W], f32, e_at + 8 * (W + 2))
        chan_t = [place(f"chan_t{p}", [P, 2, 2 * GROUP], f32r, e_at + 4096 * p) for p in range(2)]
        freq = [place(f"freq{p}", [P, 5, 2 * GROUP], f32r, e_at + 8192 + 10240 * p) for p in range(2)]
        inv_count = place("inv_count", [P, 4, PADW], f32, e_at)
        padded = [place(f"padded{j}", [P, PADW], f32, e_at + 4 * PADW * (4 + j)) for j in range(2)]
        window = [place(f"window{j}", [P, PADW], f32, e_at + 4 * PADW * (6 + j)) for j in range(2)]
        scratch = place("scratch", [P, PADW], f32, e_at + 4 * PADW * 8)
        y = place("y", [P, KC, W], f32, g_at)
        ckv_hi, ckv_lo = place("ckv_hi", [P, RC, KW], f32r), place("ckv_lo", [P, RC, KW], f32r)
        kpe_hi, kpe_lo = place("kpe_hi", [P, KW], f32r), place("kpe_lo", [P, KW], f32r)
        v_at = at[0]
        v_hi, v_lo = place("v_hi", [P, 6, 2 * VH], f32r), place("v_lo", [P, 6, 2 * VH], f32r)
        k_hi, k_lo = place("k_hi", [P, KW], f32r), place("k_lo", [P, KW], f32r)
        qpe_hi, qpe_lo = place("qpe_hi", [P, W], f32r), place("qpe_lo", [P, W], f32r)
        cq_raw = place("cq_raw", [P, QC, W], f32, v_at)
        kpe_raw, kpe_cos, kpe_sin = (place(f"kpe_{n}", [P, W], f32, v_at + 4 * W * (QC + j))
                                     for j, n in enumerate(("raw", "cos", "sin")))
        cond = place("cond", [P, 2, D], f32, at[0] - 8 * D)
        products_at = at[0] - 8 * D - 16 * UNIT
        products = [[place(f"products{u}{z}", [P, UNIT], f32, products_at + 4 * UNIT * (2 * u + z)) for z in range(2)]
                    for u in range(2)]
        SUM, SQ, RSTD, HF = 0, 1, 2, 5
        XN = (3, 4, SQ)
        row = lambda i: rows[:, i, :]
        tab_cos, tab_sin = row(5), row(6)
        sum_q, rstd_q = row(3), row(4)
        probs = [row(3), row(4)]
        q_raw, q_rot = row(0), row(1)

        acc = [pb("acc0", [P, 2, 512]), pb("acc1", [P, 2, 512])]
        sacc = [pb("sacc0", [P, 2, 512]), pb("sacc1", [P, 2, 512])]
        halves = lambda t: t[:, :, 0:HALF]
        two = lambda ap: ap.rearrange("p (a b) -> p a b", a=2)

        first_loaded = sem("first_loaded")
        loaded = sem("loaded")
        layer_loaded = sem("layer_loaded")
        table_loaded = sem("table_loaded")
        raw_ready = [sem(f"raw_ready{s}") for s in range(SLOTS)]
        unit_done = [sem(f"unit_done{s}") for s in range(SLOTS)]
        weights_hi = sem("weights_hi")
        result_ready = sem("result_ready")
        result_taken = sem("result_taken")
        result_rounded = sem("result_rounded")
        ada_summed = sem("ada_summed")
        ada_biased = sem("ada_biased")
        cond_ready = sem("cond_ready")
        centered = sem("centered")
        left_done = sem("left_done")
        silu_done = sem("silu_done")
        gated_done = sem("gated_done")
        g_rounded = sem("g_rounded")
        g_ready = sem("g_ready")
        squared = sem("squared")
        summed = sem("summed")
        stat_ready = sem("stat_ready")
        rooted = sem("rooted")
        rstd_done = sem("rstd_done")
        xn_ready = sem("xn_ready")
        h_full = sem("h_full")
        h_affine = sem("h_affine")
        h_rounded = sem("h_rounded")
        h_ready = sem("h_ready")
        mod_ready = sem("mod_ready")
        setup_done = sem("setup_done")
        pool_step = sem("pool_step")
        pooled_full = sem("pooled_full")
        rope_step = sem("rope_step")
        score_ready = sem("score_ready")
        score_taken = sem("score_taken")
        top_done = sem("top_done")
        bias_done = sem("bias_done")
        exp_done = sem("exp_done")
        inverse_done = sem("inverse_done")
        latent_normed = sem("latent_normed")
        latent_squared = sem("latent_squared")
        latent_rounded = sem("latent_rounded")
        latent_ready = sem("latent_ready")
        sum_cleared = sem("sum_cleared")
        conv_padded = sem("conv_padded")
        cached = sem("cached")
        cache_rounded = sem("cache_rounded")
        stored = sem("stored")
        y_ready = sem("y_ready")

        block = ctx.enter_context(nc.Block())

        CXS, LTS = slice(0, CTX), slice(LAT0, LAT1)

        def fnet_tables():
            out = [(chan_t[0][:, k, :], chan_t[1][:, k, :], 2 * GROUP) for k in range(2)]
            out += [(ctx_t[0][:, c, :], ctx_t[1][:, c, :], CTX) for c in range(2)]
            flat = lambda t, k: t[:, 2 * k:2 * k + 2, :].rearrange("p a b -> p (a b)")
            out += [(flat(seq_t[c][0], k), flat(seq_t[c][1], k), UNIT) for c in range(2) for k in range(2)]
            return out

        def transposed_pieces(dst, src, tiles):
            flat = lambda z0, z1: dst[:, z0:z1, :].rearrange("p a b -> p (a b)")
            if tiles == 1:
                return [(flat(0, 1), src[:, 0, 0:P])]
            return [(flat(0, 4), src[:, 0, :]), (flat(4, 5), src[:, 1, 0:P])]

        def head_out(dst, i, h2, hh, q0):
            return dst[:, ds(4 * i + 2 * h2 + hh, 1), q0:q0 + P].rearrange("p o t -> p (o t)")

        def after_ffn_in(n, layer, count):
            n.unit += 4 * count if ada_in_ffn(layer) else 2 * count
            n.split += 2 * count
            n.result += 2 * count
            n.pair += count
            n.ada += 2 * count if ada_in_ffn(layer) else 0

        def after_project(n, units=KC, squares=True):
            n.unit += units
            n.split += units
            n.result += KC
            n.squared += KC if squares else 0

        @block.sync
        def _(sp):
            for s in range(SLOTS):
                sp.dma_start(raw[s][:], a["stream"][s]).then_inc(raw_ready[s], 16)
            with sp.Fori(1, n_units // SLOTS) as i:
                for s in range(SLOTS):
                    sp.wait_ge(unit_done[s], i)
                    sp.dma_start(raw[s][:], a["stream"][ds(i * SLOTS + s, 1)].rearrange("o p n -> (o p) n")
                                 ).then_inc(raw_ready[s], 16)

        @block.gpsimd
        def _(pool):
            n = Counts()

            def cut(slot, split, hi, lo, raw_size):
                pool.wait_ge(weights_hi, split + 1)
                nc.gpsimd.tensor_tensor(lo, raw[slot][:, 0:raw_size], hi.bitcast(f32), ALU.subtract
                                        ).then_inc(unit_done[slot], 1)

            def ring(slot, split, size=UNIT):
                cut(slot, split, w_hi[slot % 2][:, 0:size], w_lo[slot % 2][:, 0:size], size)

            def lo_parts():
                for c in range(KC):
                    pool.wait_ge(h_rounded, n.chunk + c + 1)
                    nc.gpsimd.tensor_tensor(h_lo[:, c, :], row(HF + c % 2), h_hi[:, c, :].bitcast(f32), ALU.subtract
                                            ).then_inc(h_ready, 1)
                n.chunk += KC

            def pooling():
                def scale_x(c):
                    nc.gpsimd.tensor_tensor(row(XN[c % 3]), x[:, c, :], row(RSTD), ALU.mult).then_inc(xn_ready, 1)

                def pooled_lo(c):
                    pool.wait_ge(h_rounded, n.chunk + c + 1)
                    for to, cols in ((CXS, slice(PC, PC + CTX)), (LTS, slice(PL, PL + LAT))):
                        done = nc.gpsimd.tensor_tensor(h_lo[:, c, to], window[c % 2][:, cols],
                                                       h_hi[:, c, to].bitcast(f32), ALU.subtract)
                    done.then_inc(h_ready, 1)

                pool.wait_ge(rstd_done, n.stat + 1)
                scale_x(0)
                scale_x(1)
                for c in range(KC):
                    if c + 2 < KC:
                        if c:
                            pool.wait_ge(h_full, n.full + c)
                        scale_x(c + 2)
                    if c:
                        pooled_lo(c - 1)
                pooled_lo(KC - 1)
                n.chunk += KC

            def project(size, last=False):
                for j in range(6 if last else 8):
                    ring((j + 2) % SLOTS, n.split + 2 + j, size if j < 6 else UNIT)

            def ffn(layer):
                lo_parts()
                n.stat += 1
                for part, (_, count) in enumerate(PARTS):
                    if ada_in_ffn(layer):
                        with pool.Fori(0, count) as i:
                            ring(0, n.split + 2 * i + 2)
                            ring(1, n.split + 2 * i + 3)
                    else:
                        with pool.Fori(0, count // 2) as i:
                            for j in range(4):
                                ring((j + 2) % SLOTS, n.split + 4 * i + 2 + j)
                    after_ffn_in(n, layer, count)
                    project(count * P, part == 2 and layer == DEPTH - 1)
                    after_project(n, squares=part == 2)

            ring(0, n.split)
            ring(1, n.split + 1)
            for layer, kind in enumerate(MIXERS):
                if kind == "fnet":
                    n.full += KC // 2
                    n.chunk += KC
                    for j, (hi, lo, size) in enumerate(fnet_tables()):
                        cut((2 + j) % SLOTS, n.split + 2 + j, hi, lo, size)
                    n.split += TABLES
                    project(UNIT)
                    n.split += KC
                elif kind == "pool":
                    pooling()
                    for j in range(2, 6):
                        ring(j % SLOTS, n.split + j, 2 * GROUP if j < 4 else UNIT)
                    n.split += 4
                else:
                    lo_parts()
                    for j in range(2, 14):
                        ring(j % SLOTS, n.split + j, (LATENT_SIZES + HEAD_SIZES)[j])
                    n.split += len(LATENT_SIZES)
                    with pool.Fori(0, 2) as i:
                        for j in range(12):
                            ring((j + 2) % SLOTS, n.split + 12 * i + j + 2, UNIT if j > 9 else HEAD_SIZES[(j + 2) % 6])
                    n.split += 24
                    project(UNIT)
                    n.split += KC
                n.stat += 3 if kind == "mla" else 1
                ffn(layer)

        @block.tensor
        def _(pe):
            n = Counts()

            def product(outs, lhs, rhs, first=True, last=True):
                for z, (lp, rp) in enumerate(((0, 0), (0, 1), (1, 0))):
                    for o, r in zip(outs, rhs[rp]):
                        done = nc.tensor.matmul(o, lhs[lp], r, start=first and z == 0, stop=last and z == 2)
                return done

            def token_halves(hi, lo):
                return [[t[:, 0:HALF], t[:, HALF:W]] for t in (hi, lo)]

            def acc_halves(p, size=HALF):
                return [acc[p][:, b, 0:size] for b in range(2)]

            def weights(slot, k, width=P):
                return [w[slot % 2][:, k * width:(k + 1) * width] for w in (w_hi, w_lo)]

            def uses(*units):
                return [(u % SLOTS, u // SLOTS + 1) for u in units]

            def statistics(source):
                for b in range(2):
                    done = nc.tensor.matmul(sacc[0][:, b, 0:HALF], ones[:], source[:, b * HALF:(b + 1) * HALF],
                                            start=True, stop=True)
                done.then_inc(stat_ready, 1)
                n.stat += 1

            def norm():
                pe.wait_ge(summed, n.squared)
                statistics(row(SUM))
                n.chunk += KC

            def project(source, kn, ready=None, ready_from=0, extra_units=(0, 0)):
                def turn(i, base, late_base):
                    for j in range(4):
                        pe.wait_ge(unit_done[j], (base if j < 2 else late_base) // SLOTS + i + 1)
                        pe.wait_ge(result_taken, n.result + 4 * i + j - 1)
                        for k in range(kn):
                            if j == 0 and ready is not None:
                                pe.wait_ge(ready, ready_from + k + 1)
                            done = product(acc_halves(j % 2), weights(j, k),
                                           token_halves(source[0][:, k, :], source[1][:, k, :]),
                                           k == 0, k == kn - 1)
                        done.then_inc(result_ready, 1)

                if any(extra_units):
                    for i, more in enumerate(extra_units):
                        turn(i, n.unit, n.unit + more)
                        n.unit += more
                else:
                    with pe.Fori(0, 2) as i:
                        turn(i, n.unit, n.unit)

            def first_two():
                for j in range(2):
                    pe.wait_ge(unit_done[j], n.unit // SLOTS + 1)
                    pe.wait_ge(result_taken, n.result + j - 1)

                def chunk(j, k):
                    done = product(acc_halves(j), weights(j, k), token_halves(h_hi[:, k, :], h_lo[:, k, :]),
                                   k == 0, k == KC - 1)
                    if k == KC - 1:
                        done.then_inc(result_ready, 1)

                for k in range(KC):
                    pe.wait_ge(h_ready, n.chunk - KC + k + 1)
                    chunk(0, k)
                    if k % 2:
                        chunk(1, k // 2)
                for k in range(KC // 2, KC):
                    chunk(1, k)

            def ffn(layer):
                norm()
                for part, (_, count) in enumerate(PARTS):
                    turn = 1 if ada_in_ffn(layer) else 2

                    def gate_or_value(i, j):
                        pe.wait_ge(unit_done[j], n.unit // SLOTS + i + 1)
                        pe.wait_ge(result_taken, n.result + 2 * turn * i + j - 1)
                        for k in range(KC):
                            done = product(acc_halves(j % 2), weights(j, k),
                                           token_halves(h_hi[:, k, :], h_lo[:, k, :]), k == 0, k == KC - 1)
                        done.then_inc(result_ready, 1)

                    if part == 0:
                        first_two()
                        for j in range(2, 2 * turn):
                            gate_or_value(0, j)
                    with pe.Fori(int(part == 0), count // turn) as i:
                        for j in range(2 * turn):
                            gate_or_value(i, j)
                    after_ffn_in(n, layer, count)
                    project((g_hi, g_lo), count, g_ready, n.pair - count, (extra(layer, part), 0))
                    after_project(n, squares=part == 2)

            def fnet(layer):
                r = n.result
                for g in range(GROUPS):
                    for t in range(5):
                        first = 0 if t == 0 else LAT0 + P * (t - 1)
                        if r >= 2:
                            pe.wait_ge(result_taken, r - 1)
                        if g == 0 and t == 0:
                            for slot, use in uses(n.unit + 2, n.unit + 3):
                                pe.wait_ge(unit_done[slot], use)
                        for k in range(2):
                            c = 2 * g + k
                            if t == 0:
                                pe.wait_ge(h_ready, n.chunk - KC + c + 1)
                            done = product([acc[r % 2][:, 0, :]],
                                           [hh[:, c, first:first + P] for hh in (h_hi, h_lo)],
                                           [[chan_t[p][:, k, :]] for p in range(2)], k == 0, k == 1)
                        done.then_inc(result_ready, 1)
                        r += 1
                    if g == 0:
                        for slot, use in uses(*range(n.unit + TABLES - 2, n.unit + 2 + TABLES)):
                            pe.wait_ge(unit_done[slot], use)
                    for m in range(2):
                        pe.wait_ge(result_taken, r if m == 0 else r - 1)
                        for c in range(2):
                            col = c * GROUP + m * P
                            product([acc[r % 2][:, 0, 0:CTX]], [f[:, 0, col:col + P] for f in freq],
                                    [[ctx_t[p][:, c, :]] for p in range(2)], c == 0, c == 1)
                        for c in range(2):
                            col = c * GROUP + m * P
                            for t in range(4):
                                done = product([acc[r % 2][:, 1, :]],
                                               [f[:, t + 1, col:col + P] for f in freq],
                                               [[seq_t[c][p][:, t, :]] for p in range(2)],
                                               c == 0 and t == 0, c == 1 and t == 3)
                        done.then_inc(result_ready, 1)
                        r += 1
                n.result = r
                n.unit += TABLES
                pe.wait_ge(result_taken, n.result)
                project((h_hi, h_lo), KC, extra_units=(late_mods(layer), product_mods(layer)))
                after_project(n)

            def pool_mix():
                for j in range(KC):
                    u = j // 2
                    pe.wait_ge(unit_done[u], n.unit // SLOTS + 1)
                    pe.wait_ge(result_taken, n.result - 1 + j)
                    for k in range(2):
                        c = 2 * u + k
                        pe.wait_ge(h_ready, n.chunk - KC + c + 1)
                        done = product(acc_halves(j % 2), weights(u, 2 * (j % 2) + k),
                                       token_halves(h_hi[:, c, :], h_lo[:, c, :]), k == 0, k == 1)
                    done.then_inc(result_ready, 1)
                after_project(n, 4)

            def rotate(source, out):
                for b in range(2):
                    done = nc.tensor.matmul(out[:, b, 0:HALF], perm[:], source[:, b * HALF:(b + 1) * HALF],
                                            start=True, stop=True)
                done.then_inc(result_ready, 1)

            def unit_product(out, unit, size, rhs, first=True, last=True, k0=0):
                pe.wait_ge(unit_done[unit % SLOTS], unit // SLOTS + 1)
                for k in range(size):
                    done = product(out, weights(unit, k), rhs(k0 + k), first and k == 0, last and k == size - 1)
                return done

            def latents():
                h_of = lambda k: token_halves(h_hi[:, k, :], h_lo[:, k, :])
                r, u = n.result, n.unit
                first_two()
                r, u = r + 2, u + 2
                for m in range(2, RC):
                    pe.wait_ge(result_taken, r - 1)
                    unit_product(acc_halves(r % 2), u, KC, h_of).then_inc(result_ready, 1)
                    r, u = r + 1, u + 1
                pe.wait_ge(result_taken, r - 1)
                unit_product(acc_halves(r % 2), u, 4, h_of, last=False)
                unit_product(acc_halves(r % 2), u + 1, 4, h_of, first=False, k0=4).then_inc(result_ready, 1)
                r, u = r + 1, u + 2
                for m in range(QC):
                    pe.wait_ge(result_taken, r - 1)
                    unit_product(acc_halves(r % 2), u, KC, h_of).then_inc(result_ready, 1)
                    r, u = r + 1, u + 1
                    if m == 0:
                        pe.wait_ge(result_taken, r - 1)
                        rotate(kpe_raw, acc[r % 2])
                        r += 1
                    if m == 1:
                        pe.wait_ge(result_taken, n.result + RC)
                        statistics(row(SUM))
                pe.wait_ge(result_taken, r)
                pe.wait_ge(rooted, n.stat)
                statistics(sum_q)
                n.result, n.unit = r, u

            def attention():
                with pe.Fori(0, 2) as i:
                    for h2 in range(2):
                        r = n.result + 64 * i + 32 * h2
                        s = n.score + 20 * i + 10 * h2
                        use = lambda j: n.unit // SLOTS + 3 * i + (6 * h2 + j) // SLOTS + 1
                        slot = lambda j: (6 * h2 + j) % SLOTS

                        def accumulator(index):
                            pe.wait_ge(result_taken, r + index - 1)
                            return index % 2

                        def project_unit(index, j, size, half, source, ready=None, ready_from=0):
                            pe.wait_ge(unit_done[slot(j)], use(j))
                            p = accumulator(index)
                            for k in range(size):
                                if ready is not None:
                                    pe.wait_ge(ready, ready_from + k + 1)
                                done = product(acc_halves(p, half), weights(slot(j), k),
                                               [[c[:, k, 0:half], c[:, k, half:2 * half]] for c in source],
                                               k == 0, k == size - 1)
                            done.then_inc(result_ready, 1)

                        def values(t):
                            p = accumulator(V_RESULT + t)
                            first = [0, LAT0, LAT0 + P, LAT0 + 2 * P, LAT0 + 3 * P, LAT1][t]
                            for k in range(RC):
                                done = product([acc[p][:, 0, 0:2 * VH]],
                                               [c[:, k, first:first + P] for c in (ckv_hi, ckv_lo)],
                                               [[w] for w in weights(slot(3), k, 2 * VH)], k == 0, k == RC - 1)
                            done.then_inc(result_ready, 1)

                        def scores(hh, t):
                            q0, k0, width, banks = Q_TILES[t]
                            b = (5 * hh + t) % 2
                            head_rows = slice(ROPE * hh, ROPE * hh + ROPE)
                            if t == 0:
                                pe.wait_ge(result_taken, r + Q_RESULTS[hh] + 1)
                                pe.wait_ge(rope_step, 3 + (2 * i + h2 + 1) * 3)
                            pe.wait_ge(score_taken, s + 5 * hh + t + 1)
                            keys = lambda src, rows_: [[src_[rows_, k0 + width * z:k0 + width * (z + 1)]
                                                        for z in range(banks)] for src_ in src]
                            out = [sacc[b][:, z, 0:width] for z in range(banks)]
                            product(out, [q[:, q0:q0 + P] for q in (q_hi, q_lo)],
                                    keys((k_hi, k_lo), slice(0, P)), True, False)
                            product(out, [q[head_rows, q0:q0 + P] for q in (qpe_hi, qpe_lo)],
                                    keys((kpe_hi, kpe_lo), head_rows), False, True
                                    ).then_inc(score_ready, 1)

                        def transpose(hh, t):
                            q0, k0, width, banks = Q_TILES[t]
                            pe.wait_ge(score_taken, s + 5 * hh + t + 3)
                            p = accumulator(T_RESULTS[hh][t])
                            for z in range(width * banks // P):
                                done = nc.tensor.transpose(acc[p][:, z // 4, (z % 4) * P:(z % 4 + 1) * P],
                                                           probs[(5 * hh + t) % 2][:, z * P:(z + 1) * P], ident[:])
                            done.then_inc(result_ready, 1)

                        def weigh(hh, t):
                            q0, k0, width, banks = Q_TILES[t]
                            tiles = width * banks // P
                            pe.wait_ge(result_taken, r + T_RESULTS[hh][t] + 1)
                            p = accumulator(O_RESULTS[hh][t])
                            for z in range(tiles):
                                v = z + 1 if t < 4 else 0
                                done = product([acc[p][:, 0, 0:P]],
                                               [vv[:, v, hh * VH:(hh + 1) * VH] for vv in (v_hi, v_lo)],
                                               [[pt[:, z, :]] for pt in (pt_hi, pt_lo)],
                                               z == 0, z == tiles - 1)
                            done.then_inc(result_ready, 1)

                        cq, ckv = (cq_hi, cq_lo), (ckv_hi, ckv_lo)
                        if h2 == 0:
                            pe.wait_ge(cached, 2)
                            pe.wait_ge(latent_ready, 1 + RC)
                        project_unit(K_RESULTS[0], 0, RC, KHALF, ckv)
                        project_unit(QPE_RESULT, 1, QC, HALF, cq, latent_ready, 1 + RC)
                        project_unit(Q_RESULTS[0], 2, QC, HALF, cq)
                        p = accumulator(ROTATION)
                        pe.wait_ge(result_taken, r + QPE_RESULT + 1)
                        rotate(q_raw, acc[p])
                        pe.wait_ge(unit_done[slot(3)], use(3))
                        for t in range(6):
                            values(t)
                            if t in (1, 3):
                                scores(0, t // 2)
                        for t in range(3):
                            transpose(0, t)
                            scores(0, t + 2)
                            weigh(0, t)
                        project_unit(K_RESULTS[1], 4, RC, KHALF, ckv)
                        project_unit(Q_RESULTS[1], 5, QC, HALF, cq)
                        transpose(0, 3)
                        scores(1, 0)
                        weigh(0, 3)
                        transpose(0, 4)
                        scores(1, 1)
                        weigh(0, 4)
                        for t in range(5):
                            transpose(1, t)
                            if t < 3:
                                scores(1, t + 2)
                            weigh(1, t)
                n.result += 128
                n.score += 40
                n.unit += 24

            pe.wait_ge(cond_ready, 1)
            for m, place_ in enumerate(PE_PLACES):
                slot = place_ % SLOTS
                pe.wait_ge(raw_ready[slot], 16 * (place_ // SLOTS + 1))
                for k in range(KC):
                    done = nc.tensor.matmul(sacc[1][:, 0, 2 * m:2 * m + 2], raw[slot][:, k * P:(k + 1) * P],
                                            cond_columns[:, k, :], start=k == 0, stop=k == KC - 1)
                done.then_inc(unit_done[slot], 1)
            n.unit, n.squared = FIRST_MODS, KC
            pe.wait_ge(loaded, SMALL_LOADS)
            pe.wait_ge(setup_done, 1)
            for layer, kind in enumerate(MIXERS):
                norm()
                if kind == "fnet":
                    fnet(layer)
                elif kind == "pool":
                    pool_mix()
                else:
                    latents()
                    attention()
                    pe.wait_ge(result_taken, n.result)
                    project((h_hi, h_lo), KC)
                    after_project(n)
                ffn(layer)
            pe.wait_ge(summed, n.squared)
            statistics(row(SUM))

        @block.scalar
        def _(act):
            n = Counts()

            def round_unit(slot, use, hi, size, free=None):
                act.wait_ge(raw_ready[slot], 16 * use)
                if free is not None:
                    act.wait_ge(result_ready, free)
                nc.scalar.activation(hi, raw[slot][:, 0:size], ACT.Copy).then_inc(weights_hi, 1)

            def round_ring(slot, use, free=None, size=UNIT):
                round_unit(slot, use, w_hi[slot % 2][:, 0:size], size, free)

            def take(r, pieces):
                act.wait_ge(result_ready, r + 1)
                for dst, src in pieces:
                    done = nc.scalar.activation(dst, src, ACT.Copy)
                done.then_inc(result_rounded, 1)

            def root(width, to=row(RSTD)):
                act.wait_ge(stat_ready, n.stat + 1)
                nc.scalar.activation(two(to), halves(sacc[0]), ACT.Sqrt, bias=eps[:], scale=1.0 / width
                                     ).then_inc(rooted, 1)
                n.stat += 1

            def norm(layer, shift, scale, mine=lambda c: False, target=None, after_root=None, after_chunk=None):
                root(D)
                if after_root is not None:
                    after_root()
                for c in range(KC):
                    out = row(HF + c % 2) if target is None else padded[c % 2]
                    if mine(c):
                        act.wait_ge(xn_ready, n.chunk + c + 1)
                        if c >= 2 and target is None:
                            act.wait_ge(h_ready, n.chunk + c - 1)
                        elif c >= 2:
                            act.wait_ge(pooled_full, c - 1)
                        places = (CXS, LTS) if target is None else (slice(PC, PC + CTX), slice(PL, PL + LAT))
                        for z, (cols, to) in enumerate(zip((CXS, LTS), places)):
                            done = nc.scalar.activation(out[:, to], row(XN[c % 3])[:, cols], ACT.Identity,
                                                        bias=mod[:, layer % 2, shift + c, z:z + 1],
                                                        scale=mod[:, layer % 2, scale + c, z:z + 1])
                        done.then_inc(h_full, 1)
                        n.full += 1
                    else:
                        n.affine += 1
                    if target is None:
                        act.wait_ge(h_full if mine(c) else h_affine, n.full if mine(c) else n.affine)
                        nc.scalar.activation(h_hi[:, c, :], out, ACT.Copy).then_inc(h_rounded, 1)
                    else:
                        target(c)
                    if after_chunk is not None:
                        after_chunk(c)
                n.chunk += KC

            def square(source):
                nc.scalar.activation(row(SQ), source, ACT.Square).then_inc(squared, 1)

            def project_steps(i, squares, rounds=4):
                for j in range(4):
                    if j < rounds:
                        round_ring((j + 2) % SLOTS, n.unit // SLOTS + i + (j + 2) // SLOTS + 1, n.result + 4 * i + j + 1)
                    if squares:
                        act.wait_ge(result_taken, n.result + 4 * i + j + 1)
                        square(x[:, ds(4 * i + j, 1), :].rearrange("p o t -> p (o t)"))

            def project(squares=True, last=False, more=0):
                if more:
                    project_steps(0, squares)
                    n.unit += more
                    project_steps(1, squares)
                    return
                with act.Fori(0, 1 if last else 2) as i:
                    project_steps(i, squares)
                if last:
                    project_steps(1, squares, 2)

            def ffn(layer):
                act.wait_ge(mod_ready, layer + 2)
                norm(layer, SH2, SC2)
                nc.scalar.preload_act_table(ACT.Silu)
                if MIXERS[layer] == "mla":
                    activate_cond(FIRST_LOADS + 16)
                act.wait_ge(layer_loaded, layer_loads(layer))
                for part, (_, count) in enumerate(PARTS):
                    turn = 1 if ada_in_ffn(layer) else 2
                    with act.Fori(0, count // turn) as i:
                        for z in range(turn):
                            gate = turn * i + z
                            r = n.result + 2 * gate

                            def ahead_ring(k, free):
                                j = k + (2 * z if turn == 2 else 2)
                                round_ring(j % SLOTS, n.unit // SLOTS + i + j // SLOTS + 1, free)

                            channel = n.pair - layer * PAIRS + gate
                            taps = lambda half: [conv_w[:, ds(channel + half * PAIRS, 1), t:t + 1
                                                        ].rearrange("p o t -> p (o t)") for t in (1, 3)]
                            ahead_ring(2, r + 1)
                            w1, b1 = taps(0)
                            nc.scalar.activation(two(conv[0][:, 1:W + 1]), halves(acc[0]), ACT.Identity,
                                                 bias=b1, scale=w1).then_inc(centered, 1)
                            act.wait_ge(result_taken, r + 1)
                            nc.scalar.activation(gated[:], conv[0][:, 1:W + 1], ACT.Silu).then_inc(silu_done, 1)
                            ahead_ring(3, r + 2)
                            w1, b1 = taps(1)
                            nc.scalar.activation(two(conv[1][:, 1:W + 1]), halves(acc[1]), ACT.Identity,
                                                 bias=b1, scale=w1).then_inc(centered, 1)
                            act.wait_ge(gated_done, n.pair + gate + 1)
                            nc.scalar.activation(g_hi[:, ds(gate, 1), :].rearrange("p o t -> p (o t)"), gated[:],
                                                 ACT.Copy).then_inc(g_rounded, 1)
                    after_ffn_in(n, layer, count)
                    last = part == 2
                    n.unit += extra(layer, part)
                    if last:
                        nc.scalar.preload_act_table(ACT.Sqrt)
                    project(last, last and layer == DEPTH - 1)
                    after_project(n, squares=last)

            def fnet(layer):
                tables = fnet_tables()

                def table(j):
                    hi, _, size = tables[j]
                    u = n.unit + 2 + j
                    round_unit(u % SLOTS, u // SLOTS + 1, hi, size)

                if layer:
                    act.wait_ge(result_ready, n.result)
                table(0)
                table(1)

                def early_tables():
                    for j in range(2, EARLY_TABLES):
                        table(j)

                norm(layer, SH1, SC1, lambda c: c % 2 == 0, after_root=early_tables,
                     after_chunk=lambda c: table(EARLY_TABLES + c) if EARLY_TABLES + c < TABLES else None)
                r = n.result
                for g in range(GROUPS):
                    for t in range(5):
                        take(r, [(freq[0][:, t, :], acc[r % 2][:, 0, :])])
                        r += 1
                    for m in range(2):
                        c = 2 * g + m
                        take(r, [(h_hi[:, c, CXS], acc[r % 2][:, 0, 0:CTX]), (h_hi[:, c, LTS], acc[r % 2][:, 1, :])])
                        r += 1
                n.result = r
                n.unit += TABLES + late_mods(layer)
                project(more=product_mods(layer))
                after_project(n)

            def pool_mix(layer):
                def pooled_hi(c):
                    if c >= 1:
                        round_pooled(c - 1)

                def round_pooled(c):
                    act.wait_ge(pooled_full, c + 1)
                    for to, cols in ((CXS, slice(PC, PC + CTX)), (LTS, slice(PL, PL + LAT))):
                        done = nc.scalar.activation(h_hi[:, c, to], window[c % 2][:, cols], ACT.Copy)
                    done.then_inc(h_rounded, 1)

                norm(layer, SH1, SC1, lambda c: True, target=pooled_hi)
                round_pooled(KC - 1)
                for j in range(KC):
                    if j % 2 == 1:
                        u = j // 2 + 2
                        round_ring(u % SLOTS, n.unit // SLOTS + u // SLOTS + 1, n.result + j + 1,
                                   2 * GROUP if u < 4 else UNIT)
                    act.wait_ge(result_taken, n.result + j + 1)
                    square(x[:, j, :])
                after_project(n, 4)

            def mla(layer):
                act.wait_ge(table_loaded, TABLES_MLA)
                nc.scalar.activation(ckv_hi[:, :, LAT1:KEYS], cache[:, 0:RC, :], ACT.Copy)
                nc.scalar.activation(kpe_hi[:, LAT1:KEYS], cache[:, RC, :], ACT.Copy).then_inc(cache_rounded, 1)
                norm(layer, SH1, SC1)
                act.wait_ge(h_ready, n.chunk)
                act.dma_start(rows[:, 5:7, :], a["rope"]).then_inc(table_loaded, 16)
                r0, u0 = n.result, n.unit
                ring = lambda j, free: round_ring((u0 + j) % SLOTS, (u0 + j) // SLOTS + 1, free,
                                                  (LATENT_SIZES + HEAD_SIZES)[j])

                def latent(r, raw_, previous):
                    act.wait_ge(result_ready, r + 1)
                    if previous is not None:
                        act.wait_ge(result_taken, previous + 1)
                    nc.scalar.activation(two(raw_), halves(acc[r % 2]), ACT.Copy)
                    nc.scalar.activation(two(row(SQ)), halves(acc[r % 2]), ACT.Square).then_inc(latent_squared, 1)

                for m in range(RC):
                    ring(m + 2, r0 + m + 1)
                    latent(r0 + m, ckv_raw[:, m, :], r0 + m - 1 if m else None)
                ring(6, r0 + 5)
                ring(7, r0 + 5)
                ring(8, r0 + 6)
                latent(r0 + 5, cq_raw[:, 0, :], r0 + 3)
                act.wait_ge(rope_step, 3)
                nc.scalar.activation(kpe_hi[:, 0:LAT1], kpe_sin[:, 0:LAT1], ACT.Copy
                                     ).then_inc(latent_rounded, 1)
                ring(9, r0 + 8)
                latent(r0 + 7, cq_raw[:, 1, :], r0 + 5)
                root(KV_RANK)
                for m in range(RC):
                    act.wait_ge(latent_normed, m + 1)
                    nc.scalar.activation(ckv_hi[:, m, 0:LAT1], ckv_raw[:, m, 0:LAT1], ACT.Copy
                                         ).then_inc(latent_rounded, 1)
                act.dma_start(a["state_ckv"], ckv_raw[:, :, CXS]).then_inc(stored, 16)
                act.dma_start(a["state_kpe"], kpe_raw[0:ROPE, CXS]).then_inc(stored, 16)
                for m in range(2, QC):
                    ring(m + 8, r0 + m + 7)
                    latent(r0 + m + 6, cq_raw[:, m, :], r0 + m + 5)
                root(Q_RANK, rstd_q)
                act.wait_ge(cached, 2)
                for m in range(QC):
                    act.wait_ge(latent_normed, RC + m + 1)
                    nc.scalar.activation(cq_hi[:, m, :], cq_raw[:, m, :], ACT.Copy).then_inc(latent_rounded, 1)
                act.wait_ge(stored, 32)
                act.wait_ge(latent_ready, 1 + RC + QC)
                n.result += 12
                n.unit += 12
                nc.scalar.preload_act_table(ACT.Exp)
                with act.Fori(0, 2) as i:
                    for h2 in range(2):
                        attend(i, h2)
                n.result += 128
                n.unit += 24
                n.score += 40

                act.wait_ge(result_ready, n.result)
                act.wait_ge(result_taken, n.result)
                act.dma_start(cond[:], a["cond"]).then_inc(first_loaded, 16)
                project()
                after_project(n)

            def attend(i, h2):
                r = n.result + 64 * i + 32 * h2
                s = n.score + 20 * i + 10 * h2

                def ring(j, free):
                    at_ = 6 * h2 + j
                    round_ring(at_ % SLOTS, n.unit // SLOTS + 3 * i + at_ // SLOTS + 1, free,
                               HEAD_SIZES[j] if j < 6 else UNIT)

                def exponentials(hh, t):
                    q0, k0, width, banks = Q_TILES[t]
                    b = (5 * hh + t) % 2
                    act.wait_ge(bias_done, s + 5 * hh + t + 1)
                    nc.scalar.activation(
                        probs[b][:, 0:width * banks].rearrange("p (a b) -> p a b", a=banks),
                        sacc[b][:, 0:banks, 0:width], ACT.Exp, bias=negtop[:, b:b + 1], scale=SM_SCALE,
                        accum_out=total[:, b:b + 1]).then_inc(exp_done, 1)

                def take_transposed(hh, t):
                    q0, k0, width, banks = Q_TILES[t]
                    index = T_RESULTS[hh][t]
                    take(r + index, transposed_pieces(pt_hi, acc[index % 2], width * banks // P))

                def take_out(hh, t):
                    index = O_RESULTS[hh][t]
                    take(r + index, [(head_out(h_hi, i, h2, hh, Q_TILES[t][0]), acc[index % 2][:, 0, 0:P])])

                def take_keys(hh):
                    p = K_RESULTS[hh] % 2
                    take(r + K_RESULTS[hh], [(k_hi[:].rearrange("p (a b) -> p a b", a=2), acc[p][:, :, 0:KHALF])])

                def take_queries(hh):
                    take(r + Q_RESULTS[hh], [(two(q_hi[:]), halves(acc[Q_RESULTS[hh] % 2]))])

                ring(2, r + K_RESULTS[0] + 1)
                take_keys(0)
                ring(3, r + QPE_RESULT + 1)
                take_queries(0)
                act.wait_ge(rope_step, 5 + (2 * i + h2) * 3)
                nc.scalar.activation(qpe_hi[:], q_rot, ACT.Copy).then_inc(result_rounded, 1)
                ring(4, r + Q_RESULTS[0] + 1)
                for t in range(6):
                    take(r + V_RESULT + t, [(v_hi[:, t, :], acc[t % 2][:, 0, 0:2 * VH])])
                    if t in (2, 4):
                        exponentials(0, t // 2 - 1)
                ring(5, r + V_RESULT + 6)
                for t in range(3):
                    take_transposed(0, t)
                    exponentials(0, t + 2)
                    take_out(0, t)
                take_keys(1)
                ring(6, r + K_RESULTS[1] + 1)
                take_queries(1)
                ring(7, r + Q_RESULTS[1] + 1)
                take_transposed(0, 3)
                exponentials(1, 0)
                take_out(0, 3)
                take_transposed(0, 4)
                exponentials(1, 1)
                take_out(0, 4)
                for t in range(5):
                    take_transposed(1, t)
                    if t < 3:
                        exponentials(1, t + 2)
                    take_out(1, t)

            def activate_cond(loads):
                act.wait_ge(first_loaded, loads)
                if loads == FIRST_LOADS:
                    nc.scalar.activation(cond_columns[:], cond_columns[:], ACT.Silu)
                nc.scalar.activation(cond[:], cond[:], ACT.Silu).then_inc(cond_ready, 1)

            def load_layer(layer):
                if layer:
                    act.wait_ge(result_taken, n.result)
                act.dma_start(conv_w[:], a["conv_w"][layer]).then_inc(layer_loaded, 16)
                if layer + 1 < DEPTH:
                    act.dma_start(b_ada[:, (layer + 1) % 2, :, :], a["b_ada"][layer + 1]).then_inc(layer_loaded, 16)

            act.dma_start(cond[:], a["cond"]).then_inc(first_loaded, 16)
            act.dma_start(cond_columns[:], a["cond_columns"]).then_inc(first_loaded, 16)
            act.dma_start(b_ada[:, 0, :, :], a["b_ada"][0]).then_inc(first_loaded, 16)
            for c in range(KC):
                act.dma_start(x[:, c, :], a["x"][c]).then_inc(loaded, 16)
            for dst, name in ((ident, "ident"), (ones, "ones"), (perm, "perm"), (gains, "gains")):
                act.dma_start(dst[:], a[name]).then_inc(loaded, 16)
            activate_cond(FIRST_LOADS)
            act.wait_ge(setup_done, 1)
            act.wait_ge(loaded, SMALL_LOADS)
            n.unit, n.squared = FIRST_MODS, KC
            for c in range(KC):
                if c:
                    act.wait_ge(summed, c)
                square(x[:, c, :])
            load_layer(0)
            round_ring(0, n.unit // SLOTS + 1)
            round_ring(1, n.unit // SLOTS + 1)
            for layer, kind in enumerate(MIXERS):
                if layer:
                    load_layer(layer)
                    if kind == "pool":
                        act.dma_start(inv_count[:], a["inv_count"]).then_inc(table_loaded, 16)
                    if kind == "mla":
                        act.wait_ge(result_ready, n.result)
                        act.dma_start(cache[:], a["cache"]).then_inc(table_loaded, 16)
                act.wait_ge(mod_ready, layer + 1 + (layer > 0))
                {"fnet": fnet, "pool": pool_mix, "mla": mla}[kind](layer)
                ffn(layer)
            root(D)
            for c in range(KC):
                act.wait_ge(y_ready, c + 1)
                act.dma_start(a["y"][c], y[:, c, :]).then_inc(stored, 16)
            act.wait_ge(stored, 32 + 16 * KC)

        @block.vector
        def _(dve):
            n = Counts()
            biased = [0]

            def recip(width_row):
                dve.wait_ge(rooted, n.stat + 1)
                nc.vector.reciprocal(width_row, width_row).then_inc(rstd_done, 1)
                n.stat += 1
                dve.wait_ge(rstd_done, n.stat)

            def clear_sum():
                nc.vector.memset(row(SUM), 0.0).then_inc(sum_cleared, 1)
                n.cleared += 1

            def scale_x(c):
                nc.vector.tensor_tensor(row(XN[c % 3]), x[:, c, :], row(RSTD), ALU.mult).then_inc(xn_ready, 1)

            def lo_part(ready, hi, lo, full, inc, rounded=h_rounded):
                dve.wait_ge(rounded, ready)
                nc.vector.tensor_tensor(lo, full, hi.bitcast(f32), ALU.subtract).then_inc(inc, 1)

            def norm(layer, shift, scale, fnet=False):
                recip(row(RSTD))
                scale_x(0)
                modulated = []
                for c in range(KC):
                    if c + 1 < KC:
                        if c >= 2:
                            dve.wait_ge(*modulated[c - 2])
                        scale_x(c + 1)
                    if not (fnet and c % 2 == 0):
                        dve.wait_ge(xn_ready, n.chunk + c + 1)
                        if c >= 2:
                            dve.wait_ge(h_ready, n.chunk + c - 1)
                        for z, cols in enumerate((CXS, LTS)):
                            done = nc.vector.tensor_scalar(row(HF + c % 2)[:, cols], row(XN[c % 3])[:, cols],
                                                           mod[:, layer % 2, scale + c, z:z + 1],
                                                           mod[:, layer % 2, shift + c, z:z + 1], ALU.mult, ALU.add)
                        done.then_inc(h_affine, 1)
                        n.affine += 1
                        modulated.append((h_affine, n.affine))
                    else:
                        n.full += 1
                        modulated.append((h_full, n.full))
                    if fnet and c:
                        lo_part(n.chunk + c, h_hi[:, c - 1, :], h_lo[:, c - 1, :], row(HF + (c - 1) % 2), h_ready)
                    if c == 2:
                        clear_sum()
                if fnet:
                    lo_part(n.chunk + KC, h_hi[:, KC - 1, :], h_lo[:, KC - 1, :], row(HF + (KC - 1) % 2), h_ready)
                n.chunk += KC

            def take(r, rounded, pieces):
                dve.wait_ge(result_rounded, rounded)
                for lo, hi, src in pieces:
                    done = nc.vector.tensor_tensor(lo, src, hi.bitcast(f32), ALU.subtract)
                done.then_inc(result_taken, 1)

            def project(gate, squares=True):
                if squares:
                    dve.wait_ge(sum_cleared, n.cleared)
                with dve.Fori(0, 2) as i:
                    for j in range(4):
                        update_x(4 * i + j, 4 * i + j, gate(4 * i + j), j % 2, squares)

            def project_with_units(gate, squares, layer, before, steps, place_):
                first = n.ada

                def unit():
                    u = n.unit + place_ + n.ada - first
                    modulate(layer, n.ada - MODS * layer, u % SLOTS, u // SLOTS + 1, n.ada)
                    n.ada += 1

                for _ in range(before):
                    unit()
                for j in range(KC):
                    update_x(j, j, gate(j), j % 2, squares)
                    for _ in range(steps[j]):
                        unit()
                n.unit += n.ada - first

            def update_x(c, j, gate, pair, squares):
                dve.wait_ge(result_ready, n.result + j + 1)
                for cond_, x0, x1, bank, p0 in ((0, 0, CTX, 0, 0), (1, LAT0, HALF, 0, LAT0), (1, HALF, LAT1, 1, 0)):
                    xs = x[:, ds(c, 1), x0:x1].rearrange("p o t -> p (o t)")
                    done = nc.vector.scalar_tensor_tensor(xs, acc[pair][:, bank, p0:p0 + x1 - x0], gate(cond_), xs,
                                                          ALU.mult, ALU.add)
                done.then_inc(result_taken, 1)
                if squares:
                    dve.wait_ge(summed, n.squared + j)
                    add_square(row(SUM), n.squared + j, summed)

            def add_square(total_, index, inc, ready=squared):
                dve.wait_ge(ready, index + 1)
                nc.vector.tensor_tensor(total_, total_, row(SQ), ALU.add).then_inc(inc, 1)

            def mod_gate(layer, which):
                return lambda c: lambda z: mod[:, layer % 2, ds(which + c, 1), z:z + 1].rearrange("p o t -> p (o t)")

            def modulate(layer, index, slot, use, count, buffer=None):
                dve.wait_ge(raw_ready[slot], 16 * use)
                wait_past(dve, ada_summed, count - PE_MODS if buffer is None else count)
                out = products[slot % 2 if buffer is None else buffer]
                for z, signal in enumerate((ada_summed, unit_done[slot])):
                    nc.vector.scalar_tensor_tensor(
                        out[z][:], raw[slot][:], 1.0, cond[:, z, :], ALU.mult, ALU.mult,
                        accum_out=mod[:, layer % 2, ds(index, 1), z:z + 1].rearrange("p o t -> p (o t)")
                    ).then_inc(signal, 1)

            def add_bias(layer, first, last):
                of_layer = mod[:, layer % 2, first:last, :]
                biased[0] += 1
                nc.vector.tensor_tensor(of_layer, of_layer, b_ada[:, layer % 2, first:last, :], ALU.add
                                        ).then_inc(ada_biased, 1)
                dve.wait_ge(ada_biased, biased[0])
                if not any(first <= scale < last for scale in (SC1, SC2)):
                    return
                for scale in (SC1, SC2):
                    if first <= scale < last:
                        part = mod[:, layer % 2, scale:scale + KC, :]
                        done = nc.vector.tensor_scalar(part, part, 1.0, None, ALU.add)
                done.then_inc(mod_ready, 1)

            def ffn(layer):
                norm(layer, SH2, SC2)
                for t in conv:
                    nc.vector.memset(t[:, 0:1], 0.0)
                    nc.vector.memset(t[:, W + 1:W + 2], 0.0).then_inc(conv_padded, 1)
                dve.wait_ge(conv_padded, 2 * layer + 2)
                if MIXERS[layer] == "mla":
                    dve.wait_ge(cond_ready, 2)
                dve.wait_ge(layer_loaded, layer_loads(layer))
                for part, (_, count) in enumerate(PARTS):
                    turn = 1 if ada_in_ffn(layer) else 2
                    with dve.Fori(0, count // turn) as i:
                        def modulation_unit(u):
                            return (layer + 1, n.ada - MODS * (layer + 1) + 2 * i + u, 2 + u,
                                    n.unit // SLOTS + i + 1, n.ada + 2 * i + u)

                        if turn == 1:
                            modulate(*modulation_unit(0))
                        for z in range(turn):
                            pair = n.pair + turn * i + z
                            for half in range(2):
                                k = 2 * pair + half
                                tap = lambda t: conv_w[:, ds(pair - layer * PAIRS + half * PAIRS, 1),
                                                       t:t + 1].rearrange("p o t -> p (o t)")
                                dve.wait_ge(centered, k + 1)
                                to = two(conv[half][:, 2:W + 2])
                                nc.vector.scalar_tensor_tensor(to, halves(acc[half]), tap(0), to, ALU.mult, ALU.add
                                                               ).then_inc(left_done, 1)
                                dve.wait_ge(left_done, k + 1)
                                to = two(conv[half][:, 0:W])
                                nc.vector.scalar_tensor_tensor(to, halves(acc[half]), tap(2), to, ALU.mult, ALU.add
                                                               ).then_inc(result_taken, 1)
                                if turn == 1 and half == 0:
                                    modulate(*modulation_unit(1))
                            dve.wait_ge(silu_done, pair + 1)
                            dve.wait_ge(result_taken, n.result + 2 * (turn * i + z) + 2)
                            nc.vector.tensor_tensor(gated[:], gated[:], conv[1][:, 1:W + 1], ALU.mult
                                                    ).then_inc(gated_done, 1)
                            dve.wait_ge(g_rounded, pair + 1)
                            gc = ds(turn * i + z, 1)
                            nc.vector.tensor_tensor(
                                g_lo[:, gc, :].rearrange("p o t -> p (o t)"), gated[:],
                                g_hi[:, gc, :].rearrange("p o t -> p (o t)").bitcast(f32), ALU.subtract
                            ).then_inc(g_ready, 1)
                    after_ffn_in(n, layer, count)
                    if extra(layer, part):
                        project_with_units(mod_gate(layer, G2), False, layer + 1, 2, (1, 1, 0, 0, 0, 0, 0, 0), 2)
                    else:
                        project(mod_gate(layer, G2), part == 2)
                    after_project(n, squares=part == 2)

            def fnet(layer):
                norm(layer, SH1, SC1, fnet=True)
                r = n.result

                def late(step):
                    for _ in range(LATE_STEPS[step] if late_mods(layer) else 0):
                        u = n.unit + 2 + TABLES + n.ada - FIRST_MODS
                        modulate(0, n.ada, u % SLOTS, u // SLOTS + 1, n.ada)
                        n.ada += 1

                for g in range(GROUPS):
                    for t in range(5):
                        n.rounded += 1
                        take(r, n.rounded, [(freq[1][:, t, :], freq[0][:, t, :], acc[r % 2][:, 0, :])])
                        r += 1
                        late(t)
                    for m in range(2):
                        c = 2 * g + m
                        n.rounded += 1
                        take(r, n.rounded, [(h_lo[:, c, CXS], h_hi[:, c, CXS], acc[r % 2][:, 0, 0:CTX]),
                                            (h_lo[:, c, LTS], h_hi[:, c, LTS], acc[r % 2][:, 1, :])])
                        r += 1
                        late(5 + m)
                n.result = r
                n.unit += TABLES + late_mods(layer)
                if late_mods(layer):
                    dve.wait_ge(unit_done[(n.unit + 1) % SLOTS], (n.unit + 1) // SLOTS + 1)
                    add_bias(layer, FIRST_MODS, MODS - PRODUCT_MODS)
                    dve.wait_ge(sum_cleared, n.cleared)
                    project_with_units(mod_gate(layer, G1), True, 0, 0, PRODUCT_STEPS, 6)
                    dve.wait_ge(unit_done[(n.unit + 5) % SLOTS], (n.unit + 5) // SLOTS + 1)
                    add_bias(layer, MODS - PRODUCT_MODS, MODS)
                else:
                    project(mod_gate(layer, G1))
                after_project(n)

            def pool_mix(layer):
                steps = [0]

                def step(ins):
                    steps[0] += 1
                    ins.then_inc(pool_step, 1)
                    dve.wait_ge(pool_step, steps[0])

                for t in padded:
                    for lo, hi in ((0, PC), (PC + CTX, PL), (PL + LAT, PADW)):
                        last = nc.vector.memset(t[:, lo:hi], 0.0)
                step(last)
                for z in range(2):
                    last = nc.vector.tensor_tensor(gate_pool[:, :, z], mod[:, layer % 2, G1:G1 + KC, z],
                                                   pool_scale, ALU.mult)
                step(last)
                dve.wait_ge(table_loaded, TABLES_POOL)
                recip(row(RSTD))
                clear_sum()
                for c in range(KC):
                    n.full += 1
                    dve.wait_ge(h_full, n.full)
                    if c >= 2:
                        dve.wait_ge(h_ready, n.chunk + c - 1)
                    source, lo, hi = padded[c % 2], 0, PADW
                    levels = c // 2 + 1
                    a_, b_ = window[c % 2], scratch
                    outs = [a_ if (levels - l) % 2 == 0 else b_ for l in range(levels)]
                    for level in range(levels):
                        back = 1 if level == 0 else 2 ** (level - 1)
                        ahead = 0 if level == 0 else back
                        lo, hi = lo + back, hi - ahead
                        out = outs[level]
                        step(nc.vector.tensor_tensor(out[:, lo:hi], source[:, lo - back:hi - back],
                                                     source[:, lo + ahead:hi + ahead], ALU.add))
                        source = out
                    out = window[c % 2]
                    step(nc.vector.tensor_tensor(out[:, PC:PL + LAT], source[:, PC:PL + LAT],
                                                 inv_count[:, c // 2, PC:PL + LAT], ALU.mult))
                    nc.vector.tensor_tensor(out[:, PC:PL + LAT], out[:, PC:PL + LAT], padded[c % 2][:, PC:PL + LAT],
                                            ALU.subtract).then_inc(pooled_full, 1)
                n.chunk += KC
                for c in range(KC):
                    update_x(c, c, lambda z: gate_pool[:, c, z:z + 1], c % 2, True)
                after_project(n, 4)

            def mla(layer):
                for t in (ckv_hi, ckv_lo):
                    nc.vector.memset(t[:, :, KEYS:KW].bitcast(f32), 0.0)
                nc.vector.memset(kpe_lo[:, KEYS:KW].bitcast(f32), 0.0).then_inc(cached, 1)
                dve.wait_ge(cache_rounded, 1)
                nc.vector.tensor_tensor(kpe_lo[:, LAT1:KEYS], cache[:, RC, :], kpe_hi[:, LAT1:KEYS].bitcast(f32),
                                        ALU.subtract)
                nc.vector.tensor_tensor(ckv_lo[:, :, LAT1:KEYS], cache[:, 0:RC, :],
                                        ckv_hi[:, :, LAT1:KEYS].bitcast(f32), ALU.subtract).then_inc(cached, 1)
                norm(layer, SH1, SC1)
                r0 = n.result
                dve.wait_ge(sum_cleared, n.cleared)
                for m in range(RC):
                    if m:
                        dve.wait_ge(result_taken, r0 + m)
                    add_square(row(SUM), m, result_taken, latent_squared)
                dve.wait_ge(result_ready, r0 + 5)
                nc.vector.tensor_copy(two(kpe_raw[:]), halves(acc[(r0 + 4) % 2])).then_inc(result_taken, 1)
                dve.wait_ge(result_taken, r0 + 5)
                dve.wait_ge(table_loaded, TABLES_ROPE)
                nc.vector.tensor_tensor(kpe_cos[:], kpe_raw[:], tab_cos, ALU.mult).then_inc(rope_step, 1)
                nc.vector.memset(sum_q, 0.0).then_inc(rope_step, 1)
                dve.wait_ge(rope_step, 2)
                add_square(sum_q, RC, result_taken, latent_squared)
                dve.wait_ge(result_ready, r0 + 7)
                nc.vector.tensor_tensor(two(kpe_sin[:]), halves(acc[(r0 + 6) % 2]), two(tab_sin), ALU.mult
                                        ).then_inc(result_taken, 1)
                dve.wait_ge(result_taken, r0 + 7)
                nc.vector.tensor_tensor(kpe_sin[:], kpe_sin[:], kpe_cos[:], ALU.add).then_inc(rope_step, 1)
                dve.wait_ge(rope_step, 3)
                lo_part(1, kpe_hi[:, 0:LAT1], kpe_lo[:, 0:LAT1], kpe_sin[:, 0:LAT1], latent_ready, latent_rounded)
                add_square(sum_q, RC + 1, result_taken, latent_squared)
                recip(row(RSTD))

                def normed(raw_, gain, rstd, width=W):
                    nc.vector.scalar_tensor_tensor(raw_, raw_, gain, rstd, ALU.mult, ALU.mult
                                                   ).then_inc(latent_normed, 1)

                for m in range(RC):
                    normed(ckv_raw[:, m, :], g_kv[:, m:m + 1], row(RSTD))
                dve.wait_ge(latent_normed, RC)
                for m in range(RC):
                    lo_part(2 + m, ckv_hi[:, m, 0:LAT1], ckv_lo[:, m, 0:LAT1], ckv_raw[:, m, 0:LAT1],
                            latent_ready, latent_rounded)
                for m in range(2, QC):
                    dve.wait_ge(result_taken, r0 + 6 + m)
                    add_square(sum_q, RC + m, result_taken, latent_squared)
                recip(rstd_q)
                for m in range(QC):
                    normed(cq_raw[:, m, :], g_q[:, m:m + 1], rstd_q)
                dve.wait_ge(latent_normed, RC + QC)
                for m in range(QC):
                    lo_part(RC + 2 + m, cq_hi[:, m, :], cq_lo[:, m, :], cq_raw[:, m, :], latent_ready, latent_rounded)
                n.result += 12
                n.unit += 12
                for t in (top, total):
                    nc.vector.memset(t[:], 0.0).then_inc(score_taken, 1)
                with dve.Fori(0, 2) as i:
                    for h2 in range(2):
                        attend(i, h2)
                n.result += 128
                n.rounded += 4 * 31
                n.unit += 24
                n.score += 40
                clear_sum()
                dve.wait_ge(sum_cleared, n.cleared)
                project(mod_gate(layer, G1))
                after_project(n)

            def attend(i, h2):
                r = n.result + 64 * i + 32 * h2
                s = n.score + 20 * i + 10 * h2
                rounded = n.rounded + 62 * i + 31 * h2
                ropes = 3 + (2 * i + h2) * 3

                def take_keys(hh, count):
                    take(None, rounded + count, [(k_lo[:].rearrange("p (a b) -> p a b", a=2),
                                                  k_hi[:].rearrange("p (a b) -> p a b", a=2),
                                                  acc[K_RESULTS[hh] % 2][:, :, 0:KHALF])])

                def take_queries(hh, count):
                    take(None, rounded + count, [(two(q_lo[:]), two(q_hi[:]), halves(acc[Q_RESULTS[hh] % 2]))])

                def maximum(hh, t):
                    q0, k0, width, banks = Q_TILES[t]
                    b = (5 * hh + t) % 2
                    k = s + 5 * hh + t + 1
                    dve.wait_ge(score_ready, k)
                    nc.vector.tensor_reduce(top[:, b:b + 1], sacc[b][:, 0:banks, 0:width], AX.XY, ALU.max
                                            ).then_inc(top_done, 1)
                    dve.wait_ge(top_done, k)
                    nc.vector.tensor_scalar(negtop[:, b:b + 1], top[:, b:b + 1], -SM_SCALE, None, ALU.mult
                                            ).then_inc(bias_done, 1)

                def normalise(hh, t):
                    q0, k0, width, banks = Q_TILES[t]
                    b = (5 * hh + t) % 2
                    k = s + 5 * hh + t + 1
                    dve.wait_ge(exp_done, k)
                    nc.vector.reciprocal(inverse[:, b:b + 1], total[:, b:b + 1]).then_inc(inverse_done, 1)
                    dve.wait_ge(inverse_done, k)
                    pr = probs[b][:, 0:width * banks]
                    nc.vector.tensor_scalar(pr, pr, inverse[:, b:b + 1], None, ALU.mult).then_inc(score_taken, 1)

                def take_transposed(hh, t):
                    q0, k0, width, banks = Q_TILES[t]
                    tiles = width * banks // P
                    index = T_RESULTS[hh][t]
                    take(None, rounded + index, [(lo, hi, src) for (lo, src), (hi, _) in zip(
                        transposed_pieces(pt_lo, acc[index % 2], tiles),
                        transposed_pieces(pt_hi, acc[index % 2], tiles))])

                def take_out(hh, t):
                    index = O_RESULTS[hh][t]
                    q0 = Q_TILES[t][0]
                    take(None, rounded + index, [(head_out(h_lo, i, h2, hh, q0), head_out(h_hi, i, h2, hh, q0),
                                                  acc[index % 2][:, 0, 0:P])])

                take_keys(0, 1)
                dve.wait_ge(result_ready, r + QPE_RESULT + 1)
                nc.vector.tensor_copy(two(q_raw), halves(acc[1])).then_inc(result_taken, 1)
                take_queries(0, 2)
                dve.wait_ge(result_ready, r + ROTATION + 1)
                nc.vector.tensor_tensor(two(q_rot), halves(acc[1]), two(tab_sin), ALU.mult).then_inc(result_taken, 1)
                nc.vector.tensor_tensor(q_raw, q_raw, tab_cos, ALU.mult).then_inc(rope_step, 1)
                dve.wait_ge(result_taken, r + ROTATION + 1)
                dve.wait_ge(rope_step, ropes + 1)
                nc.vector.tensor_tensor(q_rot, q_rot, q_raw, ALU.add).then_inc(rope_step, 1)
                dve.wait_ge(result_rounded, rounded + 3)
                nc.vector.tensor_tensor(qpe_lo[:], q_rot, qpe_hi[:].bitcast(f32), ALU.subtract).then_inc(rope_step, 1)
                for t in range(6):
                    take(None, rounded + V_RESULT + t, [(v_lo[:, t, :], v_hi[:, t, :], acc[t % 2][:, 0, 0:2 * VH])])
                    if t == 1:
                        maximum(0, 0)
                    if t == 3:
                        normalise(0, 0)
                        maximum(0, 1)
                for t in range(3):
                    take_transposed(0, t)
                    normalise(0, t + 1)
                    maximum(0, t + 2)
                    take_out(0, t)
                take_keys(1, K_RESULTS[1])
                take_queries(1, Q_RESULTS[1])
                normalise(0, 4)
                take_transposed(0, 3)
                maximum(1, 0)
                take_out(0, 3)
                normalise(1, 0)
                take_transposed(0, 4)
                maximum(1, 1)
                take_out(0, 4)
                for t in range(5):
                    take_transposed(1, t)
                    if t < 4:
                        normalise(1, t + 1)
                    if t < 3:
                        maximum(1, t + 2)
                    take_out(1, t)

            nc.vector.memset(rows[:], 0.0)
            nc.vector.memset(eps[:], EPS).then_inc(setup_done, 1)
            dve.wait_ge(first_loaded, FIRST_LOADS)
            dve.wait_ge(setup_done, 1)
            dve.wait_ge(cond_ready, 1)
            places = [p for p in range(FIRST_MODS) if p not in PE_PLACES]
            for u, p in enumerate(places):
                modulate(0, u, p % SLOTS, p // SLOTS + 1, u, u % 2)
                c = u - (DVE_MODS - KC)
                if c == 0:
                    dve.wait_ge(loaded, SMALL_LOADS)
                if c >= 0:
                    if c:
                        dve.wait_ge(summed, c)
                    add_square(row(SUM), c, summed)
            for slot_done in unit_done:
                dve.wait_ge(slot_done, FIRST_MODS // SLOTS)
            biased[0] += 1
            nc.vector.tensor_copy(mod[:, 0, DVE_MODS:FIRST_MODS, :].rearrange("p u c -> p (u c)"),
                                  sacc[1][:, 0, 0:2 * PE_MODS]).then_inc(ada_biased, 1)
            dve.wait_ge(ada_biased, biased[0])
            n.unit, n.ada, n.squared = FIRST_MODS, FIRST_MODS, KC
            for layer, kind in enumerate(MIXERS):
                add_bias(layer, 0, FIRST_MODS if late_mods(layer) else MODS)
                {"fnet": fnet, "pool": pool_mix, "mla": mla}[kind](layer)
                ffn(layer)
            recip(row(RSTD))
            for c in range(KC):
                nc.vector.scalar_tensor_tensor(y[:, c, :], x[:, c, :], g_final[:, c:c + 1], row(RSTD),
                                               ALU.mult, ALU.mult).then_inc(y_ready, 1)


def _weight_units(w, rows=None, cols=None):
    k, m = w.shape
    u = w.reshape(k // P, P, m // P, P).transpose(2, 1, 0, 3).reshape(m // P, P, k)
    return _padded(u)


def _padded(u):
    out = np.zeros((u.shape[0], P, UNIT), np.float32)
    out[:, :, :u.shape[2]] = u
    return out


def _fourier_units():
    def angle(size):
        i = np.arange(size)
        return 2 * np.pi * ((i[:, None] * i[None, :]) % size) / size
    ch, cx, sq = angle(GROUP), angle(CTX), angle(LAT)
    chan = np.concatenate([np.cos(ch), np.sin(ch)], 1) / np.sqrt(GROUP)
    units = [chan.reshape(2, P, 2 * GROUP)]
    units += [t[None] / np.sqrt(CTX) for t in (np.cos(cx), -np.sin(cx))]
    for t in (np.cos(sq), -np.sin(sq)):
        units.append((t / np.sqrt(LAT)).reshape(2, 2, P, LAT).transpose(0, 2, 1, 3).reshape(2, P, 2 * LAT))
    return np.concatenate([_padded(u.astype(np.float32)) for u in units])


def _stream(w):
    ada = [w["w_ada"][l].T.reshape(MODS, P, D) for l in range(DEPTH)]
    columns = iter(_weight_units(w["w_ada"][0][:, DVE_MODS * P:FIRST_MODS * P]))
    rows = iter(ada[0])
    out = [np.stack([next(columns if p in PE_PLACES else rows) for p in range(FIRST_MODS)])]
    f = 0
    for layer, kind in enumerate(MIXERS):
        if kind == "fnet":
            u = _weight_units(w["w_fnet"][f])
            f += 1
            out += [u[:2], _fourier_units(), ada[0][FIRST_MODS:FIRST_MODS + late_mods(layer)], u[2:6],
                    ada[0][MODS - product_mods(layer):], u[6:]]
        elif kind == "pool":
            g = w["w_pool"][0].reshape(GROUPS, 2, P, 2, P).transpose(0, 2, 3, 1, 4).reshape(GROUPS, P, 4 * P)
            u = _padded(g)
            out += [u]
        else:
            dkv = w["w_dkv"][0]
            ckv = _weight_units(dkv[:, :KV_RANK])
            kpe = np.concatenate([dkv[:, KV_RANK:]] * 2, 1)
            kpe = np.concatenate([_weight_units(kpe[:D // 2]), _weight_units(kpe[D // 2:])])
            out += [ckv, kpe, _weight_units(w["w_dq"][0])]
            uq = w["w_uq"][0].reshape(Q_RANK, HEADS, NOPE + ROPE)
            ukv = w["w_ukv"][0].reshape(KV_RANK, HEADS, NOPE + VH)
            for h in range(0, HEADS, 2):
                v = ukv[:, h:h + 2, NOPE:].reshape(RC, P, 2 * VH).transpose(1, 0, 2).reshape(1, P, RC * 2 * VH)
                kq = [[_weight_units(ukv[:, k, :NOPE]), _weight_units(uq[:, k, :NOPE])] for k in (h, h + 1)]
                rotated = _weight_units(uq[:, h:h + 2, NOPE:].reshape(Q_RANK, 2 * ROPE))
                out += [kq[0][0], rotated, kq[0][1], v, *kq[1]]
            out.append(_weight_units(w["w_o"][0]))
        w_in, w_out = _weight_units(w["w_ffn_in"][layer]), w["w_ffn_out"][layer]
        for part, (first, count) in enumerate(PARTS):
            for p in range(first, first + count):
                out += [w_in[p:p + 1], w_in[PAIRS + p:PAIRS + p + 1]]
                if ada_in_ffn(layer):
                    taken = 2 * p + extra(layer, EXTRA_PART) * (part > EXTRA_PART)
                    out.append(ada[layer + 1][taken:taken + 2])
            u = _weight_units(w_out[first * P:(first + count) * P])
            taken = 2 * (first + count)
            rest = ada[layer + 1][taken:taken + ADA_EXTRA] if extra(layer, part) else u[:0]
            out += [u[:2], rest, u[2:]]
    return np.concatenate(out)


def _tokens(ctx_t, lat_t):
    c = ctx_t.shape[0]
    out = np.zeros((c // P, P, W), np.float32)
    out[:, :, 0:CTX] = ctx_t.reshape(c // P, P, CTX)
    out[:, :, LAT0:LAT1] = lat_t.reshape(c // P, P, LAT)
    return out


def _rope_tables():
    grid_w, axis = 64, ROPE // 2
    inv = (1.0 / (np.float32(10000.0) ** (np.arange(0, axis, 2, dtype=np.float32) / np.float32(axis)))).astype(np.float32)
    t = np.arange(LAT)
    out = np.zeros((P, 2, W), np.float32)
    out[:, 0, 0:CTX] = 1.0
    swap = np.zeros((P, P), np.float32)
    for p in range(P):
        d = p % ROPE
        pos = (t // grid_w if d < axis else t % grid_w).astype(np.float32)
        ang = pos * inv[d % (axis // 2)]
        upper = d % axis >= axis // 2
        out[p, 0, LAT0:LAT1] = np.cos(ang)
        out[p, 1, LAT0:LAT1] = np.sin(ang) if upper else -np.sin(ang)
        swap[p - axis // 2 if upper else p + axis // 2, p] = 1.0
    return out, swap


def _inverse_counts():
    out = np.zeros((4, PADW), np.float32)
    for g in range(4):
        w = 2 ** (g + 1)
        for start, size in ((PC, CTX), (PL, LAT)):
            t = np.arange(size)
            lo, hi = np.clip(t - w // 2, 0, size), np.clip(t - w // 2 + w, 0, size)
            out[g, start:start + size] = 1.0 / (hi - lo)
    return np.ascontiguousarray(np.broadcast_to(out, (P, 4, PADW)))


def _columns(v):
    return np.moveaxis(v.reshape(*v.shape[:-1], -1, P), -1, -2)


def kernel(**inputs):
    import concourse.bacc as bacc
    from concourse.bass_utils import run_bass_kernel_spmd

    w = {k: np.asarray(v) for k, v in inputs.items()}
    rope, swap = _rope_tables()
    conv = np.concatenate([w["w_ffn_conv"], w["b_ffn_conv"][:, None]], 1)
    cache = np.zeros((P, RC + 1, PAST), np.float32)
    cache[:, :RC] = w["cache_ckv"][0, 0].T.reshape(RC, P, PAST).transpose(1, 0, 2)
    cache[:, RC] = np.concatenate([w["cache_kpe"][0, 0].T] * 2, 0)
    arrays = {
        "stream": _stream(w),
        "x": _tokens(w["x_prompt"][0].T, w["x_sample"][0].T),
        "cond": np.broadcast_to(np.stack([w["c_ctx"], w["c"][0]]), (P, 2, D)),
        "cond_columns": np.stack([_columns(w["c_ctx"]), _columns(w["c"][0])], -1),
        "b_ada": np.stack([_columns(w["b_ada"])] * 2, -1),
        "conv_w": _columns(conv).transpose(0, 2, 3, 1),
        "gains": np.concatenate([_columns(w["g_q"][0]), _columns(w["g_kv"][0]), _columns(w["g_final"]),
                                 _columns(w["pool_scale"][0])], 1),
        "cache": cache,
        "rope": rope,
        "perm": swap,
        "ident": np.eye(P, dtype=np.float32),
        "ones": np.ones((P, P), np.float32),
        "inv_count": _inverse_counts(),
    }
    arrays = {k: np.ascontiguousarray(v) for k, v in arrays.items()}
    outs = {"y": (KC, P, W), "state_ckv": (P, RC, CTX), "state_kpe": (ROPE, CTX)}
    nc = bacc.Bacc("TRN2", target_bir_lowering=False, num_devices=1)
    f32 = mybir.dt.float32
    aps = {k: nc.dram_tensor(f"in_{k}", v.shape, f32, kind="ExternalInput").ap() for k, v in arrays.items()}
    aps |= {k: nc.dram_tensor(f"out_{k}", s, f32, kind="ExternalOutput").ap() for k, s in outs.items()}
    build_backbone(nc, aps)
    r = run_bass_kernel_spmd(nc, [{f"in_{k}": v for k, v in arrays.items()}], core_ids=[0]).results[0]
    y = r["out_y"].reshape(D, W)
    ckv = r["out_state_ckv"].transpose(1, 0, 2).reshape(KV_RANK, CTX)
    return (np.ascontiguousarray(y[:, :CTX].T)[None], np.ascontiguousarray(y[:, LAT0:LAT1].T)[None],
            np.ascontiguousarray(ckv.T)[None, None], np.ascontiguousarray(r["out_state_kpe"].T)[None, None])
```
